# Optimizing a Trainium2 kernel written in Bass

```python
import jax, jax.numpy as jnp
from jax import lax
import numpy as np

D_MODEL = 1024
BATCH = 1
SEQ = 512
DEPTH = 2

RMS_EPS = 1e-6
NEG_INF = -1e30
Q_BLOCK = 128

GLA_HEADS = 4
GLA_DK = 64
GLA_DV = 128
GLA_GATE_RANK = 16
GLA_TAU = 16.0
GLA_CHUNK = 64

DSA_HEADS = 4
DSA_HEAD_DIM = 64
IDX_HEADS = 8
IDX_DIM = 32
DSA_TOPK = 256

MLA_HEADS = 4
MLA_Q_RANK = 192
MLA_KV_RANK = 128
MLA_NOPE_DIM = 64
MLA_ROPE_DIM = 32
MLA_V_DIM = 64
MLA_QK_DIM = MLA_NOPE_DIM + MLA_ROPE_DIM
ROPE_THETA = 10000.0

D_FF = 4 * D_MODEL

GLA_WIDTH = GLA_HEADS * GLA_DV
DSA_WIDTH = DSA_HEADS * DSA_HEAD_DIM
MLA_WIDTH = MLA_HEADS * MLA_V_DIM
D_MIX = GLA_WIDTH + DSA_WIDTH + MLA_WIDTH

IN_SPLITS = (
    GLA_HEADS * GLA_DK,
    GLA_HEADS * GLA_DK,
    GLA_WIDTH,
    GLA_WIDTH,
    GLA_GATE_RANK,
    DSA_WIDTH,
    DSA_WIDTH,
    DSA_WIDTH,
    IDX_HEADS * IDX_DIM,
    IDX_DIM,
    IDX_HEADS,
    MLA_Q_RANK,
    MLA_KV_RANK,
    MLA_ROPE_DIM,
)
D_IN = sum(IN_SPLITS)

kernel_name = "hybrid_gla_dsa_mla_parallel_heads"

def rms_norm(x, gain):
    xf = x.astype(jnp.float32)
    y = xf * lax.rsqrt(jnp.mean(xf * xf, axis=-1, keepdims=True) + RMS_EPS)
    return (y * gain.astype(jnp.float32)).astype(x.dtype)

def rotary(x, pos):
    half = x.shape[-1] // 2
    inv_freq = ROPE_THETA ** (-jnp.arange(half, dtype=jnp.float32) / half)
    ang = pos.astype(jnp.float32)[:, None] * inv_freq[None, :]
    cos = jnp.cos(ang)[None, :, None, :]
    sin = jnp.sin(ang)[None, :, None, :]
    xf = x.astype(jnp.float32)
    x1, x2 = xf[..., :half], xf[..., half:]
    return jnp.concatenate([x1 * cos - x2 * sin, x2 * cos + x1 * sin], axis=-1).astype(x.dtype)

def split_columns(proj):
    outs, start = [], 0
    for width in IN_SPLITS:
        outs.append(proj[..., start:start + width])
        start += width
    return outs

def gla_chunked(q, k, v, log_a):
    B, S, H, DK = q.shape
    DV = v.shape[-1]
    C = GLA_CHUNK
    N = S // C

    def chunks(t):
        return t.astype(jnp.float32).reshape(B, N, C, H, t.shape[-1]).transpose(0, 1, 3, 2, 4)

    qc = chunks(q) * (DK ** -0.5)
    kc, vc, gc = chunks(k), chunks(v), chunks(log_a)
    b = jnp.cumsum(gc, axis=3)
    b_end = b[:, :, :, -1:, :]
    q_dec = qc * jnp.exp(b)
    k_inv = kc * jnp.exp(-b)
    causal = jnp.tril(jnp.ones((C, C), dtype=bool))
    scores = jnp.where(causal, jnp.einsum('bnhcd,bnhsd->bnhcs', q_dec, k_inv), 0.0)
    o_intra = jnp.einsum('bnhcs,bnhsv->bnhcv', scores, vc)
    k_end = kc * jnp.exp(b_end - b)
    state_inc = jnp.einsum('bnhcd,bnhcv->bnhdv', k_end, vc)
    chunk_decay = jnp.exp(b_end[:, :, :, 0, :])

    def step(state, inp):
        dec, inc = inp
        return dec[..., None] * state + inc, state

    init = jnp.zeros((B, H, DK, DV), jnp.float32)
    _, s_prev = lax.scan(step, init, (jnp.moveaxis(chunk_decay, 1, 0), jnp.moveaxis(state_inc, 1, 0)))
    s_prev = jnp.moveaxis(s_prev, 0, 1)
    o = o_intra + jnp.einsum('bnhcd,bnhdv->bnhcv', q_dec, s_prev)
    return o.transpose(0, 1, 3, 2, 4).reshape(B, S, H, DV)

def to_blocks(t, nb):
    return jnp.moveaxis(t.reshape((t.shape[0], nb, Q_BLOCK) + t.shape[2:]), 1, 0)

def dsa_attention(q, k, v, iq, ik, iw):
    B, S, H, Dh = q.shape
    L = k.shape[1]
    top_k = min(DSA_TOPK, L // 4)
    nb = S // Q_BLOCK
    key_pos = jnp.arange(L)
    starts = jnp.arange(nb) * Q_BLOCK
    gather = jax.vmap(lambda table, idx: table[idx])
    scale = Dh ** -0.5

    def one_block(args):
        qb, iqb, iwb, t0 = args
        q_pos = t0 + jnp.arange(Q_BLOCK)
        rel = jax.nn.relu(jnp.einsum('bqhd,bsd->bqhs', iqb, ik))
        score = jnp.einsum('bqhs,bqh->bqs', rel, iwb).astype(jnp.float32)
        visible = key_pos[None, :] <= q_pos[:, None]
        score = jnp.where(visible[None], score, NEG_INF)
        _, idx = lax.top_k(score, top_k)
        valid = idx <= q_pos[None, :, None]
        k_sel = gather(k, idx)
        v_sel = gather(v, idx)
        logits = jnp.einsum('bqhd,bqkhd->bqhk', qb, k_sel).astype(jnp.float32) * scale
        logits = jnp.where(valid[:, :, None, :], logits, NEG_INF)
        p = jax.nn.softmax(logits, axis=-1).astype(v.dtype)
        return jnp.einsum('bqhk,bqkhd->bqhd', p, v_sel)

    out = lax.map(one_block, (to_blocks(q, nb), to_blocks(iq, nb), to_blocks(iw, nb), starts))
    return jnp.moveaxis(out, 0, 1).reshape(B, S, H, Dh)

def causal_block_attention(q, k, v):
    B, S, H, Dq = q.shape
    Dv = v.shape[-1]
    L = k.shape[1]
    nb = S // Q_BLOCK
    key_pos = jnp.arange(L)
    starts = jnp.arange(nb) * Q_BLOCK
    scale = Dq ** -0.5

    def one_block(args):
        qb, t0 = args
        q_pos = t0 + jnp.arange(Q_BLOCK)
        logits = jnp.einsum('bqhd,bshd->bhqs', qb, k).astype(jnp.float32) * scale
        visible = key_pos[None, :] <= q_pos[:, None]
        logits = jnp.where(visible[None, None], logits, NEG_INF)
        p = jax.nn.softmax(logits, axis=-1).astype(v.dtype)
        return jnp.einsum('bhqs,bshd->bqhd', p, v)

    out = lax.map(one_block, (to_blocks(q, nb), starts))
    return jnp.moveaxis(out, 0, 1).reshape(B, S, H, Dv)

def token_mix(h, pos, w_in, gla_gate_up, gla_gate_bias, gla_out_norm,
              dsa_q_norm, dsa_k_norm, dsa_out_norm,
              mla_q_latent_norm, mla_kv_latent_norm, mla_w_uq, mla_w_ukv,
              mla_q_norm, mla_k_norm, mla_out_norm, w_out):
    B, S, _ = h.shape
    proj = h @ w_in
    (g_q, g_k, g_v, g_gate, g_lr, d_q, d_k, d_v,
     i_q, i_k, i_w, m_cq, m_ckv, m_kr) = split_columns(proj)

    def heads(t, n):
        return t.reshape(B, S, n, t.shape[-1] // n)

    log_a = jax.nn.log_sigmoid((g_lr @ gla_gate_up + gla_gate_bias).astype(jnp.float32)) / GLA_TAU
    o_gla = gla_chunked(heads(g_q, GLA_HEADS), heads(g_k, GLA_HEADS),
                        heads(g_v, GLA_HEADS), heads(log_a, GLA_HEADS)).astype(h.dtype)
    o_gla = rms_norm(o_gla, gla_out_norm).reshape(B, S, GLA_WIDTH) * jax.nn.silu(g_gate)

    q_d = rms_norm(heads(d_q, DSA_HEADS), dsa_q_norm)
    k_d = rms_norm(heads(d_k, DSA_HEADS), dsa_k_norm)
    v_d = heads(d_v, DSA_HEADS)
    idx_w = i_w * ((IDX_HEADS * IDX_DIM) ** -0.5)
    o_dsa = dsa_attention(q_d, k_d, v_d, heads(i_q, IDX_HEADS), i_k, idx_w)
    o_dsa = rms_norm(o_dsa, dsa_out_norm).reshape(B, S, DSA_WIDTH)

    q_m = heads(rms_norm(m_cq, mla_q_latent_norm) @ mla_w_uq, MLA_HEADS)
    kv_m = heads(rms_norm(m_ckv, mla_kv_latent_norm) @ mla_w_ukv, MLA_HEADS)
    k_nope, v_m = kv_m[..., :MLA_NOPE_DIM], kv_m[..., MLA_NOPE_DIM:]
    k_rope = jnp.broadcast_to(m_kr[:, :, None, :], (B, S, MLA_HEADS, MLA_ROPE_DIM))
    q_m = rms_norm(q_m, mla_q_norm)
    k_m = rms_norm(jnp.concatenate([k_nope, k_rope], axis=-1), mla_k_norm)
    q_m = jnp.concatenate([q_m[..., :MLA_NOPE_DIM], rotary(q_m[..., MLA_NOPE_DIM:], pos)], axis=-1)
    k_m = jnp.concatenate([k_m[..., :MLA_NOPE_DIM], rotary(k_m[..., MLA_NOPE_DIM:], pos)], axis=-1)
    o_mla = causal_block_attention(q_m, k_m, v_m)
    o_mla = rms_norm(o_mla, mla_out_norm).reshape(B, S, MLA_WIDTH)

    return jnp.concatenate([o_gla, o_dsa, o_mla], axis=-1) @ w_out

def squared_relu_mlp(h, w_up, w_down):
    return jnp.square(jax.nn.relu(h @ w_up)) @ w_down

def setup_inputs(seed: int = 0) -> dict:
    key = jax.random.key(seed)
    ks = jax.random.split(key, 24)
    f32 = jnp.float32

    def dense(k, shape, fan_in, scale=1.0):
        return jax.random.normal(k, shape, f32) * (scale * fan_in ** -0.5)

    def gain(k, shape):
        return 1.0 + 0.02 * jax.random.normal(k, shape, f32)

    res_scale = (2 * DEPTH) ** -0.5
    return {
        "x": jax.random.normal(ks[0], (BATCH, SEQ, D_MODEL), f32),
        "attn_norm": gain(ks[1], (DEPTH, D_MODEL)),
        "w_in": dense(ks[2], (DEPTH, D_MODEL, D_IN), D_MODEL),
        "gla_gate_up": dense(ks[3], (DEPTH, GLA_GATE_RANK, GLA_HEADS * GLA_DK), GLA_GATE_RANK),
        "gla_gate_bias": 0.1 * jax.random.normal(ks[4], (DEPTH, GLA_HEADS * GLA_DK), f32),
        "gla_out_norm": gain(ks[5], (DEPTH, GLA_HEADS, GLA_DV)),
        "dsa_q_norm": gain(ks[6], (DEPTH, DSA_HEAD_DIM)),
        "dsa_k_norm": gain(ks[7], (DEPTH, DSA_HEAD_DIM)),
        "dsa_out_norm": gain(ks[8], (DEPTH, DSA_HEADS, DSA_HEAD_DIM)),
        "mla_q_latent_norm": gain(ks[9], (DEPTH, MLA_Q_RANK)),
        "mla_kv_latent_norm": gain(ks[10], (DEPTH, MLA_KV_RANK)),
        "mla_w_uq": dense(ks[11], (DEPTH, MLA_Q_RANK, MLA_HEADS * MLA_QK_DIM), MLA_Q_RANK),
        "mla_w_ukv": dense(ks[12], (DEPTH, MLA_KV_RANK, MLA_HEADS * (MLA_NOPE_DIM + MLA_V_DIM)), MLA_KV_RANK),
        "mla_q_norm": gain(ks[13], (DEPTH, MLA_QK_DIM)),
        "mla_k_norm": gain(ks[14], (DEPTH, MLA_QK_DIM)),
        "mla_out_norm": gain(ks[15], (DEPTH, MLA_HEADS, MLA_V_DIM)),
        "w_out": dense(ks[16], (DEPTH, D_MIX, D_MODEL), D_MIX, res_scale),
        "mlp_norm": gain(ks[17], (DEPTH, D_MODEL)),
        "w_up": dense(ks[18], (DEPTH, D_MODEL, D_FF), D_MODEL),
        "w_down": dense(ks[19], (DEPTH, D_FF, D_MODEL), D_FF, res_scale),
    }

def reference(x, attn_norm, w_in, gla_gate_up, gla_gate_bias, gla_out_norm,
              dsa_q_norm, dsa_k_norm, dsa_out_norm,
              mla_q_latent_norm, mla_kv_latent_norm, mla_w_uq, mla_w_ukv,
              mla_q_norm, mla_k_norm, mla_out_norm, w_out,
              mlp_norm, w_up, w_down):
    pos = jnp.arange(x.shape[1], dtype=jnp.int32)
    for l in range(DEPTH):
        h = rms_norm(x, attn_norm[l])
        x = x + token_mix(h, pos, w_in[l], gla_gate_up[l], gla_gate_bias[l], gla_out_norm[l],
                          dsa_q_norm[l], dsa_k_norm[l], dsa_out_norm[l],
                          mla_q_latent_norm[l], mla_kv_latent_norm[l], mla_w_uq[l], mla_w_ukv[l],
                          mla_q_norm[l], mla_k_norm[l], mla_out_norm[l], w_out[l])
        h = rms_norm(x, mlp_norm[l])
        x = x + squared_relu_mlp(h, w_up[l], w_down[l])
    return x


_drawn_inputs = setup_inputs


def setup_inputs(seed=0):
    import zlib

    import numpy as np

    out = dict(_drawn_inputs(seed))
    spreads = {}
    factors = {'gla_gate_bias': 3.843,
     'gla_out_norm': 6.698,
     'dsa_q_norm': 6.673,
     'dsa_k_norm': 6.726,
     'dsa_out_norm': 6.32,
     'mla_q_latent_norm': 7.266,
     'mla_kv_latent_norm': 4.711,
     'mla_q_norm': 6.879,
     'mla_k_norm': 7.346,
     'mla_out_norm': 5.911,
     'mlp_norm': 3.119}
    for name, (base, spread) in spreads.items():
        noise = np.random.default_rng([zlib.crc32(name.encode()), seed]).standard_normal(out[name].shape)
        drawn = base * np.exp(spread * noise) if base else spread * noise
        out[name] = __import__('jax').numpy.asarray(drawn.astype(out[name].dtype))
    for name, factor in factors.items():
        out[name] = (out[name] * factor).astype(out[name].dtype)
    return out
```

```python
from contextlib import ExitStack

import numpy as np

import concourse.bass as bass
from concourse import mybir

F32 = mybir.dt.float32
F32R = mybir.dt.float32r
ALU = mybir.AluOpType
ACT = mybir.ActivationFunctionType

P = 128
T = 512
D = 1024
KB = D // P
TB = T // P
DEPTH = 2
D_FF = 4096
EPS = 1e-6
NEG = -1e30
TAKEN = -3e38
GLA_H, GLA_DK, GLA_DV, RANK, TAU, CHUNK = 4, 64, 128, 16, 16.0, 64
H, DH = 4, 64
IDX_H, IDX_D = 8, 32
TOPK = min(256, T // 4)
SEL_AT = {1: 0, 2: 2 * P, 3: 5 * P, 4: 9 * P}
Q_RANK, KV_RANK, NOPE, ROPE = 192, 128, 64, 32
QK = NOPE + ROPE
NCHUNK = T // CHUNK

_WIDTHS = [256, 256, 512, 512, RANK, 256, 256, 256, IDX_H * IDX_D, IDX_D, IDX_H, Q_RANK, KV_RANK, ROPE]
_C = np.concatenate([[0], np.cumsum(_WIDTHS)]).tolist()
GQ, GK, GV, GG, GLR, DQ, DK, DV, IQ, IK, IW, CQ, CKV, KR, D_IN = _C

UNITS = ["iq0", "iq1", "small", "dv", "dv", "dv", "cq", "ckv", "dq0", "dq1", "dk0", "dk1",
         "gq0", "gq1", "gk0", "gk1", "gg0", "gg1", "gg2", "gg3", "gv", "gv", "gv", "gv"]
N_IN = len(UNITS)
N_OUT = KB
GROUPS = D_FF // (8 * P)
N_MLP = GROUPS * 16
N_UNIT = N_IN + N_OUT + N_MLP
AHEAD = 2
DVW = H * DH + IDX_H + RANK
DV_BLOCKS = [(0, 3), (3, 6), (6, 8)]

G_ATTN, G_MLP, G_BIAS, G_GLA, G_DQ, G_DK, G_DSA, G_QLAT, G_KVLAT, G_MQ, G_MK, G_MLA = (
    0, 8, 16, 18, 22, 23, 24, 26, 28, 29, 30, 31)
W_GATE = 33
W_UQ = W_GATE + 256
W_UKV = W_UQ + 2 * H * QK
N_PAR = W_UKV + H * (NOPE + DH)

C_ID = 0
C_BLK = C_ID + P
C_ROT = C_BLK + P
C_EPS = C_ROT + ROPE
C_GM = C_EPS + 1
C_CAUSAL = C_GM + CHUNK
C_SCAN = C_CAUSAL + T
C_COS = C_SCAN + T
C_SIN = C_COS + T
N_CONST = C_SIN + T


class Sem:

    def __init__(self, ctx, nc, name, per, start=0):
        self.sem = ctx.enter_context(nc.semaphore(name))
        self.per, self.start = per, start

    def at(self, layer, k):
        return self.sem, layer * self.per + (self.start + k + 1)


USES = (
    [("iq0", 0), ("xstat", 6), ("iq1", 1), ("rcol", 7), ("small", 0),
     ("dv0", 4), ("dv1", 5), ("dv2", 6), ("dv3", 7), ("cq", 1), ("glr", 6)]
    + [(f"rel{i}", 2 + i % 2) for i in range(3 * IDX_H)]
    + [("ckv", 0), ("gz0", 4), ("gz1", 5), ("dq0", 1), ("cqst", 6), ("ckvst", 7)]
    + [("dq1", 0), ("dqst0", 2), ("mq0", 4), ("dk0", 1), ("mqst0", 6), ("mrot0", 7)]
    + [("dqst1", 3), ("mq1", 5), ("dk1", 0), ("mqst1", 6), ("mrot1", 7), ("dkst0", 2), ("mq2", 4)]
    + [("gq0", 1), ("mqst2", 6), ("mrot2", 7), ("dkst1", 3), ("mq3", 5)]
    + [("gq1", 0), ("mqst3", 6), ("mrot3", 7), ("krot", 2), ("mk0", 4)]
    + [("gk0", 1), ("mkst0", 6), ("mk1", 5), ("gk1", 0), ("mkst1", 7), ("mk2", 4)]
    + [("gg0", 1), ("mkst2", 6), ("mk3", 5), ("gg1", 0), ("mkst3", 7), ("mv0", 4)]
    + [("gg2", 1), ("mv1", 5), ("ketr0", 2), ("ketr1", 3), ("gg3", 0)]
    + [("gv0", 4), ("gv1", 5), ("gv2", 6), ("gv3", 7)]
    + [("inc00", 4), ("inc01", 5), ("inc10", 6), ("inc11", 7)]
    + [(f"gs{h}", 2 + h % 2) for h in range(GLA_H)]
    + [(f"go{h}", h % 2) for h in range(GLA_H)] + [(f"gst{h}", 6 + h % 2) for h in range(GLA_H)]
    + [(f"{a}lg{i}", 2 + i % 2) for a in "md" for i in range(H * TB)]
    + [(f"{a}pt{i}", 4 + i % 2) for a in "md" for i in range(H * TB)]
    + [(f"{a}o{p}", p) for a in "md" for p in range(2)]
    + [(f"{a}ost{p}", 6 + p) for a in "md" for p in range(2)]
    + [(f"out{d}", d % 2) for d in range(KB)] + [("mstat", 6)]
)
NO_FILL = ("mo0", "mo1", "do0", "do1")


class Banks:

    def __init__(self, ctx, nc):
        self.place, self.per, self.fills = {}, [0] * 8, [0] * 8
        for name, b in USES:
            self.place[name] = (b, self.per[b], self.fills[b])
            self.per[b] += 1
            self.fills[b] += name not in NO_FILL
        self.t = [ctx.enter_context(nc.psum_tensor(f"bank{b}", [P, T], F32)) for b in range(8)]
        self.fill = [ctx.enter_context(nc.semaphore(f"bank{b}_filled")) for b in range(8)]
        self.free = [ctx.enter_context(nc.semaphore(f"bank{b}_freed")) for b in range(8)]

    def __getitem__(self, name):
        return self.t[self.place[name][0]]

    def filled(self, l, name):
        b, _, k = self.place[name]
        return self.fill[b], l * self.fills[b] + (k + 1)

    def vacant(self, l, name):
        b, k, _ = self.place[name]
        return self.free[b], l * self.per[b] + (k + 1)

    def freed(self, l, name):
        b, k, _ = self.place[name]
        return self.free[b], l * self.per[b] + (k + 2)

    def on_fill(self, name):
        return self.fill[self.place[name][0]], 1

    def on_read(self, name):
        return self.free[self.place[name][0]], 1


NORMS = (["cqst", "ckvst", "dqst0", "mqst0", "dqst1", "mqst1", "dkst0", "mqst2", "dkst1", "mqst3"]
         + [f"mkst{h}" for h in range(H)] + [f"gst{h}" for h in range(GLA_H)]
         + ["most0", "most1", "dost0", "dost1"])
N_NORM = len(NORMS)

VEC_LINKS = 400
ACT_LINKS = 2


def build_trunk(nc, x_in, stream, params, consts, out):
    with ExitStack() as ctx:
        base = nc.sbuf_base if isinstance(nc.sbuf_base, int) else nc.sbuf_base()
        slab = ctx.enter_context(nc.sbuf_tensor("slab", [P, 207 * 256], F32))
        del slab
        base = (base + 31) // 32 * 32
        cursor = [base]

        def place(name, shape, dt=F32, at=None):
            words = int(np.prod(shape[1:]))
            off = cursor[0] if at is None else at
            if at is None:
                cursor[0] += (4 * words + 31) // 32 * 32
                assert cursor[0] <= base + 207 * 1024, (name, cursor[0] - base)
            t = nc.alloc_sbuf_tensor_at(name, list(shape), dt, offset=off)
            return t, off

        x, _ = place("x", [P, KB, T])
        xgh, _ = place("xgh", [P, KB, T], F32R)
        xgl, _ = place("xgl", [P, KB, T], F32R)
        raw, _ = place("raw", [P, 2, 1024])
        wh, _ = place("wh", [P, 2, 1024], F32R)
        wl, _ = place("wl", [P, 2, 1024], F32R)
        gqp, g0 = place("gqp", [P, GLA_H, T])
        kinv, _ = place("kinv", [P, 2, T])
        ke, ke0 = place("ke", [P, 2, TB, 256])
        gvt, _ = place("gvt", [P, TB, GLA_H * GLA_DV])
        e1, _ = place("e1", [P, 2, T])
        hh, _ = place("hh", [P, 8, T], F32R, at=g0)
        hl, _ = place("hl", [P, 8, T], F32R, at=g0 + 16384)
        cqn, _ = place("cqn", [P, 2, T], at=ke0)
        ckvn, _ = place("ckvn", [P, T], at=ke0 + 4096)
        qT, m0 = place("qT", [P, H, T])
        kT, _ = place("kT", [P, H, T])
        dqp, _ = place("dqp", [P, H, T])
        dkn, _ = place("dkn", [P, 2, T])
        vm, _ = place("vm", [P, TB, H * DH])
        xmh, _ = place("xmh", [P, KB, T], F32R, at=m0)
        xml, _ = place("xml", [P, KB, T], F32R, at=m0 + 16384)
        iqT, a0 = place("iqT", [P, 2, T])
        ikp, _ = place("ikp", [P, 4, T])
        st, _ = place("st", [P, NCHUNK, 2, GLA_DV], at=a0)
        sct, _ = place("sct", [P, 2, TB, P], at=a0 + 8192)
        gg, _ = place("gg", [P, GLA_H, T])
        sel, _ = place("sel", [P, SEL_AT[4]])
        dvt, _ = place("dvt", [P, TB, DVW])
        pb, pb0 = place("pb", [P, 2, T])
        ptb, pt0 = place("ptb", [P, 2, T])
        e2, _ = place("e2", [P, 2, T], at=pt0)
        dqr, _ = place("dqr", [P, 2, T], at=pb0)
        sqb, _ = place("sqb", [P, 2, T])
        lnb, _ = place("lnb", [P, T])
        rsb, _ = place("rsb", [P, 2, T])
        tf, _ = place("tf", [P, 2, T])
        rb, _ = place("rb", [P, T])
        glrs, _ = place("glrs", [RANK, T], at=pb0 + 2048)
        con, _ = place("con", [P, N_CONST])
        par, _ = place("par", [P, N_PAR])
        ones, _ = place("ones", [P, P])
        rcol, _ = place("rcol", [P, TB])
        iws, _ = place("iws", [P, 3, IDX_H])
        m8, _ = place("m8", [P, 3, 8])
        mx, _ = place("mx", [P, 2, H * TB])
        nb, _ = place("nb", [P, 2, H * TB])
        rsum, _ = place("rsum", [P, 2, H * TB])
        rinv, _ = place("rinv", [P, 2, H * TB])

        ident = con[:, C_ID:C_ID + P]
        cos = con[64:QK, C_COS:C_COS + T]
        sin = con[64:QK, C_SIN:C_SIN + T]
        blk = con[:, C_BLK:C_BLK + P]
        eps = con[:, C_EPS:C_EPS + 1]

        def causal(qb):
            return con[:, C_CAUSAL + (TB - 1 - qb) * P:C_CAUSAL + T]

        def gain(c, lo=0, hi=P):
            return par[lo:hi, c:c + 1]

        B = Banks(ctx, nc)

        def S(name, per=1, start=0):
            return Sem(ctx, nc, name, per, start)

        x_loaded = ctx.enter_context(nc.semaphore("x_loaded"))
        const_loaded = ctx.enter_context(nc.semaphore("const_loaded"))
        par_loaded = ctx.enter_context(nc.semaphore("par_loaded"))
        raw_loaded = [ctx.enter_context(nc.semaphore(f"raw_loaded{i}")) for i in range(2)]
        out_stored = ctx.enter_context(nc.semaphore("out_stored"))
        hi_ready = S("hi_ready", N_UNIT)
        lo_ready = S("lo_ready", N_UNIT, start=2)
        token_spent = S("token_spent", 5)
        x_ready = S("x_ready", 8 * GROUPS, start=8)
        xh_ready = S("xh_ready", 2 * KB)
        xl_ready = S("xl_ready", 2 * KB, start=1)
        sq_ready = S("sq_ready", 2 * KB)
        sq_summed = S("sq_summed", 2 * KB)
        rb_ready = S("rb_ready", 2)
        ones_ready = S("ones_ready", 0)
        zeroed = S("zeroed", 5)
        ik_ready = S("ik_ready", 4)
        kr_ready = S("kr_ready")
        rel_used = S("rel_used", 3 * IDX_H)
        gate_ready = S("gate_ready", 2)
        decay_ready = S("decay_ready", 2)
        exp_ready = S("exp_ready", 2)
        nsq_ready = S("nsq_ready", N_NORM)
        nrs_ready = S("nrs_ready", N_NORM, start=1)
        nrs_used = S("nrs_used", N_NORM, start=2)
        krsq_ready = S("krsq_ready")
        krg_ready = S("krg_ready")
        qg_ready = S("qg_ready", H)
        kend_ready = S("kend_ready", 2)
        gexp_ready = S("gexp_ready", GLA_H)
        gg_ready = S("gg_ready", GLA_H)
        lg_ready = S("lg_ready", 2 * H * TB)
        p_ready = S("p_ready", 2 * H * TB)
        pn_ready = S("pn_ready", 2 * H * TB)
        weighed = S("weighed", 2 * H * TB, start=2)
        mixf_ready = S("mixf_ready", KB)
        mixh_ready = S("mixh_ready", KB)
        mix_ready = S("mix_ready", KB)
        up_filled = [S(f"up_filled{b}", GROUPS * 4) for b in range(2)]
        up_freed = [S(f"up_freed{b}", GROUPS * 4, start=1) for b in range(2)]
        dn_filled = [S(f"down_filled{b}", GROUPS * 4) for b in range(2)]
        dn_freed = [S(f"down_freed{b}", GROUPS * 4, start=1) for b in range(2)]
        hh_ready = S("hh_ready", GROUPS * 8)
        hid_ready = S("hid_ready", GROUPS * 8)
        hl_ready = S("hl_ready", GROUPS * 8, start=2)
        vec_chain = S("vec_chain", VEC_LINKS)
        act_chain = S("act_chain", ACT_LINKS)

        block = ctx.enter_context(nc.Block())

        def unit_done(l, u):
            if u >= N_IN:
                return B.filled(l, f"out{u - N_IN}")
            if UNITS[u] == "dv":
                return B.filled(l, "dv3") if u == 5 else token_spent.at(l, u - 3)
            if UNITS[u] == "gv":
                return B.filled(l, "gv3") if u == 23 else token_spent.at(l, u - 20 + 2)
            return B.filled(l, UNITS[u])


        passed = ctx.enter_context(nc.semaphore("passed"))

        def alone(eng):
            eng.sem_inc(passed, 1)

        def norm_index(name):
            return NORMS.index(name)

        REL = [(qb, h) for qb in (3, 2, 1) for h in range(IDX_H)]

        def scores_of(qb):
            return sel[:, SEL_AT[qb]:SEL_AT[qb + 1]]

        @block.sync
        def _(sp):
            sp.dma_start(x[:], x_in).then_inc(x_loaded, 16)
            with sp.Fori(0, (DEPTH * N_UNIT + AHEAD) // 2) as i:
                for s in range(2):
                    sp.wait_ge(lo_ready.sem, 2 * i + (s + 1))
                    sp.dma_start(raw[:, s], stream[2 * i + s]).then_inc(raw_loaded[s], 16)
            for d in range(KB):
                sp.wait_ge(*x_ready.at(DEPTH, d - KB))
                sp.dma_start(out[:, d], x[:, d]).then_inc(out_stored, 16)
            sp.wait_ge(out_stored, 16 * KB)

        @block.gpsimd
        def _(pool):
            pool.memset(ones[:], 1.0).then_inc(ones_ready.sem, 1)

            def sum_squares(l, half):
                for k in range(KB):
                    e = half * KB + k
                    pool.wait_ge(*sq_ready.at(l, e))
                    if k == 0:
                        alone(pool)
                        op = pool.tensor_copy(lnb[:], sqb[:, k % 2])
                    else:
                        pool.wait_ge(*sq_summed.at(l, e - 1))
                        op = pool.tensor_tensor(lnb[:], lnb[:], sqb[:, k % 2], ALU.add)
                    op.then_inc(sq_summed.sem, 1)

            with pool.Fori(0, DEPTH) as l:
                pool.wait_ge(*xl_ready.at(l, -1))
                pool.dma_start(par[:], params[l]).then_inc(par_loaded, 16)
                sum_squares(l, 0)
                pool.wait_ge(*x_ready.at(l, -1))
                alone(pool)
                pool.memset(ikp[:], 0.0).then_inc(zeroed.sem, 1)
                pool.memset(dqp[:], 0.0).then_inc(zeroed.sem, 1)
                pool.memset(gqp[:], 0.0).then_inc(zeroed.sem, 1)
                pool.wait_ge(*B.filled(l, "rel23"))
                alone(pool)
                pool.memset(sct[:], 0.0).then_inc(zeroed.sem, 1)
                pool.wait_ge(*B.filled(l, "mv1"))
                alone(pool)
                pool.memset(ke[:], 0.0).then_inc(zeroed.sem, 1)
                sum_squares(l, 1)
                with pool.Fori(0, GROUPS) as g:
                    for d in range(KB):
                        pool.wait_ge(dn_freed[d % 2].sem, l * 16 + g * 4 + (d // 2 + 2))
                        pool.tensor_tensor(x[:, d], x[:, d], rsb[:, d % 2], ALU.add).then_inc(x_ready.sem, 1)

        @block.tensor
        def _(pe):
            def weights_ready(l, u):
                pe.wait_ge(*lo_ready.at(l, u))

            def n_block(k):
                return slice(k * P, (k + 1) * P)

            def feature_unit(l, u, name, act_h, act_l, order=range(KB), before=None):
                s = u % 2
                weights_ready(l, u)
                pe.wait_ge(*B.vacant(l, name))
                bank = B[name]
                order = list(order)
                for n, k in enumerate(order):
                    if before is not None:
                        before(k)
                    wk_h, wk_l = wh[:, s, n_block(k)], wl[:, s, n_block(k)]
                    last = n == len(order) - 1
                    pe.matmul(bank[:], wk_l, act_h[:, k], start=(n == 0), stop=False)
                    pe.matmul(bank[:], wk_h, act_h[:, k], start=False, stop=False)
                    m = pe.matmul(bank[:], wk_h, act_l[:, k], start=False, stop=last)
                m.then_inc(*B.on_fill(name))

            def token_units(l, u0, blocks, width, stem):
                for i, (ka, kb) in enumerate(blocks):
                    u = u0 + i
                    s = u % 2
                    weights_ready(l, u)
                    for tb in range(TB):
                        bank = B[f"{stem}{tb}"]
                        if i == 0:
                            pe.wait_ge(*B.vacant(l, f"{stem}{tb}"))
                        for k in range(ka, kb):
                            c = (k - ka) * width
                            r_h, r_l = wh[:, s, c:c + width], wl[:, s, c:c + width]
                            a_h = xgh[:, k, tb * P:(tb + 1) * P]
                            a_l = xgl[:, k, tb * P:(tb + 1) * P]
                            last = k == KB - 1
                            pe.matmul(bank[:, 0:width], a_l, r_h, start=(k == 0), stop=False)
                            pe.matmul(bank[:, 0:width], a_h, r_h, start=False, stop=False)
                            m = pe.matmul(bank[:, 0:width], a_h, r_l, start=False, stop=last)
                        if i == len(blocks) - 1 and tb < TB - 1:
                            m.then_inc(*B.on_fill(f"{stem}{tb}"))
                    if i == len(blocks) - 1:
                        m.then_inc(*B.on_fill(f"{stem}{TB - 1}"))
                    else:
                        m.then_inc(token_spent.sem, 1)

            def stat(l, name, lhsT, rhs, rows=P):
                pe.wait_ge(*nsq_ready.at(l, norm_index(name)))
                pe.wait_ge(*B.vacant(l, name))
                pe.matmul(B[name][0:rows, :], lhsT, rhs, start=True, stop=True).then_inc(*B.on_fill(name))

            def sq_of(name):
                return sqb[:, norm_index(name) % 2]

            pe.wait_ge(const_loaded, 16)
            pe.wait_ge(*ones_ready.at(0, 0))
            with pe.Fori(0, DEPTH) as l:
                def x_part(k):
                    pe.wait_ge(*xl_ready.at(l, k))

                def unit(u, before=None):
                    feature_unit(l, u, UNITS[u], xgh, xgl, before=before)

                def total(name, half):
                    pe.wait_ge(*sq_summed.at(l, half * KB + KB - 1))
                    pe.wait_ge(*B.vacant(l, name))
                    pe.matmul(B[name][:], ones[:], lnb[:], start=True, stop=True).then_inc(*B.on_fill(name))

                def mla_q(h):
                    name = f"mq{h}"
                    pe.wait_ge(*nrs_used.at(l, 0))
                    pe.wait_ge(*B.vacant(l, name))
                    c = W_UQ + h * QK
                    pe.matmul(B[name][0:QK], par[:, c:c + QK], cqn[:, 0], start=True, stop=False)
                    c += H * QK
                    pe.matmul(B[name][0:QK], par[0:64, c:c + QK], cqn[0:64, 1], start=False, stop=True)\
                        .then_inc(*B.on_fill(name))

                def mla_q_rest(h):
                    stat(l, f"mqst{h}", ones[0:QK, 0:QK], sq_of(f"mqst{h}")[0:QK], QK)
                    pe.wait_ge(*qg_ready.at(l, h))
                    pe.wait_ge(*B.vacant(l, f"mrot{h}"))
                    alone(pe)
                    pe.matmul(B[f"mrot{h}"][64:QK], con[64:QK, C_ROT:C_ROT + ROPE], tf[64:QK, h % 2],
                              start=True, stop=True).then_inc(*B.on_fill(f"mrot{h}"))

                def mla_k(h):
                    name = f"mk{h}"
                    pe.wait_ge(*nrs_used.at(l, 1))
                    pe.wait_ge(*B.vacant(l, name))
                    c = W_UKV + h * (NOPE + DH)
                    pe.matmul(B[name][0:NOPE], par[:, c:c + NOPE], ckvn[:], start=True, stop=True)\
                        .then_inc(*B.on_fill(name))

                def mla_k_stat(h):
                    name = f"mkst{h}"
                    pe.wait_ge(*nsq_ready.at(l, norm_index(name)))
                    pe.wait_ge(*krsq_ready.at(l, 0))
                    pe.wait_ge(*B.vacant(l, name))
                    pe.matmul(B[name][0:QK], ones[0:NOPE, 0:QK], sq_of(name)[0:NOPE], start=True, stop=False)
                    pe.matmul(B[name][0:QK], ones[64:QK, 0:QK], cqn[64:QK, 1], start=False, stop=True)\
                        .then_inc(*B.on_fill(name))

                def mla_v(i):
                    name = f"mv{i}"
                    pe.wait_ge(*B.vacant(l, name))
                    vcols = par[:, W_UKV:N_PAR].rearrange("p (h c) -> p h c", h=H)[:, :, NOPE:NOPE + DH]
                    for j in range(2):
                        tb = 2 * i + j
                        m = pe.matmul(B[name][:, j * 256:(j + 1) * 256], ckvn[:, tb * P:(tb + 1) * P], vcols,
                                      start=True, stop=True)
                    m.then_inc(*B.on_fill(name))

                unit(0, before=x_part)
                total("xstat", 0)
                unit(1)
                pe.wait_ge(*rb_ready.at(l, 0))
                pe.wait_ge(*B.vacant(l, "rcol"))
                for tb in range(TB):
                    m = pe.transpose(B["rcol"][:, tb * P:(tb + 1) * P], rb[:, tb * P:(tb + 1) * P], ident)
                m.then_inc(*B.on_fill("rcol"))
                unit(2)
                token_units(l, 3, DV_BLOCKS, DVW, "dv")
                unit(6)
                pe.wait_ge(*B.freed(l, "dv3"))
                pe.wait_ge(*B.vacant(l, "glr"))
                for tb in range(TB):
                    m = pe.transpose(B["glr"][0:RANK, tb * P:(tb + 1) * P],
                                     dvt[:, tb, DVW - RANK:DVW], ident)
                m.then_inc(*B.on_fill("glr"))
                pe.wait_ge(*B.freed(l, "iq1"))
                pe.wait_ge(*ik_ready.at(l, 3))
                for i, (qb, h) in enumerate(REL):
                    pe.wait_ge(*B.vacant(l, f"rel{i}"))
                    n = (qb + 1) * P
                    pe.matmul(B[f"rel{i}"][:, 0:n], iqT[:, h // 4, qb * P:(qb + 1) * P], ikp[:, h % 4, 0:n],
                              start=True, stop=True).then_inc(*B.on_fill(f"rel{i}"))
                unit(7)
                pe.wait_ge(*B.freed(l, "glr"))
                for pr in range(2):
                    pe.wait_ge(*B.vacant(l, f"gz{pr}"))
                    pe.matmul(B[f"gz{pr}"][:], par[0:RANK, W_GATE + pr * P:W_GATE + (pr + 1) * P], glrs[:],
                              start=True, stop=True).then_inc(*B.on_fill(f"gz{pr}"))
                unit(8)
                pe.wait_ge(*nsq_ready.at(l, 0))
                pe.wait_ge(*B.vacant(l, "cqst"))
                pe.matmul(B["cqst"][:], ones[:], sqb[:, 0], start=True, stop=False)
                pe.matmul(B["cqst"][:], ones[0:64, :], lnb[0:64], start=False, stop=True)\
                    .then_inc(*B.on_fill("cqst"))
                stat(l, "ckvst", ones[:], sq_of("ckvst"))
                unit(9)
                stat(l, "dqst0", blk, sq_of("dqst0"))
                mla_q(0)
                unit(10)
                mla_q_rest(0)
                stat(l, "dqst1", blk, sq_of("dqst1"))
                mla_q(1)
                unit(11)
                mla_q_rest(1)
                stat(l, "dkst0", blk, sq_of("dkst0"))
                mla_q(2)
                unit(12)
                mla_q_rest(2)
                stat(l, "dkst1", blk, sq_of("dkst1"))
                mla_q(3)
                unit(13)
                mla_q_rest(3)
                pe.wait_ge(*krg_ready.at(l, 0))
                pe.wait_ge(*B.vacant(l, "krot"))
                alone(pe)
                pe.matmul(B["krot"][64:QK], con[64:QK, C_ROT:C_ROT + ROPE], kT[64:QK, 2],
                          start=True, stop=True).then_inc(*B.on_fill("krot"))
                mla_k(0)
                unit(14)
                mla_k_stat(0)
                mla_k(1)
                unit(15)
                mla_k_stat(1)
                mla_k(2)
                unit(16)
                mla_k_stat(2)
                mla_k(3)
                unit(17)
                mla_k_stat(3)
                mla_v(0)
                unit(18)
                mla_v(1)
                for pr in range(2):
                    pe.wait_ge(*kend_ready.at(l, pr))
                    pe.wait_ge(*B.vacant(l, f"ketr{pr}"))
                    for tb in range(TB):
                        m = pe.transpose(B[f"ketr{pr}"][:, tb * P:(tb + 1) * P],
                                         tf[:, pr, tb * P:(tb + 1) * P], ident)
                    m.then_inc(*B.on_fill(f"ketr{pr}"))
                unit(19)
                token_units(l, 20, [(0, 2), (2, 4), (4, 6), (6, 8)], GLA_H * GLA_DV, "gv")

                for tb in range(TB):
                    pe.wait_ge(*B.freed(l, f"gv{tb}"))
                pe.wait_ge(*B.freed(l, "ketr1"))
                for pr in range(2):
                    for half in range(2):
                        name = f"inc{pr}{half}"
                        pe.wait_ge(*B.vacant(l, name))
                        for c in range(4 * half, min(4 * half + 4, NCHUNK - 1)):
                            for hp in range(2):
                                h = 2 * pr + hp
                                m = pe.matmul(B[name][hp * 64:(hp + 1) * 64, (c % 4) * P:(c % 4 + 1) * P],
                                              ke[:, c % 2, c // 2, h * GLA_DK:(h + 1) * GLA_DK],
                                              gvt[:, c // 2, h * GLA_DV:(h + 1) * GLA_DV], start=True, stop=True)
                        m.then_inc(*B.on_fill(name))
                pe.wait_ge(*B.freed(l, "gq1"))
                pe.wait_ge(*B.freed(l, "gk1"))

                def gla_scores(h):
                    pe.wait_ge(*B.vacant(l, f"gs{h}"))
                    for tb in range(TB):
                        tk = slice(tb * P, (tb + 1) * P)
                        m = pe.matmul(B[f"gs{h}"][:, tk], kinv[:, h // 2, tk], gqp[:, h, tk], start=True, stop=True)
                    m.then_inc(*B.on_fill(f"gs{h}"))

                def gla_out(h):
                    name = f"go{h}"
                    pe.wait_ge(*B.vacant(l, name))
                    pe.wait_ge(*B.freed(l, f"gs{h}"))
                    if h == 0:
                        pe.wait_ge(*B.freed(l, "inc11"))
                    for tb in range(TB):
                        pe.matmul(B[name][:, tb * P:(tb + 1) * P], gvt[:, tb, h * GLA_DV:(h + 1) * GLA_DV],
                                  sct[:, h % 2, tb], start=True, stop=False)
                        for c in (2 * tb, 2 * tb + 1):
                            if c == 0:
                                continue
                            m = pe.matmul(B[name][:, c * CHUNK:(c + 1) * CHUNK], st[:, c, h // 2],
                                          gqp[:, h, c * CHUNK:(c + 1) * CHUNK], start=False,
                                          stop=(c % 2 == 1))
                    m.then_inc(*B.on_fill(name))

                gla_scores(0)
                gla_scores(1)
                for h in range(GLA_H):
                    gla_out(h)
                    if h + 2 < GLA_H:
                        gla_scores(h + 2)
                    if h >= 1:
                        stat(l, f"gst{h - 1}", ones[:], sq_of(f"gst{h - 1}"))
                stat(l, "gst3", ones[:], sq_of("gst3"))

                def attend(a):
                    base_i = 0 if a == "m" else H * TB

                    def logits(i):
                        h, qb = divmod(i, TB)
                        name = f"{a}lg{i}"
                        n = (qb + 1) * P
                        pe.wait_ge(*B.vacant(l, name))
                        if a == "m":
                            lhs, rhs = qT[0:QK, h, qb * P:(qb + 1) * P], kT[0:QK, h, 0:n]
                        else:
                            lhs, rhs = dqp[:, h, qb * P:(qb + 1) * P], dkn[:, h // 2, 0:n]
                        pe.matmul(B[name][:, 0:n], lhs, rhs, start=True, stop=True).then_inc(*B.on_fill(name))

                    def turn(i):
                        h, qb = divmod(i, TB)
                        name = f"{a}pt{i}"
                        pe.wait_ge(*B.vacant(l, name))
                        pe.wait_ge(*pn_ready.at(l, base_i + i))
                        for kb in range(qb + 1):
                            m = pe.transpose(B[name][:, kb * P:(kb + 1) * P],
                                             pb[:, i % 2, kb * P:(kb + 1) * P], ident)
                        m.then_inc(*B.on_fill(name))

                    def weigh(i):
                        h, qb = divmod(i, TB)
                        name = f"{a}o{h // 2}"
                        hp = h % 2
                        if i % (2 * TB) == 0:
                            pe.wait_ge(*B.vacant(l, name))
                        pe.wait_ge(*B.freed(l, f"{a}pt{i}"))
                        v = vm if a == "m" else dvt
                        for kb in range(qb + 1):
                            m = pe.matmul(B[name][hp * 64:(hp + 1) * 64, qb * P:(qb + 1) * P],
                                          v[:, kb, h * DH:(h + 1) * DH], ptb[:, i % 2, kb * P:(kb + 1) * P],
                                          start=(kb == 0), stop=(kb == qb))
                        m.then_inc(weighed.sem, 1)

                    logits(0)
                    for i in range(H * TB):
                        if i + 1 < H * TB:
                            logits(i + 1)
                        turn(i)
                        if i >= 1:
                            weigh(i - 1)
                        if i == 2 * TB + 2:
                            stat(l, f"{a}ost0", blk, sq_of(f"{a}ost0"))
                    weigh(H * TB - 1)
                    stat(l, f"{a}ost1", blk, sq_of(f"{a}ost1"))

                pe.wait_ge(*nrs_used.at(l, norm_index("mkst3")))
                pe.wait_ge(*B.freed(l, "mv1"))
                attend("m")
                pe.wait_ge(*nrs_used.at(l, norm_index("dkst1")))
                attend("d")

                mixed = [0, 1, 2, 3, 6, 7, 4, 5]

                def mix_part(k):
                    pe.wait_ge(*mix_ready.at(l, mixed.index(k)))

                for d in range(KB):
                    feature_unit(l, N_IN + d, f"out{d}", xgh, xgl, order=mixed,
                                 before=mix_part if d == 0 else None)

                def mlp_unit(s, waits, src_h, src_l, filled, before=None):
                    for w in waits:
                        pe.wait_ge(*w)
                    for k in range(KB):
                        if before is not None:
                            before(k)
                        pe.matmul(B.t[s][:], wl[:, s, n_block(k)], src_h[:, k], start=(k == 0), stop=False)
                        pe.matmul(B.t[s][:], wh[:, s, n_block(k)], src_h[:, k], start=False, stop=False)
                        m = pe.matmul(B.t[s][:], wh[:, s, n_block(k)], src_l[:, k], start=False, stop=(k == KB - 1))
                    m.then_inc(filled.sem, 1)

                pe.wait_ge(*xl_ready.at(l, 2 * KB - 1))
                total("mstat", 1)
                alone(pe)
                with pe.Fori(0, GROUPS) as g:
                    with pe.Fori(0, 4) as p:
                        for s in range(2):
                            mlp_unit(s, [(lo_ready.sem, l * N_UNIT + g * 16 + p * 2 + (N_IN + N_OUT + s + 3)),
                                         (up_freed[s].sem, l * 16 + g * 4 + p + 1),
                                         (dn_freed[s].sem, l * 16 + g * 4 + 1)],
                                     xmh, xml, up_filled[s])
                    pe.wait_ge(hl_ready.sem, l * 32 + g * 8 + 10)
                    alone(pe)
                    with pe.Fori(0, 4) as p:
                        for s in range(2):
                            mlp_unit(s, [(lo_ready.sem, l * N_UNIT + g * 16 + p * 2 + (N_IN + N_OUT + 8 + s + 3)),
                                         (up_freed[s].sem, l * 16 + g * 4 + 5),
                                         (dn_freed[s].sem, l * 16 + g * 4 + p + 1)],
                                     hh, hl, dn_filled[s])

        @block.scalar
        def _(act):
            act.dma_start(con[:], consts).then_inc(const_loaded, 16)
            act.wait_ge(const_loaded, 16)
            act.wait_ge(*ones_ready.at(0, 0))

            def split(s, loads):
                act.wait_ge(raw_loaded[s], 16 * loads)
                act.activation(wh[:, s], raw[:, s], ACT.Copy).then_inc(hi_ready.sem, 1)

            split(0, 1)
            split(1, 1)
            with act.Fori(0, DEPTH) as l:
                links = [0]

                def link(ins):
                    links[0] += 1
                    ins.then_inc(act_chain.sem, 1)
                    act.wait_ge(*act_chain.at(l, links[0] - 1))

                def next_unit(u):
                    act.wait_ge(*unit_done(l, u))
                    split(u % 2, l * (N_UNIT // 2) + ((u + AHEAD) // 2 + 1))

                def gained(k, e, dst, g):
                    act.activation(dst[:, k], x[:, k], ACT.Copy, scale=gain(g + k)).then_inc(xh_ready.sem, 1)
                    if e >= 2:
                        act.wait_ge(*sq_summed.at(l, e - 2))
                    act.activation(sqb[:, k % 2], x[:, k], ACT.Square).then_inc(sq_ready.sem, 1)

                def square(name, src, rows=slice(0, P), wait=None):
                    if wait is not None:
                        act.wait_ge(*wait)
                    act.activation(sqb[rows, norm_index(name) % 2], src, ACT.Square).then_inc(nsq_ready.sem, 1)

                def factor(name, n, rows=P):
                    i = norm_index(name)
                    act.wait_ge(*B.filled(l, name))
                    act.wait_ge(*nrs_ready.at(l, i - 1))
                    act.activation(lnb[0:rows], B[name][0:rows, :], ACT.Ln, scale=1.0 / n, bias=eps[0:rows])\
                        .then_inc(*B.on_read(name))
                    act.wait_ge(*B.freed(l, name))
                    act.wait_ge(*nrs_used.at(l, i - 2))
                    act.activation(rsb[0:rows, i % 2], lnb[0:rows], ACT.Exp, scale=-0.5).then_inc(nrs_ready.sem, 1)

                act.wait_ge(par_loaded, 16 * l + 16)
                for k in range(KB):
                    act.wait_ge(*x_ready.at(l, k - KB))
                    gained(k, k, xgh, G_ATTN)

                def tasks(u):
                    if u == 0:
                        act.wait_ge(*B.filled(l, "xstat"))
                        act.activation(rb[:], B["xstat"][:], ACT.Ln, scale=1.0 / D, bias=eps)\
                            .then_inc(*B.on_read("xstat"))
                        act.wait_ge(*B.freed(l, "xstat"))
                        act.activation(rb[:], rb[:], ACT.Exp, scale=-0.5).then_inc(rb_ready.sem, 1)
                    if u == 2:
                        act.wait_ge(*ik_ready.at(l, 0))
                        for j in (0, 1, 3):
                            act.activation(ikp[32 * j:32 * j + 32, j], ikp[64:96, 2], ACT.Copy)\
                                .then_inc(ik_ready.sem, 1)
                        act.wait_ge(*kr_ready.at(l, 0))
                        act.activation(cqn[64:QK, 1], kT[64:QK, 0], ACT.Square).then_inc(krsq_ready.sem, 1)
                    if u == 6:
                        act.wait_ge(*B.filled(l, "glr"))
                        act.activation(glrs[:], B["glr"][0:RANK, :], ACT.Copy).then_inc(*B.on_read("glr"))
                        for i, (qb, h) in enumerate(REL):
                            n = (qb + 1) * P
                            act.wait_ge(*B.filled(l, f"rel{i}"))
                            if i >= 2:
                                act.wait_ge(*rel_used.at(l, i - 2))
                            act.activation(sqb[:, i % 2, 0:n], B[f"rel{i}"][:, 0:n], ACT.Relu)\
                                .then_inc(*B.on_read(f"rel{i}"))
                    if u == 7:
                        for pr in range(2):
                            act.wait_ge(*B.filled(l, f"gz{pr}"))
                            bias = gain(G_BIAS + pr)
                            act.activation(tf[:, pr], B[f"gz{pr}"][:], ACT.Identity, bias=bias)
                            act.activation(e2[:, pr], B[f"gz{pr}"][:], ACT.Abs, bias=bias)\
                                .then_inc(*B.on_read(f"gz{pr}"))
                            act.wait_ge(*B.freed(l, f"gz{pr}"))
                            link(act.activation(e2[:, pr], e2[:, pr], ACT.Exp, scale=-1.0))
                            act.activation(e2[:, pr], e2[:, pr], ACT.Ln, bias=ones[:, 0:1])\
                                .then_inc(gate_ready.sem, 1)
                        act.wait_ge(*rel_used.at(l, 3 * IDX_H - 1))
                        act.wait_ge(*B.freed(l, "cq"))
                        act.activation(lnb[0:64], cqn[0:64, 1], ACT.Square)
                        square("cqst", cqn[:, 0])
                        square("ckvst", ckvn[:], wait=B.freed(l, "ckv"))
                    if u == 8:
                        for pr in range(2):
                            act.wait_ge(*decay_ready.at(l, pr))
                            act.activation(e1[:, pr], tf[:, pr], ACT.Exp, scale=1.0 / TAU)
                            act.activation(e2[:, pr], tf[:, pr], ACT.Exp, scale=-1.0 / TAU)\
                                .then_inc(exp_ready.sem, 1)
                        factor("cqst", Q_RANK)
                        factor("ckvst", KV_RANK)
                        square("dqst0", dqr[:, 0], wait=B.freed(l, "dq0"))
                    if u == 9:
                        square("mqst0", B["mq0"][0:QK, :], slice(0, QK), wait=B.filled(l, "mq0"))
                        factor("dqst0", DH)
                        square("dqst1", dqr[:, 1], wait=B.freed(l, "dq1"))
                    if u == 10:
                        factor("mqst0", QK, QK)
                        square("mqst1", B["mq1"][0:QK, :], slice(0, QK), wait=B.filled(l, "mq1"))
                        factor("dqst1", DH)
                        square("dkst0", dkn[:, 0], wait=B.freed(l, "dk0"))
                    if u == 11:
                        factor("mqst1", QK, QK)
                        square("mqst2", B["mq2"][0:QK, :], slice(0, QK), wait=B.filled(l, "mq2"))
                        factor("dkst0", DH)
                        square("dkst1", dkn[:, 1], wait=B.freed(l, "dk1"))
                    if u == 12:
                        factor("mqst2", QK, QK)
                        square("mqst3", B["mq3"][0:QK, :], slice(0, QK), wait=B.filled(l, "mq3"))
                        factor("dkst1", DH)
                    if u == 13:
                        factor("mqst3", QK, QK)
                        square("mkst0", B["mk0"][0:NOPE, :], slice(0, NOPE), wait=B.filled(l, "mk0"))
                    if 14 <= u <= 17:
                        if u < 17:
                            h = u - 13
                            square(f"mkst{h}", B[f"mk{h}"][0:NOPE, :], slice(0, NOPE), wait=B.filled(l, f"mk{h}"))
                        factor(f"mkst{u - 14}", QK, QK)
                    if u in (17, 18):
                        i = u - 17
                        act.wait_ge(*B.filled(l, f"mv{i}"))
                        act.activation(vm[:, 2 * i:2 * i + 2], B[f"mv{i}"][:].rearrange("p (t c) -> p t c", t=2), ACT.Copy)\
                            .then_inc(*B.on_read(f"mv{i}"))
                    if 16 <= u <= 19:
                        h = u - 16
                        act.wait_ge(*B.freed(l, f"gg{h}"))
                        if h == 0:
                            act.wait_ge(*nrs_used.at(l, norm_index("dqst1")))
                        if h >= 2:
                            act.wait_ge(*gg_ready.at(l, h - 2))
                        act.activation(pb[:, h % 2], gg[:, h], ACT.Exp, scale=-1.0).then_inc(gexp_ready.sem, 1)

                for u in range(N_IN):
                    next_unit(u)
                    tasks(u)

                def mix_high(j, k):
                    act.wait_ge(*mixf_ready.at(l, j))
                    act.activation(xgh[:, k], tf[:, j % 2], ACT.Copy).then_inc(mixh_ready.sem, 1)

                for h in range(GLA_H):
                    square(f"gst{h}", B[f"go{h}"][:], wait=B.filled(l, f"go{h}"))
                    if h >= 1:
                        factor(f"gst{h - 1}", GLA_DV)
                        mix_high(h - 1, h - 1)
                factor("gst3", GLA_DV)
                mix_high(3, 3)

                def attend(a):
                    base_i = 0 if a == "m" else H * TB
                    scale = (QK if a == "m" else DH) ** -0.5

                    def exponentials(i):
                        qb = i % TB
                        n = (qb + 1) * P
                        act.wait_ge(*lg_ready.at(l, base_i + i))
                        ai = 0 if a == "m" else 1
                        act.activation(pb[:, i % 2, 0:n], pb[:, i % 2, 0:n], ACT.Exp, scale=scale,
                                       bias=nb[:, ai, i:i + 1], accum_out=rsum[:, ai, i:i + 1])\
                            .then_inc(p_ready.sem, 1)

                    def turned(i):
                        n = (i % TB + 1) * P
                        act.wait_ge(*B.filled(l, f"{a}pt{i}"))
                        act.wait_ge(*weighed.at(l, base_i + i - 2))
                        act.activation(ptb[:, i % 2, 0:n], B[f"{a}pt{i}"][:, 0:n], ACT.Copy)\
                            .then_inc(*B.on_read(f"{a}pt{i}"))

                    def out_square(p):
                        square(f"{a}ost{p}", B[f"{a}o{p}"][:], wait=weighed.at(l, base_i + 8 * p + 7))

                    def out_mix(p):
                        factor(f"{a}ost{p}", DH)
                        mix_high((4 if a == "m" else 6) + p, (6 if a == "m" else 4) + p)

                    exponentials(0)
                    for i in range(H * TB):
                        if i + 1 < H * TB:
                            exponentials(i + 1)
                        turned(i)
                        if i == 8:
                            out_square(0)
                        if i == 11:
                            out_mix(0)
                    out_square(1)
                    out_mix(1)

                attend("m")
                attend("d")

                for d in range(KB):
                    next_unit(N_IN + d)
                    act.wait_ge(*B.freed(l, f"out{d}"))
                    gained(d, KB + d, xmh, G_MLP)

                with act.Fori(0, GROUPS) as g:
                    with act.Fori(0, 4) as p:
                        for s in range(2):
                            act.wait_ge(up_filled[s].sem, l * 16 + g * 4 + p + 1)
                            split(s, l * 48 + g * 8 + p + 18)
                            act.wait_ge(hl_ready.sem, l * 32 + g * 8 + p * 2 + (s + 1))
                            act.activation(tf[:, s], B.t[s][:], ACT.Relu).then_inc(up_freed[s].sem, 1)
                            act.wait_ge(up_freed[s].sem, l * 16 + g * 4 + p + 2)
                            act.activation(hh[:, p * 2 + s], tf[:, s], ACT.Square).then_inc(hh_ready.sem, 1)
                    with act.Fori(0, 4) as p:
                        for s in range(2):
                            act.wait_ge(dn_filled[s].sem, l * 16 + g * 4 + p + 1)
                            split(s, l * 48 + g * 8 + p + 22)

        @block.vector
        def _(vec):
            for sem in (lo_ready, xl_ready, nrs_ready, nrs_used, weighed, hl_ready, *up_freed, *dn_freed):
                vec.sem_inc(sem.sem, sem.start)
            for freed in B.free:
                vec.sem_inc(freed, 1)
            vec.wait_ge(const_loaded, 16)

            def low_part(s, hi_wait):
                vec.wait_ge(*hi_wait)
                vec.tensor_tensor(wl[:, s], raw[:, s], wh[:, s], ALU.subtract).then_inc(lo_ready.sem, 1)

            low_part(0, hi_ready.at(0, 0))
            low_part(1, hi_ready.at(0, 1))
            vec.wait_ge(x_loaded, 16)
            vec.sem_inc(x_ready.sem, 8)
            with vec.Fori(0, DEPTH) as l:
                links = [0]

                def link(ins):
                    links[0] += 1
                    ins.then_inc(vec_chain.sem, 1)
                    vec.wait_ge(*vec_chain.at(l, links[0] - 1))

                def after(ins, sem, value):
                    ins.then_inc(sem, 1)
                    vec.wait_ge(sem, value)

                def gained_low(k, e, dst_h, dst_l, g):
                    vec.wait_ge(*xh_ready.at(l, e))
                    vec.scalar_tensor_tensor(dst_l[:, k], x[:, k], gain(g + k), dst_h[:, k],
                                             ALU.mult, ALU.subtract).then_inc(xl_ready.sem, 1)

                def evacuate(name, dst, rows=slice(0, P), factor=None):
                    vec.wait_ge(*B.filled(l, name))
                    f = rb[rows] if factor is None else factor
                    vec.tensor_tensor(dst, B[name][rows, :], f, ALU.mult).then_inc(*B.on_read(name))

                def select_step(i):
                    qb = 3 - i % 3
                    top = m8[:, qb - 1]
                    alone(vec)
                    link(vec.max(top, scores_of(qb)))
                    alone(vec)
                    link(vec.match_replace(scores_of(qb), top, scores_of(qb), TAKEN))

                def use_factor(name):
                    vec.wait_ge(*nrs_ready.at(l, norm_index(name)))
                    return rsb[:, norm_index(name) % 2]

                vec.wait_ge(par_loaded, 16 * l + 16)
                for k in range(KB):
                    gained_low(k, k, xgh, xgl, G_ATTN)
                vec.wait_ge(*rb_ready.at(l, 0))

                def dsa_queries(pr):
                    f = use_factor(f"dqst{pr}")
                    if pr == 0:
                        vec.wait_ge(*zeroed.at(l, 1))
                    for hp in range(2):
                        r = slice(64 * hp, 64 * hp + 64)
                        op = vec.scalar_tensor_tensor(dqp[r, 2 * pr + hp], dqr[r, pr], gain(G_DQ, r.start, r.stop),
                                                      f[r], ALU.mult, ALU.mult)
                    op.then_inc(nrs_used.sem, 1)

                def dsa_keys(pr):
                    f = use_factor(f"dkst{pr}")
                    vec.scalar_tensor_tensor(dkn[:, pr], dkn[:, pr], gain(G_DK), f, ALU.mult, ALU.mult)\
                        .then_inc(nrs_used.sem, 1)

                def mla_gain(h):
                    if h == 0:
                        vec.wait_ge(*exp_ready.at(l, 1))
                    vec.wait_ge(*nsq_ready.at(l, norm_index(f"mqst{h}")))
                    vec.tensor_scalar(tf[0:QK, h % 2], B[f"mq{h}"][0:QK, :], gain(G_MQ, 0, QK), None, ALU.mult)\
                        .then_inc(*B.on_read(f"mq{h}"))
                    vec.wait_ge(*B.freed(l, f"mq{h}"))
                    vec.tensor_tensor(qT[64:QK, h], tf[64:QK, h % 2], cos, ALU.mult).then_inc(qg_ready.sem, 1)

                def mla_queries(h):
                    vec.wait_ge(*B.filled(l, f"mrot{h}"))
                    vec.wait_ge(*qg_ready.at(l, h))
                    after(vec.tensor_tensor(tf[64:QK, h % 2], B[f"mrot{h}"][64:QK, :], sin, ALU.mult),
                          B.on_read(f"mrot{h}")[0], B.freed(l, f"mrot{h}")[1])
                    link(vec.tensor_tensor(tf[64:QK, h % 2], tf[64:QK, h % 2], qT[64:QK, h], ALU.add))
                    f = use_factor(f"mqst{h}")
                    after(vec.tensor_tensor(qT[0:QK, h], tf[0:QK, h % 2], f[0:QK], ALU.mult),
                          nrs_used.sem, nrs_used.at(l, norm_index(f"mqst{h}"))[1])

                def mla_keys(h):
                    f = use_factor(f"mkst{h}")
                    vec.scalar_tensor_tensor(kT[0:NOPE, h], B[f"mk{h}"][0:NOPE, :], gain(G_MK, 0, NOPE), f[0:NOPE],
                                             ALU.mult, ALU.mult).then_inc(*B.on_read(f"mk{h}"))
                    vec.tensor_tensor(kT[64:QK, h], kT[64:QK, 3], f[64:QK], ALU.mult).then_inc(nrs_used.sem, 1)

                def silu(h):
                    vec.wait_ge(*gexp_ready.at(l, h))
                    link(vec.tensor_scalar(pb[:, h % 2], pb[:, h % 2], 1.0, None, ALU.add))
                    link(vec.reciprocal(pb[:, h % 2], pb[:, h % 2]))
                    vec.tensor_tensor(gg[:, h], gg[:, h], pb[:, h % 2], ALU.mult).then_inc(gg_ready.sem, 1)

                def tasks(u):
                    if u == 0:
                        evacuate("iq0", iqT[:, 0])
                    if u == 1:
                        evacuate("iq1", iqT[:, 1])
                    if u == 2:
                        vec.wait_ge(*B.filled(l, "small"))
                        link(vec.tensor_tensor(cqn[0:64, 1], B["small"][0:64, :], rb[0:64], ALU.mult))
                        vec.wait_ge(*zeroed.at(l, 0))
                        vec.tensor_tensor(ikp[64:96, 2], B["small"][64:96, :], rb[64:96], ALU.mult)\
                            .then_inc(ik_ready.sem, 1)
                        vec.tensor_tensor(kT[64:QK, 0], B["small"][96:P, :], rb[96:P], ALU.mult)\
                            .then_inc(*B.on_read("small"))
                        vec.wait_ge(*B.freed(l, "small"))
                        vec.tensor_scalar(kT[64:QK, 2], kT[64:QK, 0], gain(G_MK, 64, QK), None, ALU.mult)\
                            .then_inc(kr_ready.sem, 1)
                        vec.wait_ge(*kr_ready.at(l, 0))
                        vec.tensor_tensor(kT[64:QK, 3], kT[64:QK, 2], cos, ALU.mult).then_inc(krg_ready.sem, 1)
                        vec.wait_ge(*B.filled(l, "rcol"))
                        vec.tensor_copy(rcol[:].unsqueeze(2),
                                        B["rcol"][:].rearrange("p (t c) -> p t c", t=TB)[:, :, 0:1])\
                            .then_inc(*B.on_read("rcol"))
                        vec.wait_ge(*B.freed(l, "rcol"))
                    if u == 5:
                        for tb in range(TB):
                            vec.wait_ge(*B.filled(l, f"dv{tb}"))
                            vec.tensor_scalar(dvt[:, tb], B[f"dv{tb}"][:, 0:DVW], rcol[:, tb:tb + 1], None, ALU.mult)\
                                .then_inc(*B.on_read(f"dv{tb}"))
                        vec.wait_ge(*B.freed(l, "dv1"))
                        vec.wait_ge(*B.freed(l, "dv2"))
                        vec.wait_ge(*B.freed(l, "dv3"))
                        link(vec.tensor_scalar(iws[:], dvt[:, 1:4, H * DH:H * DH + IDX_H],
                                               float(IDX_H * IDX_D) ** -0.5, None, ALU.mult))
                    if u == 6:
                        evacuate("cq", cqn[:, 0])
                        for i, (qb, h) in enumerate(REL):
                            n = (qb + 1) * P
                            dst = scores_of(qb)
                            vec.wait_ge(*B.freed(l, f"rel{i}"))
                            after(vec.scalar_tensor_tensor(dst, sqb[:, i % 2, 0:n], iws[:, qb - 1, h:h + 1],
                                                           causal(qb) if h == 0 else dst, ALU.mult, ALU.add),
                                  rel_used.sem, rel_used.at(l, i)[1])
                    if u == 7:
                        evacuate("ckv", ckvn[:])
                        for pr in range(2):
                            vec.wait_ge(*gate_ready.at(l, pr))
                            link(vec.scalar_tensor_tensor(e1[:, pr], tf[:, pr], 0.0, e2[:, pr],
                                                          ALU.min, ALU.subtract))
                            vec.tensor_tensor_scan(tf[:, pr], con[:, C_SCAN:C_SCAN + T], e1[:, pr], 0.0,
                                                   ALU.mult, ALU.add).then_inc(decay_ready.sem, 1)
                    if u in (8, 9):
                        evacuate(f"dq{u - 8}", dqr[:, u - 8])
                    if u == 8:
                        f = use_factor("cqst")
                        vec.scalar_tensor_tensor(cqn[:, 0], cqn[:, 0], gain(G_QLAT), f, ALU.mult, ALU.mult)
                        vec.scalar_tensor_tensor(cqn[0:64, 1], cqn[0:64, 1], gain(G_QLAT + 1, 0, 64), f[0:64],
                                                 ALU.mult, ALU.mult).then_inc(nrs_used.sem, 1)
                        f = use_factor("ckvst")
                        vec.scalar_tensor_tensor(ckvn[:], ckvn[:], gain(G_KVLAT), f, ALU.mult, ALU.mult)\
                            .then_inc(nrs_used.sem, 1)
                    if u == 9:
                        mla_gain(0)
                        dsa_queries(0)
                    if u in (10, 11):
                        evacuate(f"dk{u - 10}", dkn[:, u - 10])
                    if u == 10:
                        mla_queries(0)
                        mla_gain(1)
                        dsa_queries(1)
                    if u == 11:
                        mla_queries(1)
                        mla_gain(2)
                        dsa_keys(0)
                    if u in (12, 13):
                        pr = u - 12
                        vec.wait_ge(*exp_ready.at(l, pr))
                        vec.wait_ge(*zeroed.at(l, 2))
                        link(vec.scalar_tensor_tensor(kinv[:, pr], rb[:], GLA_DK ** -0.5, e1[:, pr],
                                                      ALU.mult, ALU.mult))
                        vec.wait_ge(*B.filled(l, f"gq{pr}"))
                        vec.tensor_tensor(gqp[0:64, 2 * pr], B[f"gq{pr}"][0:64, :], kinv[0:64, pr], ALU.mult)
                        vec.tensor_tensor(gqp[64:P, 2 * pr + 1], B[f"gq{pr}"][64:P, :], kinv[64:P, pr], ALU.mult)\
                            .then_inc(*B.on_read(f"gq{pr}"))
                    if u == 12:
                        mla_queries(2)
                        mla_gain(3)
                        dsa_keys(1)
                    if u == 13:
                        mla_queries(3)
                        vec.wait_ge(*B.filled(l, "krot"))
                        vec.wait_ge(*krg_ready.at(l, 0))
                        after(vec.tensor_tensor(kT[64:QK, 0], B["krot"][64:QK, :], sin, ALU.mult),
                              B.on_read("krot")[0], B.freed(l, "krot")[1])
                        link(vec.tensor_tensor(kT[64:QK, 3], kT[64:QK, 3], kT[64:QK, 0], ALU.add))
                    if u in (14, 15):
                        pr = u - 14
                        link(vec.tensor_tensor(e2[:, pr], e2[:, pr], rb[:], ALU.mult))
                        vec.wait_ge(*B.filled(l, f"gk{pr}"))
                        vec.tensor_tensor(kinv[:, pr], B[f"gk{pr}"][:], e2[:, pr], ALU.mult)\
                            .then_inc(*B.on_read(f"gk{pr}"))
                        vec.wait_ge(*B.freed(l, f"gk{pr}"))
                        dec = e1[:, pr].rearrange("p (c t) -> p c t", t=CHUNK)[:, :, CHUNK - 1:CHUNK]
                        vec.tensor_tensor(tf[:, pr].rearrange("p (c t) -> p c t", t=CHUNK),
                                          kinv[:, pr].rearrange("p (c t) -> p c t", t=CHUNK),
                                          dec.to_broadcast([P, NCHUNK, CHUNK]), ALU.mult)\
                            .then_inc(kend_ready.sem, 1)
                    if 14 <= u <= 17:
                        mla_keys(u - 14)
                    if 16 <= u <= 19:
                        evacuate(f"gg{u - 16}", gg[:, u - 16])
                    if 17 <= u <= 20:
                        silu(u - 17)
                    if u == 18:
                        vec.wait_ge(*zeroed.at(l, 4))
                        for pr in range(2):
                            vec.wait_ge(*B.filled(l, f"ketr{pr}"))
                            src = B[f"ketr{pr}"][:].rearrange("p (t c) -> p t c", t=TB)
                            cols = slice(pr * P, (pr + 1) * P)
                            link(vec.tensor_copy(ke[0:64, 0, :, cols], src[0:64]))
                            vec.tensor_copy(ke[64:P, 1, :, cols], src[64:P]).then_inc(*B.on_read(f"ketr{pr}"))
                    if u == 23:
                        for tb in range(TB):
                            vec.wait_ge(*B.filled(l, f"gv{tb}"))
                            vec.tensor_scalar(gvt[:, tb], B[f"gv{tb}"][:], rcol[:, tb:tb + 1], None, ALU.mult)\
                                .then_inc(*B.on_read(f"gv{tb}"))

                steps = 3 * (TOPK // 8)
                per_slot = 3
                done = 0
                for u in range(N_IN):
                    low_part(u % 2, hi_ready.at(l, u + AHEAD))
                    tasks(u)
                    if u >= 7:
                        for i in range(done, min(done + per_slot, steps)):
                            select_step(i)
                        done = min(done + per_slot, steps)
                assert done == steps
                for qb in (1, 2, 3):
                    link(vec.tensor_scalar(scores_of(qb), scores_of(qb), TAKEN * 0.5, NEG, ALU.is_gt, ALU.mult))

                vec.wait_ge(*zeroed.at(l, 3))
                for pr in range(2):
                    for c in range(NCHUNK - 1):
                        name = f"inc{pr}{c // 4}"
                        inc = B[name][:, (c % 4) * P:(c % 4 + 1) * P]
                        if c % 4 == 0:
                            vec.wait_ge(*B.filled(l, name))
                        last = c % 4 == 3 or c == NCHUNK - 2
                        if c == 0:
                            op = vec.tensor_copy(st[:, 1, pr], inc)
                        else:
                            op = vec.scalar_tensor_tensor(st[:, c + 1, pr], st[:, c, pr],
                                                          e1[:, pr, c * CHUNK + CHUNK - 1:c * CHUNK + CHUNK], inc,
                                                          ALU.mult, ALU.add)
                        if last:
                            op.then_inc(*B.on_read(name))
                            vec.wait_ge(*B.freed(l, name))
                        else:
                            link(op)

                def masked_scores(h):
                    vec.wait_ge(*B.filled(l, f"gs{h}"))
                    if h >= 2:
                        vec.wait_ge(*B.filled(l, f"go{h - 2}"))
                    src = B[f"gs{h}"][:].rearrange("p (t c) -> p t c", t=TB)
                    for hp in range(2):
                        r = slice(64 * hp, 64 * hp + 64)
                        m = con[r, C_GM:C_GM + CHUNK].unsqueeze(1).to_broadcast([64, TB, CHUNK])
                        op = vec.tensor_tensor(sct[r, h % 2, :, r], src[r, :, r], m, ALU.mult)
                    op.then_inc(*B.on_read(f"gs{h}"))

                def mix(j, k, name, bank, freed, g, gate=None):
                    f = use_factor(name)
                    op = vec.scalar_tensor_tensor(tf[:, j % 2], B[bank][:], gain(g), f, ALU.mult, ALU.mult)
                    op.then_inc(*B.on_read(bank))
                    vec.wait_ge(*B.freed(l, bank))
                    if gate is None:
                        vec.sem_inc(mixf_ready.sem, 1)
                    else:
                        vec.tensor_tensor(tf[:, j % 2], tf[:, j % 2], gg[:, gate], ALU.mult)\
                            .then_inc(mixf_ready.sem, 1)
                    vec.sem_inc(nrs_used.sem, 1)
                    vec.wait_ge(*mixh_ready.at(l, j))
                    vec.tensor_tensor(xgl[:, k], tf[:, j % 2], xgh[:, k], ALU.subtract).then_inc(mix_ready.sem, 1)

                masked_scores(0)
                masked_scores(1)
                for h in range(GLA_H):
                    if h + 2 < GLA_H:
                        masked_scores(h + 2)
                    mix(h, h, f"gst{h}", f"go{h}", None, G_GLA + h, gate=h)

                def attend(a):
                    ai = 0 if a == "m" else 1
                    base_i = ai * H * TB
                    scale = (QK if a == "m" else DH) ** -0.5

                    def mask_max(i):
                        qb = i % TB
                        n = (qb + 1) * P
                        mask = scores_of(qb) if a == "d" and qb >= 1 else causal(qb)
                        vec.wait_ge(*B.filled(l, f"{a}lg{i}"))
                        if i >= 2:
                            vec.wait_ge(*B.filled(l, f"{a}pt{i - 2}"))
                        alone(vec)
                        vec.tensor_tensor_reduce(pb[:, i % 2, 0:n], B[f"{a}lg{i}"][:, 0:n], mask, 1.0, -3.4e38,
                                                 ALU.add, ALU.max, mx[:, ai, i:i + 1]).then_inc(*B.on_read(f"{a}lg{i}"))
                        vec.wait_ge(*B.freed(l, f"{a}lg{i}"))
                        vec.tensor_scalar(nb[:, ai, i:i + 1], mx[:, ai, i:i + 1], -scale, None, ALU.mult)\
                            .then_inc(lg_ready.sem, 1)

                    def normalise(i):
                        n = (i % TB + 1) * P
                        vec.wait_ge(*p_ready.at(l, base_i + i))
                        link(vec.reciprocal(rinv[:, ai, i:i + 1], rsum[:, ai, i:i + 1]))
                        vec.tensor_scalar(pb[:, i % 2, 0:n], pb[:, i % 2, 0:n], rinv[:, ai, i:i + 1], None, ALU.mult)\
                            .then_inc(pn_ready.sem, 1)

                    def out_mix(p):
                        mix((4 if a == "m" else 6) + p, (6 if a == "m" else 4) + p, f"{a}ost{p}", f"{a}o{p}",
                            None, (G_MLA if a == "m" else G_DSA) + p)

                    mask_max(0)
                    for i in range(H * TB):
                        if i + 1 < H * TB:
                            mask_max(i + 1)
                        normalise(i)
                        if i == 11:
                            out_mix(0)
                    out_mix(1)

                attend("m")
                attend("d")

                for d in range(KB):
                    low_part(d % 2, hi_ready.at(l, N_IN + d + AHEAD))
                    vec.wait_ge(*B.filled(l, f"out{d}"))
                    vec.tensor_tensor(x[:, d], x[:, d], B[f"out{d}"][:], ALU.add).then_inc(*B.on_read(f"out{d}"))
                    gained_low(d, KB + d, xmh, xml, G_MLP)
                vec.wait_ge(*B.filled(l, "mstat"))
                vec.tensor_scalar(rb[:], B["mstat"][:], 1.0 / D, EPS, ALU.mult, ALU.add).then_inc(*B.on_read("mstat"))
                vec.wait_ge(*B.freed(l, "mstat"))
                vec.reciprocal(rb[:], rb[:]).then_inc(rb_ready.sem, 1)
                vec.wait_ge(*rb_ready.at(l, 1))
                alone(vec)

                with vec.Fori(0, GROUPS) as g:
                    with vec.Fori(0, 4) as p:
                        for s in range(2):
                            low_part(s, (hi_ready.sem, l * N_UNIT + g * 16 + p * 2 + (N_IN + N_OUT + AHEAD + 1 + s)))
                            vec.wait_ge(hh_ready.sem, l * 32 + g * 8 + p * 2 + (s + 1))
                            vec.tensor_tensor(sqb[:, s], tf[:, s], tf[:, s], ALU.mult).then_inc(hid_ready.sem, 1)
                            vec.wait_ge(hid_ready.sem, l * 32 + g * 8 + p * 2 + (s + 1))
                            vec.tensor_tensor(hl[:, p * 2 + s], sqb[:, s], hh[:, p * 2 + s], ALU.subtract)\
                                .then_inc(hl_ready.sem, 1)
                    with vec.Fori(0, 4) as p:
                        for s in range(2):
                            low_part(s, (hi_ready.sem, l * N_UNIT + g * 16 + p * 2 + (N_IN + N_OUT + 8 + AHEAD + 1 + s)))
                            vec.wait_ge(dn_filled[s].sem, l * 16 + g * 4 + p + 1)
                            vec.wait_ge(x_ready.sem, l * 32 + g * 8 + p * 2 + (7 + s))
                            vec.tensor_tensor(rsb[:, s], B.t[s][:], rb[:], ALU.mult).then_inc(dn_freed[s].sem, 1)
                assert links[0] <= VEC_LINKS
                vec.sem_inc(vec_chain.sem, VEC_LINKS - links[0])


def weight_stream(w_in, w_out, w_up, w_down):
    cols = {"iq": IQ, "dq": DQ, "dk": DK, "gq": GQ, "gk": GK, "gg": GG}

    def blocks(w, rows, columns):
        part = w[rows[0]:rows[1]][:, columns]
        return part.reshape(-1, P, part.shape[1]).transpose(1, 0, 2).reshape(P, -1)

    stream = np.zeros((DEPTH * N_UNIT + AHEAD, P, 1024), w_in.dtype)
    for l in range(DEPTH):
        n = l * N_UNIT
        token = 0
        for u, name in enumerate(UNITS):
            rows = (0, D)
            if name == "small":
                c = np.r_[CQ + P:CQ + Q_RANK, IK:IK + IDX_D, KR:KR + ROPE]
            elif name == "cq":
                c = np.r_[CQ:CQ + P]
            elif name == "ckv":
                c = np.r_[CKV:CKV + KV_RANK]
            elif name == "dv":
                a, b = DV_BLOCKS[u - 3]
                rows, c = (a * P, b * P), np.r_[DV:DV + H * DH, IW:IW + IDX_H, GLR:GLR + RANK]
            elif name == "gv":
                rows, c = (2 * (u - 20) * P, 2 * (u - 19) * P), np.r_[GV:GV + GLA_H * GLA_DV]
            else:
                c0 = cols[name[:2]] + P * int(name[2:])
                c = np.r_[c0:c0 + P]
            part = blocks(w_in[l], rows, c)
            stream[n + u, :, :part.shape[1]] = part
        n += N_IN
        for d in range(KB):
            stream[n + d] = blocks(w_out[l], (0, D), np.r_[d * P:(d + 1) * P])
        n += N_OUT
        for g in range(GROUPS):
            for j in range(8):
                c0 = (g * 8 + j) * P
                stream[n + g * 16 + j] = blocks(w_up[l], (0, D), np.r_[c0:c0 + P])
                stream[n + g * 16 + 8 + j] = blocks(w_down[l], (g * 1024, (g + 1) * 1024), np.r_[j * P:(j + 1) * P])
    return stream


def parameter_blocks(a):
    par = np.zeros((DEPTH, P, N_PAR), a["attn_norm"].dtype)
    for l in range(DEPTH):
        q = par[l]
        q[:, G_ATTN:G_ATTN + 8] = a["attn_norm"][l].reshape(KB, P).T
        q[:, G_MLP:G_MLP + 8] = a["mlp_norm"][l].reshape(KB, P).T
        q[:, G_BIAS:G_BIAS + 2] = a["gla_gate_bias"][l].reshape(2, P).T
        q[:, G_GLA:G_GLA + 4] = a["gla_out_norm"][l].T
        q[:, G_DQ] = np.concatenate([a["dsa_q_norm"][l]] * 2)
        q[:, G_DK] = np.concatenate([a["dsa_k_norm"][l]] * 2)
        q[:, G_DSA:G_DSA + 2] = a["dsa_out_norm"][l].reshape(2, P).T
        q[:, G_QLAT] = a["mla_q_latent_norm"][l][:P]
        q[0:64, G_QLAT + 1] = a["mla_q_latent_norm"][l][P:]
        q[:, G_KVLAT] = a["mla_kv_latent_norm"][l]
        q[0:QK, G_MQ] = a["mla_q_norm"][l]
        q[0:QK, G_MK] = a["mla_k_norm"][l]
        q[:, G_MLA:G_MLA + 2] = a["mla_out_norm"][l].reshape(2, P).T
        q[0:RANK, W_GATE:W_GATE + 256] = a["gla_gate_up"][l]
        q[:, W_UQ:W_UQ + H * QK] = a["mla_w_uq"][l][:P]
        q[0:64, W_UQ + H * QK:W_UKV] = a["mla_w_uq"][l][P:]
        q[:, W_UKV:] = a["mla_w_ukv"][l]
    return par


def constant_block():
    c = np.zeros((P, N_CONST), np.float32)
    i = np.arange(P)
    c[:, C_ID:C_ID + P] = np.eye(P)
    c[:, C_BLK:C_BLK + P] = (i[:, None] // 64) == (i[None, :] // 64)
    for j in range(ROPE // 2):
        c[64 + ROPE // 2 + j, C_ROT + j] = -1.0
        c[64 + j, C_ROT + ROPE // 2 + j] = 1.0
    c[:, C_EPS] = EPS
    c[:, C_GM:C_GM + CHUNK] = (i[:, None] % CHUNK) <= np.arange(CHUNK)[None, :]
    c[:, C_CAUSAL + T - P:C_CAUSAL + T] = np.where(i[None, :] <= i[:, None], 0.0, NEG)
    c[:, C_SCAN:C_SCAN + T] = (np.arange(T) % CHUNK) != 0
    half = ROPE // 2
    freq = np.float32(10000.0) ** (-np.arange(half, dtype=np.float32) / np.float32(half))
    ang = (np.arange(T, dtype=np.float32)[None, :] * freq[:, None]).astype(np.float32)
    for r in range(2):
        c[64 + half * r:64 + half * (r + 1), C_COS:C_COS + T] = np.cos(ang)
        c[64 + half * r:64 + half * (r + 1), C_SIN:C_SIN + T] = np.sin(ang)
    return c


def kernel(**inputs):
    import concourse.bacc as bacc
    from concourse.bass_utils import run_bass_kernel_spmd

    a = {k: np.asarray(v) for k, v in inputs.items()}
    arrays = {
        "in_x": np.ascontiguousarray(a["x"][0].T.reshape(KB, P, T).transpose(1, 0, 2)),
        "in_stream": weight_stream(a["w_in"], a["w_out"], a["w_up"], a["w_down"]),
        "in_params": parameter_blocks(a),
        "in_consts": constant_block(),
    }
    nc = bacc.Bacc("TRN2", target_bir_lowering=False, num_devices=1)
    args = [nc.dram_tensor(n, v.shape, F32, kind="ExternalInput").ap() for n, v in arrays.items()]
    out = nc.dram_tensor("out_y", (P, KB, T), F32, kind="ExternalOutput").ap()
    build_trunk(nc, *args, out)
    r = run_bass_kernel_spmd(nc, [arrays], core_ids=[0])
    y = r.results[0]["out_y"]
    return np.ascontiguousarray(y.transpose(2, 1, 0).reshape(1, T, D))
```

```python
from contextlib import ExitStack

import numpy as np

import concourse.bass as bass
from concourse import mybir

F32 = mybir.dt.float32
F32R = mybir.dt.float32r
ALU = mybir.AluOpType
ACT = mybir.ActivationFunctionType

P = 128
T = 512
D = 1024
KB = D // P
TB = T // P
DEPTH = 2
D_FF = 4096
EPS = 1e-6
NEG = -1e30
TAKEN = -3e38
GLA_H, GLA_DK, GLA_DV, RANK, TAU, CHUNK = 4, 64, 128, 16, 16.0, 64
H, DH = 4, 64
IDX_H, IDX_D = 8, 32
MIXED = [0, 1, 2, 3, 6, 7, 4, 5]
TOPK = min(256, T // 4)
SEL_AT = {1: 0, 2: 2 * P, 3: 5 * P, 4: 9 * P}
Q_RANK, KV_RANK, NOPE, ROPE = 192, 128, 64, 32
QK = NOPE + ROPE
NCHUNK = T // CHUNK

_WIDTHS = [256, 256, 512, 512, RANK, 256, 256, 256, IDX_H * IDX_D, IDX_D, IDX_H, Q_RANK, KV_RANK, ROPE]
_C = np.concatenate([[0], np.cumsum(_WIDTHS)]).tolist()
GQ, GK, GV, GG, GLR, DQ, DK, DV, IQ, IK, IW, CQ, CKV, KR, D_IN = _C

UNITS = ["iq0", "iq1", "small", "dv", "dv", "dv", "cq", "ckv", "dq0", "dq1", "dk0", "dk1",
         "gq0", "gq1", "gk0", "gk1", "gg0", "gg1", "gg2", "gg3", "gv", "gv", "gv", "gv"]
N_IN = len(UNITS)
N_OUT = KB
GROUPS = D_FF // (8 * P)
N_MLP = GROUPS * 16
N_UNIT = N_IN + N_OUT + N_MLP
AHEAD = 2
DVW = H * DH + IDX_H + RANK
DV_BLOCKS = [(0, 3), (3, 6), (6, 8)]

G_ATTN, G_MLP, G_BIAS, G_GLA, G_DQ, G_DK, G_DSA, G_QLAT, G_KVLAT, G_MQ, G_MK, G_MLA = (
    0, 8, 16, 18, 22, 23, 24, 26, 28, 29, 30, 31)
W_GATE = 33
W_UQ = W_GATE + 256
W_UKV = W_UQ + 2 * H * QK
N_PAR = W_UKV + H * (NOPE + DH)

C_ID = 0
C_BLK = C_ID + P
C_ROT = C_BLK + P
C_EPS = C_ROT + ROPE
C_GM = C_EPS + 1
C_CAUSAL = C_GM + CHUNK
C_SCAN = C_CAUSAL + T
C_COS = C_SCAN + T
C_SIN = C_COS + T
N_CONST = C_SIN + T


class Sem:

    def __init__(self, ctx, nc, name, per, start=0):
        self.sem = ctx.enter_context(nc.semaphore(name))
        self.per, self.start = per, start

    def at(self, layer, k):
        return self.sem, layer * self.per + (self.start + k + 1)


N_ATT = 2 * H * TB
LEAD, LAG, PLANES = 3, 2, 4
PAIR = 2 * TB

USES = (
    [("iq0", 0), ("xstat", 6), ("iq1", 1), ("rcol", 7), ("small", 0),
     ("dv0", 4), ("dv1", 5), ("dv2", 6), ("dv3", 7), ("cq", 1), ("glr", 6)]
    + [(f"rel{i}", 2 + i % 2) for i in range(3 * IDX_H)]
    + [("ckv", 0), ("gz0", 4), ("gz1", 5), ("dq0", 1), ("cqst", 6), ("ckvst", 7)]
    + [("dq1", 0), ("dqst0", 2), ("mq0", 4), ("dk0", 1), ("mqst0", 6), ("mrot0", 7)]
    + [("dqst1", 3), ("mq1", 5), ("dk1", 0), ("mqst1", 6), ("mrot1", 7), ("dkst0", 2), ("mq2", 4)]
    + [("gq0", 1), ("mqst2", 6), ("mrot2", 7), ("dkst1", 3), ("mq3", 5)]
    + [("gq1", 0), ("mqst3", 6), ("mrot3", 7), ("krot", 2), ("mk0", 4)]
    + [("gk0", 1), ("mkst0", 6), ("mk1", 5), ("gk1", 0), ("mkst1", 7), ("mk2", 4)]
    + [("gg0", 1), ("mkst2", 6), ("mk3", 5), ("gg1", 0), ("mkst3", 7), ("mv0", 4)]
    + [("gg2", 1), ("mv1", 5), ("ketr0", 2), ("ketr1", 3), ("gg3", 0)]
    + [("gv0", 4), ("gv1", 5), ("gv2", 6), ("gv3", 7)]
    + [("inc00", 4), ("inc01", 5), ("inc10", 6), ("inc11", 7)]
    + [(f"gs{h}", 2 + h % 2) for h in range(GLA_H)]
    + [(f"go{h}", h % 2) for h in range(GLA_H)] + [(f"gst{h}", 6 + h % 2) for h in range(GLA_H)]
    + [(f"lg{j}", (2, 3, 6)[j % 3]) for j in range(N_ATT)]
    + [(f"pt{j}", 4 + j % 2) for j in range(N_ATT)]
    + [(f"ao{b}", b % 2) for b in range(2 * H // 2)]
    + [(f"aost{b}", 7) for b in range(2 * H // 2)]
    + [(f"out{d}", d % 2) for d in range(KB)] + [("mstat", 6)]
)
NO_FILL = ("ao0", "ao1", "ao2", "ao3")


class Banks:

    def __init__(self, ctx, nc):
        self.place, self.per, self.fills = {}, [0] * 8, [0] * 8
        for name, b in USES:
            self.place[name] = (b, self.per[b], self.fills[b])
            self.per[b] += 1
            self.fills[b] += name not in NO_FILL
        self.t = [ctx.enter_context(nc.psum_tensor(f"bank{b}", [P, T], F32)) for b in range(8)]
        self.fill = [ctx.enter_context(nc.semaphore(f"bank{b}_filled")) for b in range(8)]
        self.free = [ctx.enter_context(nc.semaphore(f"bank{b}_freed")) for b in range(8)]

    def __getitem__(self, name):
        return self.t[self.place[name][0]]

    def filled(self, l, name):
        b, _, k = self.place[name]
        return self.fill[b], l * self.fills[b] + (k + 1)

    def vacant(self, l, name):
        b, k, _ = self.place[name]
        return self.free[b], l * self.per[b] + (k + 1)

    def freed(self, l, name):
        b, k, _ = self.place[name]
        return self.free[b], l * self.per[b] + (k + 2)

    def on_fill(self, name):
        return self.fill[self.place[name][0]], 1

    def on_read(self, name):
        return self.free[self.place[name][0]], 1


NORMS = (["cqst", "ckvst", "dqst0", "mqst0", "dqst1", "mqst1", "dkst0", "mqst2", "dkst1", "mqst3"]
         + [f"mkst{h}" for h in range(H)] + [f"gst{h}" for h in range(GLA_H)]
         + [f"aost{b}" for b in range(4)])
N_NORM = len(NORMS)

VEC_LINKS = 400
ACT_LINKS = 2


def build_trunk(nc, x_in, stream, params, consts, out):
    with ExitStack() as ctx:
        base = nc.sbuf_base if isinstance(nc.sbuf_base, int) else nc.sbuf_base()
        slab = ctx.enter_context(nc.sbuf_tensor("slab", [P, 207 * 256], F32))
        del slab
        base = (base + 31) // 32 * 32
        cursor = [base]

        def place(name, shape, dt=F32, at=None):
            words = int(np.prod(shape[1:]))
            off = cursor[0] if at is None else at
            if at is None:
                cursor[0] += (4 * words + 31) // 32 * 32
                assert cursor[0] <= base + 207 * 1024, (name, cursor[0] - base)
            t = nc.alloc_sbuf_tensor_at(name, list(shape), dt, offset=off)
            return t, off

        x, _ = place("x", [P, KB, T])
        xgh, _ = place("xgh", [P, KB, T], F32R)
        xgl, _ = place("xgl", [P, KB, T], F32R)
        raw, _ = place("raw", [P, 2, 1024])
        wh, _ = place("wh", [P, 2, 1024], F32R)
        wl, _ = place("wl", [P, 2, 1024], F32R)
        gqp, g0 = place("gqp", [P, GLA_H, T])
        kinv, _ = place("kinv", [P, 2, T])
        ke, ke0 = place("ke", [P, 2, TB, 256])
        gvt, _ = place("gvt", [P, TB, GLA_H * GLA_DV])
        e1, _ = place("e1", [P, 2, T])
        hh, _ = place("hh", [P, 8, T], F32R, at=g0)
        hl, _ = place("hl", [P, 8, T], F32R, at=g0 + 16384)
        pba, _ = place("pba", [P, PLANES, T], at=g0)
        ptba, _ = place("ptba", [P, PLANES, T], at=ke0)
        cqn, _ = place("cqn", [P, 2, T], at=ke0)
        ckvn, _ = place("ckvn", [P, T], at=ke0 + 4096)
        qT, m0 = place("qT", [P, H, T])
        kT, _ = place("kT", [P, H, T])
        dqp, _ = place("dqp", [P, H, T])
        dkn, _ = place("dkn", [P, 2, T])
        vm, _ = place("vm", [P, TB, H * DH])
        xmh, _ = place("xmh", [P, KB, T], F32R, at=m0)
        xml, _ = place("xml", [P, KB, T], F32R, at=m0 + 16384)
        iqT, a0 = place("iqT", [P, 2, T])
        ikp, _ = place("ikp", [P, 4, T])
        st, _ = place("st", [P, NCHUNK, 2, GLA_DV], at=a0)
        sct, _ = place("sct", [P, 2, TB, P], at=a0 + 8192)
        gg, _ = place("gg", [P, GLA_H, T])
        sel, _ = place("sel", [P, SEL_AT[4]])
        dvt, _ = place("dvt", [P, TB, DVW])
        pb, pb0 = place("pb", [P, 2, T])
        ptb, pt0 = place("ptb", [P, 2, T])
        e2, _ = place("e2", [P, 2, T], at=pt0)
        dqr, _ = place("dqr", [P, 2, T], at=pb0)
        sqb, _ = place("sqb", [P, 2, T])
        lnb, _ = place("lnb", [P, T])
        rsb, _ = place("rsb", [P, 2, T])
        tf, _ = place("tf", [P, 2, T])
        rb, _ = place("rb", [P, T])
        glrs, _ = place("glrs", [RANK, T], at=pb0 + 2048)
        con, _ = place("con", [P, N_CONST])
        par, _ = place("par", [P, N_PAR])
        ones, _ = place("ones", [P, P])
        rcol, _ = place("rcol", [P, TB])
        iws, _ = place("iws", [P, 3, IDX_H])
        m8, _ = place("m8", [P, 3, 8])
        mx, _ = place("mx", [P, N_ATT])
        nb, _ = place("nb", [P, N_ATT])
        rsum, _ = place("rsum", [P, N_ATT])
        rinv, _ = place("rinv", [P, N_ATT])

        ident = con[:, C_ID:C_ID + P]
        cos = con[64:QK, C_COS:C_COS + T]
        sin = con[64:QK, C_SIN:C_SIN + T]
        blk = con[:, C_BLK:C_BLK + P]
        eps = con[:, C_EPS:C_EPS + 1]

        def causal(qb):
            return con[:, C_CAUSAL + (TB - 1 - qb) * P:C_CAUSAL + T]

        def gain(c, lo=0, hi=P):
            return par[lo:hi, c:c + 1]

        B = Banks(ctx, nc)

        def S(name, per=1, start=0):
            return Sem(ctx, nc, name, per, start)

        x_loaded = ctx.enter_context(nc.semaphore("x_loaded"))
        const_loaded = ctx.enter_context(nc.semaphore("const_loaded"))
        par_loaded = ctx.enter_context(nc.semaphore("par_loaded"))
        raw_loaded = [ctx.enter_context(nc.semaphore(f"raw_loaded{i}")) for i in range(2)]
        out_stored = ctx.enter_context(nc.semaphore("out_stored"))
        hi_ready = S("hi_ready", N_UNIT)
        lo_ready = S("lo_ready", N_UNIT, start=2)
        token_spent = S("token_spent", 5)
        x_ready = S("x_ready", 8 * GROUPS, start=8)
        xh_ready = S("xh_ready", 2 * KB)
        xl_ready = S("xl_ready", 2 * KB, start=1)
        sq_ready = S("sq_ready", 2 * KB)
        sq_summed = S("sq_summed", 2 * KB)
        rb_ready = S("rb_ready", 2)
        ones_ready = S("ones_ready", 0)
        zeroed = S("zeroed", 5)
        ik_ready = S("ik_ready", 4)
        kr_ready = S("kr_ready")
        rel_used = S("rel_used", 3 * IDX_H)
        gate_ready = S("gate_ready", 2)
        decay_ready = S("decay_ready", 2)
        exp_ready = S("exp_ready", 2)
        nsq_ready = S("nsq_ready", N_NORM)
        nrs_ready = S("nrs_ready", N_NORM, start=1)
        nrs_used = S("nrs_used", N_NORM, start=2)
        krsq_ready = S("krsq_ready")
        krg_ready = S("krg_ready")
        qg_ready = S("qg_ready", H)
        kend_ready = S("kend_ready", 2)
        gexp_ready = S("gexp_ready", GLA_H)
        gg_ready = S("gg_ready", GLA_H)
        lg_ready = S("lg_ready", 2 * H * TB)
        p_ready = S("p_ready", 2 * H * TB)
        pn_ready = S("pn_ready", 2 * H * TB)
        weighed = S("weighed", 2 * H * TB, start=2)
        mixf_ready = S("mixf_ready", KB)
        mixh_ready = S("mixh_ready", KB)
        mix_ready = S("mix_ready", KB)
        up_filled = [S(f"up_filled{b}", GROUPS * 4) for b in range(2)]
        up_freed = [S(f"up_freed{b}", GROUPS * 4, start=1) for b in range(2)]
        dn_filled = [S(f"down_filled{b}", GROUPS * 4) for b in range(2)]
        dn_freed = [S(f"down_freed{b}", GROUPS * 4, start=1) for b in range(2)]
        hh_ready = S("hh_ready", GROUPS * 8)
        hid_ready = S("hid_ready", GROUPS * 8)
        hl_ready = S("hl_ready", GROUPS * 8, start=2)
        vec_chain = S("vec_chain", VEC_LINKS)
        act_chain = S("act_chain", ACT_LINKS)

        block = ctx.enter_context(nc.Block())

        def unit_done(l, u):
            if u >= N_IN:
                return B.filled(l, f"out{u - N_IN}")
            if UNITS[u] == "dv":
                return B.filled(l, "dv3") if u == 5 else token_spent.at(l, u - 3)
            if UNITS[u] == "gv":
                return B.filled(l, "gv3") if u == 23 else token_spent.at(l, u - 20 + 2)
            return B.filled(l, UNITS[u])


        passed = ctx.enter_context(nc.semaphore("passed"))

        def alone(eng):
            eng.sem_inc(passed, 1)

        def norm_index(name):
            return NORMS.index(name)

        REL = [(qb, h) for qb in (3, 2, 1) for h in range(IDX_H)]

        def scores_of(qb):
            return sel[:, SEL_AT[qb]:SEL_AT[qb + 1]]

        @block.sync
        def _(sp):
            sp.dma_start(x[:], x_in).then_inc(x_loaded, 16)
            with sp.Fori(0, (DEPTH * N_UNIT + AHEAD) // 2) as i:
                for s in range(2):
                    sp.wait_ge(lo_ready.sem, 2 * i + (s + 1))
                    sp.dma_start(raw[:, s], stream[2 * i + s]).then_inc(raw_loaded[s], 16)
            for d in range(KB):
                sp.wait_ge(*x_ready.at(DEPTH, d - KB))
                sp.dma_start(out[:, d], x[:, d]).then_inc(out_stored, 16)
            sp.wait_ge(out_stored, 16 * KB)

        @block.gpsimd
        def _(pool):
            pool.memset(ones[:], 1.0).then_inc(ones_ready.sem, 1)

            def sum_squares(l, half):
                for k in range(KB):
                    e = half * KB + k
                    pool.wait_ge(*sq_ready.at(l, e))
                    if k == 0:
                        alone(pool)
                        op = pool.tensor_copy(lnb[:], sqb[:, k % 2])
                    else:
                        pool.wait_ge(*sq_summed.at(l, e - 1))
                        op = pool.tensor_tensor(lnb[:], lnb[:], sqb[:, k % 2], ALU.add)
                    op.then_inc(sq_summed.sem, 1)

            with pool.Fori(0, DEPTH) as l:
                pool.wait_ge(*xl_ready.at(l, -1))
                pool.dma_start(par[:], params[l]).then_inc(par_loaded, 16)
                sum_squares(l, 0)
                pool.wait_ge(*x_ready.at(l, -1))
                alone(pool)
                pool.memset(ikp[:], 0.0).then_inc(zeroed.sem, 1)
                pool.memset(dqp[:], 0.0).then_inc(zeroed.sem, 1)
                pool.memset(gqp[:], 0.0).then_inc(zeroed.sem, 1)
                pool.wait_ge(*B.filled(l, "rel23"))
                alone(pool)
                pool.memset(sct[:], 0.0).then_inc(zeroed.sem, 1)
                pool.wait_ge(*B.filled(l, "mv1"))
                alone(pool)
                pool.memset(ke[:], 0.0).then_inc(zeroed.sem, 1)
                sum_squares(l, 1)
                with pool.Fori(0, GROUPS) as g:
                    for d in range(KB):
                        pool.wait_ge(dn_freed[d % 2].sem, l * 16 + g * 4 + (d // 2 + 2))
                        pool.tensor_tensor(x[:, d], x[:, d], rsb[:, d % 2], ALU.add).then_inc(x_ready.sem, 1)

        @block.tensor
        def _(pe):
            def weights_ready(l, u):
                pe.wait_ge(*lo_ready.at(l, u))

            def n_block(k):
                return slice(k * P, (k + 1) * P)

            def feature_unit(l, u, name, act_h, act_l, order=range(KB), before=None):
                s = u % 2
                weights_ready(l, u)
                pe.wait_ge(*B.vacant(l, name))
                bank = B[name]
                order = list(order)
                for n, k in enumerate(order):
                    if before is not None:
                        before(k)
                    wk_h, wk_l = wh[:, s, n_block(k)], wl[:, s, n_block(k)]
                    last = n == len(order) - 1
                    pe.matmul(bank[:], wk_l, act_h[:, k], start=(n == 0), stop=False)
                    pe.matmul(bank[:], wk_h, act_h[:, k], start=False, stop=False)
                    m = pe.matmul(bank[:], wk_h, act_l[:, k], start=False, stop=last)
                m.then_inc(*B.on_fill(name))

            def token_units(l, u0, blocks, width, stem):
                for i, (ka, kb) in enumerate(blocks):
                    u = u0 + i
                    s = u % 2
                    weights_ready(l, u)
                    for tb in range(TB):
                        bank = B[f"{stem}{tb}"]
                        if i == 0:
                            pe.wait_ge(*B.vacant(l, f"{stem}{tb}"))
                        for k in range(ka, kb):
                            c = (k - ka) * width
                            r_h, r_l = wh[:, s, c:c + width], wl[:, s, c:c + width]
                            a_h = xgh[:, k, tb * P:(tb + 1) * P]
                            a_l = xgl[:, k, tb * P:(tb + 1) * P]
                            last = k == KB - 1
                            pe.matmul(bank[:, 0:width], a_l, r_h, start=(k == 0), stop=False)
                            pe.matmul(bank[:, 0:width], a_h, r_h, start=False, stop=False)
                            m = pe.matmul(bank[:, 0:width], a_h, r_l, start=False, stop=last)
                        if i == len(blocks) - 1 and tb < TB - 1:
                            m.then_inc(*B.on_fill(f"{stem}{tb}"))
                    if i == len(blocks) - 1:
                        m.then_inc(*B.on_fill(f"{stem}{TB - 1}"))
                    else:
                        m.then_inc(token_spent.sem, 1)

            def stat(l, name, lhsT, rhs, rows=P):
                pe.wait_ge(*nsq_ready.at(l, norm_index(name)))
                pe.wait_ge(*B.vacant(l, name))
                pe.matmul(B[name][0:rows, :], lhsT, rhs, start=True, stop=True).then_inc(*B.on_fill(name))

            def sq_of(name):
                return sqb[:, norm_index(name) % 2]

            pe.wait_ge(const_loaded, 16)
            pe.wait_ge(*ones_ready.at(0, 0))
            with pe.Fori(0, DEPTH) as l:
                def x_part(k):
                    pe.wait_ge(*xl_ready.at(l, k))

                def unit(u, before=None):
                    feature_unit(l, u, UNITS[u], xgh, xgl, before=before)

                def total(name, half):
                    pe.wait_ge(*sq_summed.at(l, half * KB + KB - 1))
                    pe.wait_ge(*B.vacant(l, name))
                    pe.matmul(B[name][:], ones[:], lnb[:], start=True, stop=True).then_inc(*B.on_fill(name))

                def mla_q(h):
                    name = f"mq{h}"
                    pe.wait_ge(*nrs_used.at(l, 0))
                    pe.wait_ge(*B.vacant(l, name))
                    c = W_UQ + h * QK
                    pe.matmul(B[name][0:QK], par[:, c:c + QK], cqn[:, 0], start=True, stop=False)
                    c += H * QK
                    pe.matmul(B[name][0:QK], par[0:64, c:c + QK], cqn[0:64, 1], start=False, stop=True)\
                        .then_inc(*B.on_fill(name))

                def mla_q_rest(h):
                    stat(l, f"mqst{h}", ones[0:QK, 0:QK], sq_of(f"mqst{h}")[0:QK], QK)
                    pe.wait_ge(*qg_ready.at(l, h))
                    pe.wait_ge(*B.vacant(l, f"mrot{h}"))
                    alone(pe)
                    pe.matmul(B[f"mrot{h}"][64:QK], con[64:QK, C_ROT:C_ROT + ROPE], tf[64:QK, h % 2],
                              start=True, stop=True).then_inc(*B.on_fill(f"mrot{h}"))

                def mla_k(h):
                    name = f"mk{h}"
                    pe.wait_ge(*nrs_used.at(l, 1))
                    pe.wait_ge(*B.vacant(l, name))
                    c = W_UKV + h * (NOPE + DH)
                    pe.matmul(B[name][0:NOPE], par[:, c:c + NOPE], ckvn[:], start=True, stop=True)\
                        .then_inc(*B.on_fill(name))

                def mla_k_stat(h):
                    name = f"mkst{h}"
                    pe.wait_ge(*nsq_ready.at(l, norm_index(name)))
                    pe.wait_ge(*krsq_ready.at(l, 0))
                    pe.wait_ge(*B.vacant(l, name))
                    pe.matmul(B[name][0:QK], ones[0:NOPE, 0:QK], sq_of(name)[0:NOPE], start=True, stop=False)
                    pe.matmul(B[name][0:QK], ones[64:QK, 0:QK], cqn[64:QK, 1], start=False, stop=True)\
                        .then_inc(*B.on_fill(name))

                def mla_v(i):
                    name = f"mv{i}"
                    pe.wait_ge(*B.vacant(l, name))
                    vcols = par[:, W_UKV:N_PAR].rearrange("p (h c) -> p h c", h=H)[:, :, NOPE:NOPE + DH]
                    for j in range(2):
                        tb = 2 * i + j
                        m = pe.matmul(B[name][:, j * 256:(j + 1) * 256], ckvn[:, tb * P:(tb + 1) * P], vcols,
                                      start=True, stop=True)
                    m.then_inc(*B.on_fill(name))

                unit(0, before=x_part)
                total("xstat", 0)
                unit(1)
                pe.wait_ge(*rb_ready.at(l, 0))
                pe.wait_ge(*B.vacant(l, "rcol"))
                for tb in range(TB):
                    m = pe.transpose(B["rcol"][:, tb * P:(tb + 1) * P], rb[:, tb * P:(tb + 1) * P], ident)
                m.then_inc(*B.on_fill("rcol"))
                unit(2)
                token_units(l, 3, DV_BLOCKS, DVW, "dv")
                unit(6)
                pe.wait_ge(*B.freed(l, "dv3"))
                pe.wait_ge(*B.vacant(l, "glr"))
                for tb in range(TB):
                    m = pe.transpose(B["glr"][0:RANK, tb * P:(tb + 1) * P],
                                     dvt[:, tb, DVW - RANK:DVW], ident)
                m.then_inc(*B.on_fill("glr"))
                pe.wait_ge(*B.freed(l, "iq1"))
                pe.wait_ge(*ik_ready.at(l, 3))
                for i, (qb, h) in enumerate(REL):
                    pe.wait_ge(*B.vacant(l, f"rel{i}"))
                    n = (qb + 1) * P
                    pe.matmul(B[f"rel{i}"][:, 0:n], iqT[:, h // 4, qb * P:(qb + 1) * P], ikp[:, h % 4, 0:n],
                              start=True, stop=True).then_inc(*B.on_fill(f"rel{i}"))
                unit(7)
                pe.wait_ge(*B.freed(l, "glr"))
                for pr in range(2):
                    pe.wait_ge(*B.vacant(l, f"gz{pr}"))
                    pe.matmul(B[f"gz{pr}"][:], par[0:RANK, W_GATE + pr * P:W_GATE + (pr + 1) * P], glrs[:],
                              start=True, stop=True).then_inc(*B.on_fill(f"gz{pr}"))
                unit(8)
                pe.wait_ge(*nsq_ready.at(l, 0))
                pe.wait_ge(*B.vacant(l, "cqst"))
                pe.matmul(B["cqst"][:], ones[:], sqb[:, 0], start=True, stop=False)
                pe.matmul(B["cqst"][:], ones[0:64, :], lnb[0:64], start=False, stop=True)\
                    .then_inc(*B.on_fill("cqst"))
                stat(l, "ckvst", ones[:], sq_of("ckvst"))
                unit(9)
                stat(l, "dqst0", blk, sq_of("dqst0"))
                mla_q(0)
                unit(10)
                mla_q_rest(0)
                stat(l, "dqst1", blk, sq_of("dqst1"))
                mla_q(1)
                unit(11)
                mla_q_rest(1)
                stat(l, "dkst0", blk, sq_of("dkst0"))
                mla_q(2)
                unit(12)
                mla_q_rest(2)
                stat(l, "dkst1", blk, sq_of("dkst1"))
                mla_q(3)
                unit(13)
                mla_q_rest(3)
                pe.wait_ge(*krg_ready.at(l, 0))
                pe.wait_ge(*B.vacant(l, "krot"))
                alone(pe)
                pe.matmul(B["krot"][64:QK], con[64:QK, C_ROT:C_ROT + ROPE], kT[64:QK, 2],
                          start=True, stop=True).then_inc(*B.on_fill("krot"))
                mla_k(0)
                unit(14)
                mla_k_stat(0)
                mla_k(1)
                unit(15)
                mla_k_stat(1)
                mla_k(2)
                unit(16)
                mla_k_stat(2)
                mla_k(3)
                unit(17)
                mla_k_stat(3)
                mla_v(0)
                unit(18)
                mla_v(1)
                for pr in range(2):
                    pe.wait_ge(*kend_ready.at(l, pr))
                    pe.wait_ge(*B.vacant(l, f"ketr{pr}"))
                    for tb in range(TB):
                        m = pe.transpose(B[f"ketr{pr}"][:, tb * P:(tb + 1) * P],
                                         tf[:, pr, tb * P:(tb + 1) * P], ident)
                    m.then_inc(*B.on_fill(f"ketr{pr}"))
                unit(19)
                token_units(l, 20, [(0, 2), (2, 4), (4, 6), (6, 8)], GLA_H * GLA_DV, "gv")

                for tb in range(TB):
                    pe.wait_ge(*B.freed(l, f"gv{tb}"))
                pe.wait_ge(*B.freed(l, "ketr1"))
                for pr in range(2):
                    for half in range(2):
                        name = f"inc{pr}{half}"
                        pe.wait_ge(*B.vacant(l, name))
                        for c in range(4 * half, min(4 * half + 4, NCHUNK - 1)):
                            for hp in range(2):
                                h = 2 * pr + hp
                                m = pe.matmul(B[name][hp * 64:(hp + 1) * 64, (c % 4) * P:(c % 4 + 1) * P],
                                              ke[:, c % 2, c // 2, h * GLA_DK:(h + 1) * GLA_DK],
                                              gvt[:, c // 2, h * GLA_DV:(h + 1) * GLA_DV], start=True, stop=True)
                        m.then_inc(*B.on_fill(name))
                pe.wait_ge(*B.freed(l, "gq1"))
                pe.wait_ge(*B.freed(l, "gk1"))

                def gla_scores(h):
                    pe.wait_ge(*B.vacant(l, f"gs{h}"))
                    for tb in range(TB):
                        tk = slice(tb * P, (tb + 1) * P)
                        m = pe.matmul(B[f"gs{h}"][:, tk], kinv[:, h // 2, tk], gqp[:, h, tk], start=True, stop=True)
                    m.then_inc(*B.on_fill(f"gs{h}"))

                def gla_out(h):
                    name = f"go{h}"
                    pe.wait_ge(*B.vacant(l, name))
                    pe.wait_ge(*B.freed(l, f"gs{h}"))
                    if h == 0:
                        pe.wait_ge(*B.freed(l, "inc11"))
                    for tb in range(TB):
                        pe.matmul(B[name][:, tb * P:(tb + 1) * P], gvt[:, tb, h * GLA_DV:(h + 1) * GLA_DV],
                                  sct[:, h % 2, tb], start=True, stop=False)
                        for c in (2 * tb, 2 * tb + 1):
                            if c == 0:
                                continue
                            m = pe.matmul(B[name][:, c * CHUNK:(c + 1) * CHUNK], st[:, c, h // 2],
                                          gqp[:, h, c * CHUNK:(c + 1) * CHUNK], start=False,
                                          stop=(c % 2 == 1))
                    m.then_inc(*B.on_fill(name))

                gla_scores(0)
                gla_scores(1)
                for h in range(GLA_H):
                    gla_out(h)
                    if h + 2 < GLA_H:
                        gla_scores(h + 2)
                    if h >= 1:
                        stat(l, f"gst{h - 1}", ones[:], sq_of(f"gst{h - 1}"))
                stat(l, "gst3", ones[:], sq_of("gst3"))

                def logits(j):
                    i = j % (H * TB)
                    h, qb = divmod(i, TB)
                    name = f"lg{j}"
                    n = (qb + 1) * P
                    pe.wait_ge(*B.vacant(l, name))
                    if j < H * TB:
                        lhs, rhs = qT[0:QK, h, qb * P:(qb + 1) * P], kT[0:QK, h, 0:n]
                    else:
                        lhs, rhs = dqp[:, h, qb * P:(qb + 1) * P], dkn[:, h // 2, 0:n]
                    pe.matmul(B[name][:, 0:n], lhs, rhs, start=True, stop=True).then_inc(*B.on_fill(name))

                def turn(j):
                    name = f"pt{j}"
                    pe.wait_ge(*B.vacant(l, name))
                    pe.wait_ge(*pn_ready.at(l, j))
                    for kb in range(j % TB + 1):
                        m = pe.transpose(B[name][:, kb * P:(kb + 1) * P],
                                         pba[:, j % PLANES, kb * P:(kb + 1) * P], ident)
                    m.then_inc(*B.on_fill(name))

                def weigh(j):
                    h, qb = divmod(j % (H * TB), TB)
                    name = f"ao{j // PAIR}"
                    hp = h % 2
                    if j % PAIR == 0:
                        pe.wait_ge(*B.vacant(l, name))
                    pe.wait_ge(*B.freed(l, f"pt{j}"))
                    v = vm if j < H * TB else dvt
                    for kb in range(qb + 1):
                        m = pe.matmul(B[name][hp * 64:(hp + 1) * 64, qb * P:(qb + 1) * P],
                                      v[:, kb, h * DH:(h + 1) * DH], ptba[:, j % PLANES, kb * P:(kb + 1) * P],
                                      start=(kb == 0), stop=(kb == qb))
                    m.then_inc(weighed.sem, 1)

                pe.wait_ge(*nrs_used.at(l, norm_index("mkst3")))
                pe.wait_ge(*B.freed(l, "mv1"))
                for j in range(LEAD):
                    logits(j)
                for j in range(N_ATT + LAG):
                    if j + LEAD < N_ATT:
                        logits(j + LEAD)
                    if j < N_ATT:
                        turn(j)
                    if j >= LAG:
                        weigh(j - LAG)
                    if j % PAIR == LAG + 1 and j > PAIR:
                        b = j // PAIR - 1
                        stat(l, f"aost{b}", blk, sq_of(f"aost{b}"))
                stat(l, "aost3", blk, sq_of("aost3"))

                def mix_part(k):
                    pe.wait_ge(*mix_ready.at(l, MIXED.index(k)))

                for d in range(KB):
                    feature_unit(l, N_IN + d, f"out{d}", xgh, xgl, order=MIXED,
                                 before=mix_part if d == 0 else None)

                def mlp_unit(s, waits, src_h, src_l, filled, before=None):
                    for w in waits:
                        pe.wait_ge(*w)
                    for k in range(KB):
                        if before is not None:
                            before(k)
                        pe.matmul(B.t[s][:], wl[:, s, n_block(k)], src_h[:, k], start=(k == 0), stop=False)
                        pe.matmul(B.t[s][:], wh[:, s, n_block(k)], src_h[:, k], start=False, stop=False)
                        m = pe.matmul(B.t[s][:], wh[:, s, n_block(k)], src_l[:, k], start=False, stop=(k == KB - 1))
                    m.then_inc(filled.sem, 1)

                def up_group(g, before=None):
                    with pe.Fori(0, 4) as p:
                        for s in range(2):
                            mlp_unit(s, [(lo_ready.sem, l * N_UNIT + g * 16 + p * 2 + (N_IN + N_OUT + s + 3)),
                                         (up_freed[s].sem, l * 16 + g * 4 + p + 1),
                                         (dn_freed[s].sem, l * 16 + g * 4 + 1)],
                                     xmh, xml, up_filled[s], before if s == 0 else None)

                def down_group(g):
                    def hidden_part(k):
                        if k == 0:
                            pe.wait_ge(hl_ready.sem, l * 32 + g * 8 + (KB - 2 + 2))
                        if k >= KB - 2:
                            pe.wait_ge(hl_ready.sem, l * 32 + g * 8 + (k + 3))

                    with pe.Fori(0, 4) as p:
                        for s in range(2):
                            mlp_unit(s, [(lo_ready.sem, l * N_UNIT + g * 16 + p * 2 + (N_IN + N_OUT + 8 + s + 3)),
                                         (up_freed[s].sem, l * 16 + g * 4 + 5),
                                         (dn_freed[s].sem, l * 16 + g * 4 + p + 1)],
                                     hh, hl, dn_filled[s], hidden_part if s == 0 else None)

                def gained_part(k):
                    if k == 0:
                        pe.wait_ge(*xl_ready.at(l, 2 * KB - 3))
                    if k >= KB - 2:
                        pe.wait_ge(*xl_ready.at(l, KB + k))

                pe.wait_ge(*B.freed(l, "out6"))
                alone(pe)
                up_group(0, gained_part)
                total("mstat", 1)
                alone(pe)
                down_group(0)
                with pe.Fori(1, GROUPS) as g:
                    up_group(g)
                    down_group(g)

        @block.scalar
        def _(act):
            act.dma_start(con[:], consts).then_inc(const_loaded, 16)
            act.wait_ge(const_loaded, 16)
            act.wait_ge(*ones_ready.at(0, 0))

            def split(s, loads):
                act.wait_ge(raw_loaded[s], 16 * loads)
                act.activation(wh[:, s], raw[:, s], ACT.Copy).then_inc(hi_ready.sem, 1)

            act.preload_act_table_set("natural_log_exp_and_others")
            split(0, 1)
            split(1, 1)
            with act.Fori(0, DEPTH) as l:
                links = [0]

                def link(ins):
                    links[0] += 1
                    ins.then_inc(act_chain.sem, 1)
                    act.wait_ge(*act_chain.at(l, links[0] - 1))

                def next_unit(u):
                    act.wait_ge(*unit_done(l, u))
                    split(u % 2, l * (N_UNIT // 2) + ((u + AHEAD) // 2 + 1))

                def gained(k, e, dst, g):
                    act.activation(dst[:, k], x[:, k], ACT.Copy, scale=gain(g + k)).then_inc(xh_ready.sem, 1)
                    if e >= 2:
                        act.wait_ge(*sq_summed.at(l, e - 2))
                    act.activation(sqb[:, k % 2], x[:, k], ACT.Square).then_inc(sq_ready.sem, 1)

                def square(name, src, rows=slice(0, P), wait=None):
                    if wait is not None:
                        act.wait_ge(*wait)
                    act.activation(sqb[rows, norm_index(name) % 2], src, ACT.Square).then_inc(nsq_ready.sem, 1)

                def factor(name, n, rows=P):
                    i = norm_index(name)
                    act.wait_ge(*B.filled(l, name))
                    act.wait_ge(*nrs_ready.at(l, i - 1))
                    act.activation(lnb[0:rows], B[name][0:rows, :], ACT.Ln, scale=1.0 / n, bias=eps[0:rows])\
                        .then_inc(*B.on_read(name))
                    act.wait_ge(*B.freed(l, name))
                    act.wait_ge(*nrs_used.at(l, i - 2))
                    act.activation(rsb[0:rows, i % 2], lnb[0:rows], ACT.Exp, scale=-0.5).then_inc(nrs_ready.sem, 1)

                act.wait_ge(par_loaded, 16 * l + 16)
                for k in range(KB):
                    act.wait_ge(*x_ready.at(l, k - KB))
                    gained(k, k, xgh, G_ATTN)

                def tasks(u):
                    if u == 0:
                        act.wait_ge(*B.filled(l, "xstat"))
                        act.activation(rb[:], B["xstat"][:], ACT.Ln, scale=1.0 / D, bias=eps)\
                            .then_inc(*B.on_read("xstat"))
                        act.wait_ge(*B.freed(l, "xstat"))
                        act.activation(rb[:], rb[:], ACT.Exp, scale=-0.5).then_inc(rb_ready.sem, 1)
                    if u == 2:
                        act.wait_ge(*ik_ready.at(l, 0))
                        for j in (0, 1, 3):
                            act.activation(ikp[32 * j:32 * j + 32, j], ikp[64:96, 2], ACT.Copy)\
                                .then_inc(ik_ready.sem, 1)
                        act.wait_ge(*kr_ready.at(l, 0))
                        act.activation(cqn[64:QK, 1], kT[64:QK, 0], ACT.Square).then_inc(krsq_ready.sem, 1)
                    if u == 6:
                        act.wait_ge(*B.filled(l, "glr"))
                        act.activation(glrs[:], B["glr"][0:RANK, :], ACT.Copy).then_inc(*B.on_read("glr"))
                        for i, (qb, h) in enumerate(REL):
                            n = (qb + 1) * P
                            act.wait_ge(*B.filled(l, f"rel{i}"))
                            if i >= 2:
                                act.wait_ge(*rel_used.at(l, i - 2))
                            act.activation(sqb[:, i % 2, 0:n], B[f"rel{i}"][:, 0:n], ACT.Relu)\
                                .then_inc(*B.on_read(f"rel{i}"))
                    if u == 7:
                        for pr in range(2):
                            act.wait_ge(*B.filled(l, f"gz{pr}"))
                            bias = gain(G_BIAS + pr)
                            act.activation(tf[:, pr], B[f"gz{pr}"][:], ACT.Identity, bias=bias)
                            act.activation(e2[:, pr], B[f"gz{pr}"][:], ACT.Abs, bias=bias)\
                                .then_inc(*B.on_read(f"gz{pr}"))
                            act.wait_ge(*B.freed(l, f"gz{pr}"))
                            link(act.activation(e2[:, pr], e2[:, pr], ACT.Exp, scale=-1.0))
                            act.activation(e2[:, pr], e2[:, pr], ACT.Ln, bias=ones[:, 0:1])\
                                .then_inc(gate_ready.sem, 1)
                        act.wait_ge(*rel_used.at(l, 3 * IDX_H - 1))
                        act.wait_ge(*B.freed(l, "cq"))
                        act.activation(lnb[0:64], cqn[0:64, 1], ACT.Square)
                        square("cqst", cqn[:, 0])
                        square("ckvst", ckvn[:], wait=B.freed(l, "ckv"))
                    if u == 8:
                        for pr in range(2):
                            act.wait_ge(*decay_ready.at(l, pr))
                            act.activation(e1[:, pr], tf[:, pr], ACT.Exp, scale=1.0 / TAU)
                            act.activation(e2[:, pr], tf[:, pr], ACT.Exp, scale=-1.0 / TAU)\
                                .then_inc(exp_ready.sem, 1)
                        factor("cqst", Q_RANK)
                        factor("ckvst", KV_RANK)
                        square("dqst0", dqr[:, 0], wait=B.freed(l, "dq0"))
                    if u == 9:
                        square("mqst0", B["mq0"][0:QK, :], slice(0, QK), wait=B.filled(l, "mq0"))
                        factor("dqst0", DH)
                        square("dqst1", dqr[:, 1], wait=B.freed(l, "dq1"))
                    if u == 10:
                        factor("mqst0", QK, QK)
                        square("mqst1", B["mq1"][0:QK, :], slice(0, QK), wait=B.filled(l, "mq1"))
                        factor("dqst1", DH)
                        square("dkst0", dkn[:, 0], wait=B.freed(l, "dk0"))
                    if u == 11:
                        factor("mqst1", QK, QK)
                        square("mqst2", B["mq2"][0:QK, :], slice(0, QK), wait=B.filled(l, "mq2"))
                        factor("dkst0", DH)
                        square("dkst1", dkn[:, 1], wait=B.freed(l, "dk1"))
                    if u == 12:
                        factor("mqst2", QK, QK)
                        square("mqst3", B["mq3"][0:QK, :], slice(0, QK), wait=B.filled(l, "mq3"))
                        factor("dkst1", DH)
                    if u == 13:
                        factor("mqst3", QK, QK)
                        square("mkst0", B["mk0"][0:NOPE, :], slice(0, NOPE), wait=B.filled(l, "mk0"))
                    if 14 <= u <= 17:
                        if u < 17:
                            h = u - 13
                            square(f"mkst{h}", B[f"mk{h}"][0:NOPE, :], slice(0, NOPE), wait=B.filled(l, f"mk{h}"))
                        factor(f"mkst{u - 14}", QK, QK)
                    if u in (17, 18):
                        i = u - 17
                        act.wait_ge(*B.filled(l, f"mv{i}"))
                        act.activation(vm[:, 2 * i:2 * i + 2], B[f"mv{i}"][:].rearrange("p (t c) -> p t c", t=2), ACT.Copy)\
                            .then_inc(*B.on_read(f"mv{i}"))
                    if 16 <= u <= 19:
                        h = u - 16
                        act.wait_ge(*B.freed(l, f"gg{h}"))
                        if h == 0:
                            act.wait_ge(*nrs_used.at(l, norm_index("dqst1")))
                        if h >= 2:
                            act.wait_ge(*gg_ready.at(l, h - 2))
                        act.activation(pb[:, h % 2], gg[:, h], ACT.Exp, scale=-1.0).then_inc(gexp_ready.sem, 1)

                for u in range(N_IN):
                    next_unit(u)
                    tasks(u)

                def mix_high(j, k):
                    act.wait_ge(*mixf_ready.at(l, j))
                    act.activation(xgh[:, k], tf[:, j % 2], ACT.Copy).then_inc(mixh_ready.sem, 1)

                for h in range(GLA_H):
                    square(f"gst{h}", B[f"go{h}"][:], wait=B.filled(l, f"go{h}"))
                    if h >= 1:
                        factor(f"gst{h - 1}", GLA_DV)
                        mix_high(h - 1, h - 1)
                factor("gst3", GLA_DV)
                mix_high(3, 3)

                def exponentials(j):
                    n = (j % TB + 1) * P
                    scale = (QK if j < H * TB else DH) ** -0.5
                    act.wait_ge(*lg_ready.at(l, j))
                    act.activation(pba[:, j % PLANES, 0:n], pba[:, j % PLANES, 0:n], ACT.Exp, scale=scale,
                                   bias=nb[:, j:j + 1], accum_out=rsum[:, j:j + 1]).then_inc(p_ready.sem, 1)

                def turned(j):
                    n = (j % TB + 1) * P
                    act.wait_ge(*B.filled(l, f"pt{j}"))
                    if j >= PLANES:
                        act.wait_ge(*weighed.at(l, j - PLANES))
                    act.activation(ptba[:, j % PLANES, 0:n], B[f"pt{j}"][:, 0:n], ACT.Copy)\
                        .then_inc(*B.on_read(f"pt{j}"))

                def out_square(b):
                    square(f"aost{b}", B[f"ao{b}"][:], wait=weighed.at(l, PAIR * (b + 1) - 1))

                def out_mix(b):
                    factor(f"aost{b}", DH)
                    mix_high(4 + b, MIXED[4 + b])

                for j in range(LEAD - 1):
                    exponentials(j)
                for j in range(N_ATT):
                    if j + LEAD - 1 < N_ATT:
                        exponentials(j + LEAD - 1)
                    turned(j)
                    if j % PAIR == LAG and j > PAIR:
                        out_square(j // PAIR - 1)
                    if j % PAIR == LAG + 2 and j > PAIR:
                        out_mix(j // PAIR - 1)
                out_square(3)
                out_mix(3)

                for d in range(KB):
                    next_unit(N_IN + d)
                    act.wait_ge(*B.freed(l, f"out{d}"))
                    gained(d, KB + d, xmh, G_MLP)

                with act.Fori(0, GROUPS) as g:
                    with act.Fori(0, 4) as p:
                        for s in range(2):
                            act.wait_ge(up_filled[s].sem, l * 16 + g * 4 + p + 1)
                            act.wait_ge(hl_ready.sem, l * 32 + g * 8 + p * 2 + (s + 1))
                            act.activation(tf[:, s], B.t[s][:], ACT.Relu).then_inc(up_freed[s].sem, 1)
                            act.wait_ge(up_freed[s].sem, l * 16 + g * 4 + p + 2)
                            act.activation(hh[:, p * 2 + s], tf[:, s], ACT.Square).then_inc(hh_ready.sem, 1)
                            split(s, l * 48 + g * 8 + p + 18)
                    with act.Fori(0, 4) as p:
                        for s in range(2):
                            act.wait_ge(dn_filled[s].sem, l * 16 + g * 4 + p + 1)
                            split(s, l * 48 + g * 8 + p + 22)

        @block.vector
        def _(vec):
            for sem in (lo_ready, xl_ready, nrs_ready, nrs_used, weighed, hl_ready, *up_freed, *dn_freed):
                vec.sem_inc(sem.sem, sem.start)
            for freed in B.free:
                vec.sem_inc(freed, 1)
            vec.wait_ge(const_loaded, 16)

            def low_part(s, hi_wait):
                vec.wait_ge(*hi_wait)
                vec.tensor_tensor(wl[:, s], raw[:, s], wh[:, s], ALU.subtract).then_inc(lo_ready.sem, 1)

            low_part(0, hi_ready.at(0, 0))
            low_part(1, hi_ready.at(0, 1))
            vec.wait_ge(x_loaded, 16)
            vec.sem_inc(x_ready.sem, 8)
            with vec.Fori(0, DEPTH) as l:
                links = [0]

                def link(ins):
                    links[0] += 1
                    ins.then_inc(vec_chain.sem, 1)
                    vec.wait_ge(*vec_chain.at(l, links[0] - 1))

                def after(ins, sem, value):
                    ins.then_inc(sem, 1)
                    vec.wait_ge(sem, value)

                def gained_low(k, e, dst_h, dst_l, g):
                    vec.wait_ge(*xh_ready.at(l, e))
                    vec.scalar_tensor_tensor(dst_l[:, k], x[:, k], gain(g + k), dst_h[:, k],
                                             ALU.mult, ALU.subtract).then_inc(xl_ready.sem, 1)

                def evacuate(name, dst, rows=slice(0, P), factor=None):
                    vec.wait_ge(*B.filled(l, name))
                    f = rb[rows] if factor is None else factor
                    vec.tensor_tensor(dst, B[name][rows, :], f, ALU.mult).then_inc(*B.on_read(name))

                def select_step(i):
                    qb = 3 - i % 3
                    top = m8[:, qb - 1]
                    alone(vec)
                    link(vec.max(top, scores_of(qb)))
                    alone(vec)
                    link(vec.match_replace(scores_of(qb), top, scores_of(qb), TAKEN))

                def use_factor(name):
                    vec.wait_ge(*nrs_ready.at(l, norm_index(name)))
                    return rsb[:, norm_index(name) % 2]

                vec.wait_ge(par_loaded, 16 * l + 16)
                for k in range(KB):
                    gained_low(k, k, xgh, xgl, G_ATTN)
                vec.wait_ge(*rb_ready.at(l, 0))

                def dsa_queries(pr):
                    f = use_factor(f"dqst{pr}")
                    if pr == 0:
                        vec.wait_ge(*zeroed.at(l, 1))
                    for hp in range(2):
                        r = slice(64 * hp, 64 * hp + 64)
                        op = vec.scalar_tensor_tensor(dqp[r, 2 * pr + hp], dqr[r, pr], gain(G_DQ, r.start, r.stop),
                                                      f[r], ALU.mult, ALU.mult)
                    op.then_inc(nrs_used.sem, 1)

                def dsa_keys(pr):
                    f = use_factor(f"dkst{pr}")
                    vec.scalar_tensor_tensor(dkn[:, pr], dkn[:, pr], gain(G_DK), f, ALU.mult, ALU.mult)\
                        .then_inc(nrs_used.sem, 1)

                def mla_gain(h):
                    if h == 0:
                        vec.wait_ge(*exp_ready.at(l, 1))
                    vec.wait_ge(*nsq_ready.at(l, norm_index(f"mqst{h}")))
                    vec.tensor_scalar(tf[0:QK, h % 2], B[f"mq{h}"][0:QK, :], gain(G_MQ, 0, QK), None, ALU.mult)\
                        .then_inc(*B.on_read(f"mq{h}"))
                    vec.wait_ge(*B.freed(l, f"mq{h}"))
                    vec.tensor_tensor(qT[64:QK, h], tf[64:QK, h % 2], cos, ALU.mult).then_inc(qg_ready.sem, 1)

                def mla_queries(h):
                    vec.wait_ge(*B.filled(l, f"mrot{h}"))
                    vec.wait_ge(*qg_ready.at(l, h))
                    after(vec.tensor_tensor(tf[64:QK, h % 2], B[f"mrot{h}"][64:QK, :], sin, ALU.mult),
                          B.on_read(f"mrot{h}")[0], B.freed(l, f"mrot{h}")[1])
                    link(vec.tensor_tensor(tf[64:QK, h % 2], tf[64:QK, h % 2], qT[64:QK, h], ALU.add))
                    f = use_factor(f"mqst{h}")
                    after(vec.tensor_tensor(qT[0:QK, h], tf[0:QK, h % 2], f[0:QK], ALU.mult),
                          nrs_used.sem, nrs_used.at(l, norm_index(f"mqst{h}"))[1])

                def mla_keys(h):
                    f = use_factor(f"mkst{h}")
                    vec.scalar_tensor_tensor(kT[0:NOPE, h], B[f"mk{h}"][0:NOPE, :], gain(G_MK, 0, NOPE), f[0:NOPE],
                                             ALU.mult, ALU.mult).then_inc(*B.on_read(f"mk{h}"))
                    vec.tensor_tensor(kT[64:QK, h], kT[64:QK, 3], f[64:QK], ALU.mult).then_inc(nrs_used.sem, 1)

                def silu(h):
                    vec.wait_ge(*gexp_ready.at(l, h))
                    link(vec.tensor_scalar(pb[:, h % 2], pb[:, h % 2], 1.0, None, ALU.add))
                    link(vec.reciprocal(pb[:, h % 2], pb[:, h % 2]))
                    vec.tensor_tensor(gg[:, h], gg[:, h], pb[:, h % 2], ALU.mult).then_inc(gg_ready.sem, 1)

                def tasks(u):
                    if u == 0:
                        evacuate("iq0", iqT[:, 0])
                    if u == 1:
                        evacuate("iq1", iqT[:, 1])
                    if u == 2:
                        vec.wait_ge(*B.filled(l, "small"))
                        link(vec.tensor_tensor(cqn[0:64, 1], B["small"][0:64, :], rb[0:64], ALU.mult))
                        vec.wait_ge(*zeroed.at(l, 0))
                        vec.tensor_tensor(ikp[64:96, 2], B["small"][64:96, :], rb[64:96], ALU.mult)\
                            .then_inc(ik_ready.sem, 1)
                        vec.tensor_tensor(kT[64:QK, 0], B["small"][96:P, :], rb[96:P], ALU.mult)\
                            .then_inc(*B.on_read("small"))
                        vec.wait_ge(*B.freed(l, "small"))
                        vec.tensor_scalar(kT[64:QK, 2], kT[64:QK, 0], gain(G_MK, 64, QK), None, ALU.mult)\
                            .then_inc(kr_ready.sem, 1)
                        vec.wait_ge(*kr_ready.at(l, 0))
                        vec.tensor_tensor(kT[64:QK, 3], kT[64:QK, 2], cos, ALU.mult).then_inc(krg_ready.sem, 1)
                        vec.wait_ge(*B.filled(l, "rcol"))
                        vec.tensor_copy(rcol[:].unsqueeze(2),
                                        B["rcol"][:].rearrange("p (t c) -> p t c", t=TB)[:, :, 0:1])\
                            .then_inc(*B.on_read("rcol"))
                        vec.wait_ge(*B.freed(l, "rcol"))
                    if u == 5:
                        for tb in range(TB):
                            vec.wait_ge(*B.filled(l, f"dv{tb}"))
                            vec.tensor_scalar(dvt[:, tb], B[f"dv{tb}"][:, 0:DVW], rcol[:, tb:tb + 1], None, ALU.mult)\
                                .then_inc(*B.on_read(f"dv{tb}"))
                        vec.wait_ge(*B.freed(l, "dv1"))
                        vec.wait_ge(*B.freed(l, "dv2"))
                        vec.wait_ge(*B.freed(l, "dv3"))
                        link(vec.tensor_scalar(iws[:], dvt[:, 1:4, H * DH:H * DH + IDX_H],
                                               float(IDX_H * IDX_D) ** -0.5, None, ALU.mult))
                    if u == 6:
                        evacuate("cq", cqn[:, 0])
                        for i, (qb, h) in enumerate(REL):
                            n = (qb + 1) * P
                            dst = scores_of(qb)
                            vec.wait_ge(*B.freed(l, f"rel{i}"))
                            after(vec.scalar_tensor_tensor(dst, sqb[:, i % 2, 0:n], iws[:, qb - 1, h:h + 1],
                                                           causal(qb) if h == 0 else dst, ALU.mult, ALU.add),
                                  rel_used.sem, rel_used.at(l, i)[1])
                    if u == 7:
                        evacuate("ckv", ckvn[:])
                        for pr in range(2):
                            vec.wait_ge(*gate_ready.at(l, pr))
                            link(vec.scalar_tensor_tensor(e1[:, pr], tf[:, pr], 0.0, e2[:, pr],
                                                          ALU.min, ALU.subtract))
                            vec.tensor_tensor_scan(tf[:, pr], con[:, C_SCAN:C_SCAN + T], e1[:, pr], 0.0,
                                                   ALU.mult, ALU.add).then_inc(decay_ready.sem, 1)
                    if u in (8, 9):
                        evacuate(f"dq{u - 8}", dqr[:, u - 8])
                    if u == 8:
                        f = use_factor("cqst")
                        vec.scalar_tensor_tensor(cqn[:, 0], cqn[:, 0], gain(G_QLAT), f, ALU.mult, ALU.mult)
                        vec.scalar_tensor_tensor(cqn[0:64, 1], cqn[0:64, 1], gain(G_QLAT + 1, 0, 64), f[0:64],
                                                 ALU.mult, ALU.mult).then_inc(nrs_used.sem, 1)
                        f = use_factor("ckvst")
                        vec.scalar_tensor_tensor(ckvn[:], ckvn[:], gain(G_KVLAT), f, ALU.mult, ALU.mult)\
                            .then_inc(nrs_used.sem, 1)
                    if u == 9:
                        mla_gain(0)
                        dsa_queries(0)
                    if u in (10, 11):
                        evacuate(f"dk{u - 10}", dkn[:, u - 10])
                    if u == 10:
                        mla_queries(0)
                        mla_gain(1)
                        dsa_queries(1)
                    if u == 11:
                        mla_queries(1)
                        mla_gain(2)
                        dsa_keys(0)
                    if u in (12, 13):
                        pr = u - 12
                        vec.wait_ge(*exp_ready.at(l, pr))
                        vec.wait_ge(*zeroed.at(l, 2))
                        link(vec.scalar_tensor_tensor(kinv[:, pr], rb[:], GLA_DK ** -0.5, e1[:, pr],
                                                      ALU.mult, ALU.mult))
                        vec.wait_ge(*B.filled(l, f"gq{pr}"))
                        vec.tensor_tensor(gqp[0:64, 2 * pr], B[f"gq{pr}"][0:64, :], kinv[0:64, pr], ALU.mult)
                        vec.tensor_tensor(gqp[64:P, 2 * pr + 1], B[f"gq{pr}"][64:P, :], kinv[64:P, pr], ALU.mult)\
                            .then_inc(*B.on_read(f"gq{pr}"))
                    if u == 12:
                        mla_queries(2)
                        mla_gain(3)
                        dsa_keys(1)
                    if u == 13:
                        mla_queries(3)
                        vec.wait_ge(*B.filled(l, "krot"))
                        vec.wait_ge(*krg_ready.at(l, 0))
                        after(vec.tensor_tensor(kT[64:QK, 0], B["krot"][64:QK, :], sin, ALU.mult),
                              B.on_read("krot")[0], B.freed(l, "krot")[1])
                        link(vec.tensor_tensor(kT[64:QK, 3], kT[64:QK, 3], kT[64:QK, 0], ALU.add))
                    if u in (14, 15):
                        pr = u - 14
                        link(vec.tensor_tensor(e2[:, pr], e2[:, pr], rb[:], ALU.mult))
                        vec.wait_ge(*B.filled(l, f"gk{pr}"))
                        vec.tensor_tensor(kinv[:, pr], B[f"gk{pr}"][:], e2[:, pr], ALU.mult)\
                            .then_inc(*B.on_read(f"gk{pr}"))
                        vec.wait_ge(*B.freed(l, f"gk{pr}"))
                        dec = e1[:, pr].rearrange("p (c t) -> p c t", t=CHUNK)[:, :, CHUNK - 1:CHUNK]
                        vec.tensor_tensor(tf[:, pr].rearrange("p (c t) -> p c t", t=CHUNK),
                                          kinv[:, pr].rearrange("p (c t) -> p c t", t=CHUNK),
                                          dec.to_broadcast([P, NCHUNK, CHUNK]), ALU.mult)\
                            .then_inc(kend_ready.sem, 1)
                    if 14 <= u <= 17:
                        mla_keys(u - 14)
                    if 16 <= u <= 19:
                        evacuate(f"gg{u - 16}", gg[:, u - 16])
                    if 17 <= u <= 20:
                        silu(u - 17)
                    if u == 18:
                        vec.wait_ge(*zeroed.at(l, 4))
                        for pr in range(2):
                            vec.wait_ge(*B.filled(l, f"ketr{pr}"))
                            src = B[f"ketr{pr}"][:].rearrange("p (t c) -> p t c", t=TB)
                            cols = slice(pr * P, (pr + 1) * P)
                            link(vec.tensor_copy(ke[0:64, 0, :, cols], src[0:64]))
                            vec.tensor_copy(ke[64:P, 1, :, cols], src[64:P]).then_inc(*B.on_read(f"ketr{pr}"))
                    if u == 23:
                        for tb in range(TB):
                            vec.wait_ge(*B.filled(l, f"gv{tb}"))
                            vec.tensor_scalar(gvt[:, tb], B[f"gv{tb}"][:], rcol[:, tb:tb + 1], None, ALU.mult)\
                                .then_inc(*B.on_read(f"gv{tb}"))

                steps = 3 * (TOPK // 8)
                per_slot = 3
                done = 0
                for u in range(N_IN):
                    low_part(u % 2, hi_ready.at(l, u + AHEAD))
                    tasks(u)
                    if u >= 7:
                        for i in range(done, min(done + per_slot, steps)):
                            select_step(i)
                        done = min(done + per_slot, steps)
                assert done == steps
                for qb in (1, 2, 3):
                    link(vec.tensor_scalar(scores_of(qb), scores_of(qb), TAKEN * 0.5, NEG, ALU.is_gt, ALU.mult))

                vec.wait_ge(*zeroed.at(l, 3))
                for pr in range(2):
                    for c in range(NCHUNK - 1):
                        name = f"inc{pr}{c // 4}"
                        inc = B[name][:, (c % 4) * P:(c % 4 + 1) * P]
                        if c % 4 == 0:
                            vec.wait_ge(*B.filled(l, name))
                        last = c % 4 == 3 or c == NCHUNK - 2
                        if c == 0:
                            op = vec.tensor_copy(st[:, 1, pr], inc)
                        else:
                            op = vec.scalar_tensor_tensor(st[:, c + 1, pr], st[:, c, pr],
                                                          e1[:, pr, c * CHUNK + CHUNK - 1:c * CHUNK + CHUNK], inc,
                                                          ALU.mult, ALU.add)
                        if last:
                            op.then_inc(*B.on_read(name))
                            vec.wait_ge(*B.freed(l, name))
                        else:
                            link(op)

                def masked_scores(h):
                    vec.wait_ge(*B.filled(l, f"gs{h}"))
                    if h >= 2:
                        vec.wait_ge(*B.filled(l, f"go{h - 2}"))
                    src = B[f"gs{h}"][:].rearrange("p (t c) -> p t c", t=TB)
                    for hp in range(2):
                        r = slice(64 * hp, 64 * hp + 64)
                        m = con[r, C_GM:C_GM + CHUNK].unsqueeze(1).to_broadcast([64, TB, CHUNK])
                        op = vec.tensor_tensor(sct[r, h % 2, :, r], src[r, :, r], m, ALU.mult)
                    op.then_inc(*B.on_read(f"gs{h}"))

                def mix(j, name, bank, g, gate=None):
                    f = use_factor(name)
                    op = vec.scalar_tensor_tensor(tf[:, j % 2], B[bank][:], gain(g), f, ALU.mult, ALU.mult)
                    op.then_inc(*B.on_read(bank))
                    vec.wait_ge(*B.freed(l, bank))
                    if gate is None:
                        vec.sem_inc(mixf_ready.sem, 1)
                    else:
                        vec.tensor_tensor(tf[:, j % 2], tf[:, j % 2], gg[:, gate], ALU.mult)\
                            .then_inc(mixf_ready.sem, 1)
                    vec.sem_inc(nrs_used.sem, 1)

                def mix_low(j):
                    vec.wait_ge(*mixh_ready.at(l, j))
                    vec.tensor_tensor(xgl[:, MIXED[j]], tf[:, j % 2], xgh[:, MIXED[j]], ALU.subtract)\
                        .then_inc(mix_ready.sem, 1)

                masked_scores(0)
                masked_scores(1)
                for h in range(GLA_H):
                    if h + 2 < GLA_H:
                        masked_scores(h + 2)
                    mix(h, f"gst{h}", f"go{h}", G_GLA + h, gate=h)
                    mix_low(h)

                def mask_max(j):
                    qb = j % TB
                    n = (qb + 1) * P
                    scale = (QK if j < H * TB else DH) ** -0.5
                    mask = scores_of(qb) if j >= H * TB and qb >= 1 else causal(qb)
                    vec.wait_ge(*B.filled(l, f"lg{j}"))
                    if j >= PLANES:
                        vec.wait_ge(*B.filled(l, f"pt{j - PLANES}"))
                    alone(vec)
                    vec.tensor_tensor_reduce(pba[:, j % PLANES, 0:n], B[f"lg{j}"][:, 0:n], mask, 1.0, -3.4e38,
                                             ALU.add, ALU.max, mx[:, j:j + 1]).then_inc(*B.on_read(f"lg{j}"))
                    vec.wait_ge(*B.freed(l, f"lg{j}"))
                    vec.tensor_scalar(nb[:, j:j + 1], mx[:, j:j + 1], -scale, None, ALU.mult)\
                        .then_inc(lg_ready.sem, 1)

                def normalise(j):
                    n = (j % TB + 1) * P
                    vec.wait_ge(*p_ready.at(l, j))
                    link(vec.reciprocal(rinv[:, j:j + 1], rsum[:, j:j + 1]))
                    vec.tensor_scalar(pba[:, j % PLANES, 0:n], pba[:, j % PLANES, 0:n], rinv[:, j:j + 1], None,
                                      ALU.mult).then_inc(pn_ready.sem, 1)

                def out_mix(b):
                    mix(4 + b, f"aost{b}", f"ao{b}", (G_MLA if b < 2 else G_DSA) + b % 2)

                for j in range(LEAD):
                    mask_max(j)
                normalise(0)
                for j in range(N_ATT):
                    if j + LEAD < N_ATT:
                        mask_max(j + LEAD)
                    if j + 1 < N_ATT:
                        normalise(j + 1)
                    if j % PAIR == LAG + 2 and j > PAIR:
                        out_mix(j // PAIR - 1)
                    if j % PAIR == LAG + 3 and j > PAIR:
                        mix_low(4 + j // PAIR - 1)
                out_mix(3)
                mix_low(7)

                for d in range(KB):
                    low_part(d % 2, hi_ready.at(l, N_IN + d + AHEAD))
                    vec.wait_ge(*B.filled(l, f"out{d}"))
                    vec.tensor_tensor(x[:, d], x[:, d], B[f"out{d}"][:], ALU.add).then_inc(*B.on_read(f"out{d}"))
                    gained_low(d, KB + d, xmh, xml, G_MLP)
                def hidden_group(g):
                    with vec.Fori(0, 4) as p:
                        for s in range(2):
                            vec.wait_ge(hh_ready.sem, l * 32 + g * 8 + p * 2 + (s + 1))
                            vec.tensor_tensor(sqb[:, s], tf[:, s], tf[:, s], ALU.mult).then_inc(hid_ready.sem, 1)
                            vec.wait_ge(hid_ready.sem, l * 32 + g * 8 + p * 2 + (s + 1))
                            vec.tensor_tensor(hl[:, p * 2 + s], sqb[:, s], hh[:, p * 2 + s], ALU.subtract)\
                                .then_inc(hl_ready.sem, 1)
                            low_part(s, (hi_ready.sem, l * N_UNIT + g * 16 + p * 2 + (N_IN + N_OUT + AHEAD + 1 + s)))

                def share_group(g):
                    with vec.Fori(0, 4) as p:
                        for s in range(2):
                            low_part(s, (hi_ready.sem, l * N_UNIT + g * 16 + p * 2 + (N_IN + N_OUT + 8 + AHEAD + 1 + s)))
                            vec.wait_ge(dn_filled[s].sem, l * 16 + g * 4 + p + 1)
                            vec.wait_ge(x_ready.sem, l * 32 + g * 8 + p * 2 + (7 + s))
                            vec.tensor_tensor(rsb[:, s], B.t[s][:], rb[:], ALU.mult).then_inc(dn_freed[s].sem, 1)

                vec.wait_ge(*sq_summed.at(l, 2 * KB - 1))
                alone(vec)
                hidden_group(0)
                vec.wait_ge(*B.filled(l, "mstat"))
                vec.tensor_scalar(rb[:], B["mstat"][:], 1.0 / D, EPS, ALU.mult, ALU.add).then_inc(*B.on_read("mstat"))
                vec.wait_ge(*B.freed(l, "mstat"))
                vec.reciprocal(rb[:], rb[:]).then_inc(rb_ready.sem, 1)
                vec.wait_ge(*rb_ready.at(l, 1))
                alone(vec)
                share_group(0)
                with vec.Fori(1, GROUPS) as g:
                    hidden_group(g)
                    share_group(g)
                assert links[0] <= VEC_LINKS
                vec.sem_inc(vec_chain.sem, VEC_LINKS - links[0])


def weight_stream(w_in, w_out, w_up, w_down):
    cols = {"iq": IQ, "dq": DQ, "dk": DK, "gq": GQ, "gk": GK, "gg": GG}

    def blocks(w, rows, columns):
        part = w[rows[0]:rows[1]][:, columns]
        return part.reshape(-1, P, part.shape[1]).transpose(1, 0, 2).reshape(P, -1)

    stream = np.zeros((DEPTH * N_UNIT + AHEAD, P, 1024), w_in.dtype)
    for l in range(DEPTH):
        n = l * N_UNIT
        token = 0
        for u, name in enumerate(UNITS):
            rows = (0, D)
            if name == "small":
                c = np.r_[CQ + P:CQ + Q_RANK, IK:IK + IDX_D, KR:KR + ROPE]
            elif name == "cq":
                c = np.r_[CQ:CQ + P]
            elif name == "ckv":
                c = np.r_[CKV:CKV + KV_RANK]
            elif name == "dv":
                a, b = DV_BLOCKS[u - 3]
                rows, c = (a * P, b * P), np.r_[DV:DV + H * DH, IW:IW + IDX_H, GLR:GLR + RANK]
            elif name == "gv":
                rows, c = (2 * (u - 20) * P, 2 * (u - 19) * P), np.r_[GV:GV + GLA_H * GLA_DV]
            else:
                c0 = cols[name[:2]] + P * int(name[2:])
                c = np.r_[c0:c0 + P]
            part = blocks(w_in[l], rows, c)
            stream[n + u, :, :part.shape[1]] = part
        n += N_IN
        for d in range(KB):
            stream[n + d] = blocks(w_out[l], (0, D), np.r_[d * P:(d + 1) * P])
        n += N_OUT
        for g in range(GROUPS):
            for j in range(8):
                c0 = (g * 8 + j) * P
                stream[n + g * 16 + j] = blocks(w_up[l], (0, D), np.r_[c0:c0 + P])
                stream[n + g * 16 + 8 + j] = blocks(w_down[l], (g * 1024, (g + 1) * 1024), np.r_[j * P:(j + 1) * P])
    return stream


def parameter_blocks(a):
    par = np.zeros((DEPTH, P, N_PAR), a["attn_norm"].dtype)
    for l in range(DEPTH):
        q = par[l]
        q[:, G_ATTN:G_ATTN + 8] = a["attn_norm"][l].reshape(KB, P).T
        q[:, G_MLP:G_MLP + 8] = a["mlp_norm"][l].reshape(KB, P).T
        q[:, G_BIAS:G_BIAS + 2] = a["gla_gate_bias"][l].reshape(2, P).T
        q[:, G_GLA:G_GLA + 4] = a["gla_out_norm"][l].T
        q[:, G_DQ] = np.concatenate([a["dsa_q_norm"][l]] * 2)
        q[:, G_DK] = np.concatenate([a["dsa_k_norm"][l]] * 2)
        q[:, G_DSA:G_DSA + 2] = a["dsa_out_norm"][l].reshape(2, P).T
        q[:, G_QLAT] = a["mla_q_latent_norm"][l][:P]
        q[0:64, G_QLAT + 1] = a["mla_q_latent_norm"][l][P:]
        q[:, G_KVLAT] = a["mla_kv_latent_norm"][l]
        q[0:QK, G_MQ] = a["mla_q_norm"][l]
        q[0:QK, G_MK] = a["mla_k_norm"][l]
        q[:, G_MLA:G_MLA + 2] = a["mla_out_norm"][l].reshape(2, P).T
        q[0:RANK, W_GATE:W_GATE + 256] = a["gla_gate_up"][l]
        q[:, W_UQ:W_UQ + H * QK] = a["mla_w_uq"][l][:P]
        q[0:64, W_UQ + H * QK:W_UKV] = a["mla_w_uq"][l][P:]
        q[:, W_UKV:] = a["mla_w_ukv"][l]
    return par


def constant_block():
    c = np.zeros((P, N_CONST), np.float32)
    i = np.arange(P)
    c[:, C_ID:C_ID + P] = np.eye(P)
    c[:, C_BLK:C_BLK + P] = (i[:, None] // 64) == (i[None, :] // 64)
    for j in range(ROPE // 2):
        c[64 + ROPE // 2 + j, C_ROT + j] = -1.0
        c[64 + j, C_ROT + ROPE // 2 + j] = 1.0
    c[:, C_EPS] = EPS
    c[:, C_GM:C_GM + CHUNK] = (i[:, None] % CHUNK) <= np.arange(CHUNK)[None, :]
    c[:, C_CAUSAL + T - P:C_CAUSAL + T] = np.where(i[None, :] <= i[:, None], 0.0, NEG)
    c[:, C_SCAN:C_SCAN + T] = (np.arange(T) % CHUNK) != 0
    half = ROPE // 2
    freq = np.float32(10000.0) ** (-np.arange(half, dtype=np.float32) / np.float32(half))
    ang = (np.arange(T, dtype=np.float32)[None, :] * freq[:, None]).astype(np.float32)
    for r in range(2):
        c[64 + half * r:64 + half * (r + 1), C_COS:C_COS + T] = np.cos(ang)
        c[64 + half * r:64 + half * (r + 1), C_SIN:C_SIN + T] = np.sin(ang)
    return c


def kernel(**inputs):
    import concourse.bacc as bacc
    from concourse.bass_utils import run_bass_kernel_spmd

    a = {k: np.asarray(v) for k, v in inputs.items()}
    arrays = {
        "in_x": np.ascontiguousarray(a["x"][0].T.reshape(KB, P, T).transpose(1, 0, 2)),
        "in_stream": weight_stream(a["w_in"], a["w_out"], a["w_up"], a["w_down"]),
        "in_params": parameter_blocks(a),
        "in_consts": constant_block(),
    }
    nc = bacc.Bacc("TRN2", target_bir_lowering=False, num_devices=1)
    args = [nc.dram_tensor(n, v.shape, F32, kind="ExternalInput").ap() for n, v in arrays.items()]
    out = nc.dram_tensor("out_y", (P, KB, T), F32, kind="ExternalOutput").ap()
    build_trunk(nc, *args, out)
    r = run_bass_kernel_spmd(nc, [arrays], core_ids=[0])
    y = r.results[0]["out_y"]
    return np.ascontiguousarray(y.transpose(2, 1, 0).reshape(1, T, D))
```

```python
from contextlib import ExitStack

import numpy as np

import concourse.bass as bass
from concourse import mybir

F32 = mybir.dt.float32
F32R = mybir.dt.float32r
ALU = mybir.AluOpType
ACT = mybir.ActivationFunctionType

P = 128
T = 512
D = 1024
KB = D // P
TB = T // P
DEPTH = 2
D_FF = 4096
EPS = 1e-6
NEG = -1e30
TAKEN = -3e38
GLA_H, GLA_DK, GLA_DV, RANK, TAU, CHUNK = 4, 64, 128, 16, 16.0, 64
H, DH = 4, 64
IDX_H, IDX_D = 8, 32
MIXED = [0, 1, 2, 3, 6, 7, 4, 5]
TOPK = min(256, T // 4)
SEL_AT = {1: 0, 2: 2 * P, 3: 5 * P, 4: 9 * P}
Q_RANK, KV_RANK, NOPE, ROPE = 192, 128, 64, 32
QK = NOPE + ROPE
NCHUNK = T // CHUNK

_WIDTHS = [256, 256, 512, 512, RANK, 256, 256, 256, IDX_H * IDX_D, IDX_D, IDX_H, Q_RANK, KV_RANK, ROPE]
_C = np.concatenate([[0], np.cumsum(_WIDTHS)]).tolist()
GQ, GK, GV, GG, GLR, DQ, DK, DV, IQ, IK, IW, CQ, CKV, KR, D_IN = _C

UNITS = ["iq0", "iq1", "small", "dv", "dv", "dv", "cq", "ckv", "dq0", "dq1", "dk0", "dk1",
         "gq0", "gq1", "gk0", "gk1", "gg0", "gg1", "gg2", "gg3", "gv", "gv", "gv", "gv"]
N_IN = len(UNITS)
N_OUT = KB
GROUPS = D_FF // (8 * P)
N_MLP = GROUPS * 16
N_UNIT = N_IN + N_OUT + N_MLP
AHEAD = 2
POOL_LOW = range(6, N_IN)
DVW = H * DH + IDX_H + RANK
DV_BLOCKS = [(0, 3), (3, 6), (6, 8)]

G_ATTN, G_MLP, G_BIAS, G_GLA, G_DQ, G_DK, G_DSA, G_QLAT, G_KVLAT, G_MQ, G_MK, G_MLA = (
    0, 8, 16, 18, 22, 23, 24, 26, 28, 29, 30, 31)
W_GATE = 40
W_UQ = W_GATE + 256
W_UKV = W_UQ + 2 * H * QK
N_PAR = W_UKV + H * (NOPE + DH)

C_ID = 0
C_BLK = C_ID + P
C_ROT = C_BLK + P
C_EPS = C_ROT + ROPE
C_GM = C_EPS + 1
C_CAUSAL = C_GM + CHUNK
C_SCAN = C_CAUSAL + T
C_COS = C_SCAN + T
C_SIN = C_COS + T
N_CONST = C_SIN + T


class Sem:

    def __init__(self, ctx, nc, name, per, start=0):
        self.sem = ctx.enter_context(nc.semaphore(name))
        self.per, self.start = per, start

    def at(self, layer, k):
        return self.sem, layer * self.per + (self.start + k + 1)


N_ATT = 2 * H * TB
LEAD, LAG, PLANES = 3, 2, 4
PAIR = 2 * TB

SCORE_SLOT = {2 * h - 2: h for h in range(1, GLA_H)}
OUT_SLOT = {2 * h + 1: h for h in range(GLA_H)}
STAT_SLOT = {2 * h + 3: h for h in range(GLA_H)}

TURNING = ["gs0"] + [f"lg{j}" for j in range(LEAD)]
for _j in range(N_ATT):
    TURNING += [f"lg{_j + LEAD}"] if _j + LEAD < N_ATT else []
    TURNING += [f"gs{SCORE_SLOT[_j]}"] if _j in SCORE_SLOT else []
    TURNING += [f"gst{STAT_SLOT[_j]}"] if _j in STAT_SLOT else []

USES = (
    [("iq0", 0), ("xstat", 6), ("iq1", 1), ("rcol", 7), ("small", 0),
     ("dv0", 4), ("dv1", 5), ("dv2", 6), ("dv3", 7), ("cq", 1), ("glr", 6)]
    + [(f"rel{i}", 2 + i % 2) for i in range(3 * IDX_H)]
    + [("ckv", 0), ("gz0", 4), ("gz1", 5), ("dq0", 1), ("cqst", 6), ("ckvst", 7)]
    + [("dq1", 0), ("dqst0", 2), ("mq0", 4), ("dk0", 1), ("mqst0", 6), ("mrot0", 7)]
    + [("dqst1", 3), ("mq1", 5), ("dk1", 0), ("mqst1", 6), ("mrot1", 7), ("dkst0", 2), ("mq2", 4)]
    + [("gq0", 1), ("mqst2", 6), ("mrot2", 7), ("dkst1", 3), ("mq3", 5)]
    + [("gq1", 0), ("mqst3", 6), ("mrot3", 7), ("krot", 2), ("mk0", 4)]
    + [("gk0", 1), ("mkst0", 6), ("mk1", 5), ("gk1", 0), ("mkst1", 7), ("mk2", 4)]
    + [("gg0", 1), ("mkst2", 6), ("mk3", 5), ("gg1", 0), ("mkst3", 7), ("mv0", 4)]
    + [("gg2", 1), ("mv1", 5), ("ketr0", 2), ("ketr1", 3), ("gg3", 0)]
    + [("gv0", 4), ("gv1", 5), ("gv2", 6), ("gv3", 7)]
    + [(name, (2, 3, 6)[i % 3]) for i, name in enumerate(TURNING[:1 + LEAD])]
    + [("inc00", 4), ("inc01", 5), ("inc10", 6), ("inc11", 7)]
    + [(name, (2, 3, 6)[i % 3]) for i, name in enumerate(TURNING) if i > LEAD]
    + [(f"go{h}", 7 * (h % 2)) for h in range(GLA_H)]
    + [(f"pt{j}", 4 + j % 2) for j in range(N_ATT)]
    + [(f"ao{b}", 1 - b % 2) for b in range(2 * H // 2)]
    + [(f"aost{b}", 7) for b in range(2 * H // 2)]
    + [(f"out{d}", 4 + d % 2) for d in range(KB)] + [("mstat", 6)]
)
NO_FILL = ("ao0", "ao1", "ao2", "ao3")


class Banks:

    def __init__(self, ctx, nc):
        self.place, self.per, self.fills = {}, [0] * 8, [0] * 8
        for name, b in USES:
            self.place[name] = (b, self.per[b], self.fills[b])
            self.per[b] += 1
            self.fills[b] += name not in NO_FILL
        self.t = [ctx.enter_context(nc.psum_tensor(f"bank{b}", [P, T], F32)) for b in range(8)]
        self.fill = [ctx.enter_context(nc.semaphore(f"bank{b}_filled")) for b in range(8)]
        self.free = [ctx.enter_context(nc.semaphore(f"bank{b}_freed")) for b in range(8)]

    def __getitem__(self, name):
        return self.t[self.place[name][0]]

    def filled(self, l, name):
        b, _, k = self.place[name]
        return self.fill[b], l * self.fills[b] + (k + 1)

    def vacant(self, l, name):
        b, k, _ = self.place[name]
        return self.free[b], l * self.per[b] + (k + 1)

    def freed(self, l, name):
        b, k, _ = self.place[name]
        return self.free[b], l * self.per[b] + (k + 2)

    def on_fill(self, name):
        return self.fill[self.place[name][0]], 1

    def on_read(self, name):
        return self.free[self.place[name][0]], 1


NORMS = (["cqst", "ckvst", "dqst0", "mqst0", "dqst1", "mqst1", "dkst0", "mqst2", "dkst1", "mqst3"]
         + [f"mkst{h}" for h in range(H)] + [f"gst{h}" for h in range(GLA_H)]
         + [f"aost{b}" for b in range(4)])
N_NORM = len(NORMS)

VEC_LINKS = 400
ACT_LINKS = 6


def build_trunk(nc, x_in, stream, params, consts, out):
    with ExitStack() as ctx:
        base = nc.sbuf_base if isinstance(nc.sbuf_base, int) else nc.sbuf_base()
        slab = ctx.enter_context(nc.sbuf_tensor("slab", [P, 207 * 256], F32))
        del slab
        base = (base + 31) // 32 * 32
        cursor = [base]

        def place(name, shape, dt=F32, at=None):
            words = int(np.prod(shape[1:]))
            off = cursor[0] if at is None else at
            if at is None:
                cursor[0] += (4 * words + 31) // 32 * 32
                assert cursor[0] <= base + 207 * 1024, (name, cursor[0] - base)
            t = nc.alloc_sbuf_tensor_at(name, list(shape), dt, offset=off)
            return t, off

        x, _ = place("x", [P, KB, T])
        xgh, xh0 = place("xgh", [P, KB, T], F32R)
        xgl, xl0 = place("xgl", [P, KB, T], F32R)
        raw, _ = place("raw", [P, 2, 1024])
        wh, _ = place("wh", [P, 2, 1024], F32R)
        wl, _ = place("wl", [P, 2, 1024], F32R)
        gqp, g0 = place("gqp", [P, GLA_H, T])
        kinv, _ = place("kinv", [P, 2, T])
        ke, ke0 = place("ke", [P, 2, TB, 256])
        gvt, _ = place("gvt", [P, TB, GLA_H * GLA_DV])
        e1, _ = place("e1", [P, 2, T])
        hh, _ = place("hh", [P, 8, T], F32R, at=g0)
        hl, _ = place("hl", [P, 8, T], F32R, at=g0 + 16384)
        cqn, _ = place("cqn", [P, 2, T], at=ke0)
        ckvn, _ = place("ckvn", [P, T], at=ke0 + 4096)
        qT, m0 = place("qT", [P, H, T])
        kT, _ = place("kT", [P, H, T])
        dqp, _ = place("dqp", [P, H, T])
        dkn, _ = place("dkn", [P, 2, T])
        vm, _ = place("vm", [P, TB, H * DH])
        xmh, _ = place("xmh", [P, KB, T], F32R, at=m0)
        xml, _ = place("xml", [P, KB, T], F32R, at=m0 + 16384)
        iqT, a0 = place("iqT", [P, 2, T])
        ikp, _ = place("ikp", [P, 4, T])
        st, _ = place("st", [P, NCHUNK, 2, GLA_DV], at=a0)
        sct, _ = place("sct", [P, 2, TB, P], at=a0 + 8192)
        gg, _ = place("gg", [P, GLA_H, T])
        sel, _ = place("sel", [P, SEL_AT[4]])
        dvt, _ = place("dvt", [P, TB, DVW])
        pb, pb0 = place("pb", [P, 2, T])
        ptb, pt0 = place("ptb", [P, 2, T])
        e2, _ = place("e2", [P, 2, T], at=pt0)
        dqr, _ = place("dqr", [P, 2, T], at=pb0)
        sqb, _ = place("sqb", [P, 2, T])
        lnb, _ = place("lnb", [P, T])
        rsb, _ = place("rsb", [P, 2, T])
        tf, _ = place("tf", [P, 2, T])
        rb, _ = place("rb", [P, T])
        glrs, _ = place("glrs", [RANK, T], at=pb0 + 2048)
        con, _ = place("con", [P, N_CONST])
        par, par0 = place("par", [P, N_PAR])
        pb2, _ = place("pb2", [P, 2, T], at=par0 + 4 * W_UQ)
        pt2, _ = place("pt2", [P, T], at=xh0 + 4 * MIXED[-1] * T)
        pt3, _ = place("pt3", [P, T], at=xl0 + 4 * MIXED[-1] * T)
        ones, _ = place("ones", [P, P])
        rcol, _ = place("rcol", [P, TB])
        rinv, _ = place("rinv", [P, N_ATT])
        iws, _ = place("iws", [P, 3, IDX_H])
        m8, _ = place("m8", [P, 3, 8])
        nb, _ = place("nb", [P, N_ATT])
        rsum, _ = place("rsum", [P, N_ATT])

        ident = con[:, C_ID:C_ID + P]
        cos = con[64:QK, C_COS:C_COS + T]
        sin = con[64:QK, C_SIN:C_SIN + T]
        blk = con[:, C_BLK:C_BLK + P]
        eps = con[:, C_EPS:C_EPS + 1]

        def causal(qb):
            return con[:, C_CAUSAL + (TB - 1 - qb) * P:C_CAUSAL + T]

        def probs(j, n=T):
            i = j % PLANES
            return pb[:, i, 0:n] if i < 2 else pb2[:, i - 2, 0:n]

        def probs_t(j, n=T):
            return (ptb[:, 0, 0:n], ptb[:, 1, 0:n], pt2[:, 0:n], pt3[:, 0:n])[j % PLANES]

        def gain(c, lo=0, hi=P):
            return par[lo:hi, c:c + 1]

        B = Banks(ctx, nc)

        def S(name, per=1, start=0):
            return Sem(ctx, nc, name, per, start)

        x_loaded = [ctx.enter_context(nc.semaphore(f"x_loaded{d}")) for d in range(KB)]
        const_loaded = ctx.enter_context(nc.semaphore("const_loaded"))
        gains_loaded = ctx.enter_context(nc.semaphore("gains_loaded"))
        par_loaded = ctx.enter_context(nc.semaphore("par_loaded"))
        raw_loaded = [ctx.enter_context(nc.semaphore(f"raw_loaded{i}")) for i in range(2)]
        out_stored = ctx.enter_context(nc.semaphore("out_stored"))
        hi_ready = S("hi_ready", N_UNIT)
        lo_ready = S("lo_ready", N_UNIT, start=2)
        token_spent = S("token_spent", 5)
        x_ready = S("x_ready", 8 * GROUPS, start=8)
        xh_ready = S("xh_ready", 2 * KB)
        xl_ready = S("xl_ready", 2 * KB, start=1)
        sq_ready = S("sq_ready", 2 * KB)
        sq_summed = S("sq_summed", 2 * KB)
        rb_ready = S("rb_ready", 2)
        ones_ready = S("ones_ready", 0)
        zeroed = S("zeroed", 6)
        ik_ready = S("ik_ready", 4)
        kr_ready = S("kr_ready")
        rel_used = S("rel_used", 3 * IDX_H)
        gate_ready = S("gate_ready", 2)
        decay_ready = S("decay_ready", 2)
        exp_ready = S("exp_ready", 2)
        nsq_ready = S("nsq_ready", N_NORM)
        nrs_ready = S("nrs_ready", N_NORM, start=1)
        nrs_used = S("nrs_used", N_NORM, start=2)
        krsq_ready = S("krsq_ready")
        krg_ready = S("krg_ready")
        qg_ready = S("qg_ready", H)
        kend_ready = S("kend_ready", 2)
        gexp_ready = S("gexp_ready", GLA_H)
        gg_ready = S("gg_ready", GLA_H)
        p_ready = S("p_ready", 2 * H * TB)
        pn_ready = S("pn_ready", 2 * H * TB)
        weighed = S("weighed", 2 * H * TB, start=2)
        mixf_ready = S("mixf_ready", KB)
        mixh_ready = S("mixh_ready", KB)
        mix_ready = S("mix_ready", KB)
        up_filled = [S(f"up_filled{b}", GROUPS * 4) for b in range(2)]
        up_freed = [S(f"up_freed{b}", GROUPS * 4, start=1) for b in range(2)]
        dn_filled = [S(f"down_filled{b}", GROUPS * 4) for b in range(2)]
        dn_freed = [S(f"down_freed{b}", GROUPS * 4, start=1) for b in range(2)]
        hh_ready = S("hh_ready", GROUPS * 8)
        hid_ready = S("hid_ready", GROUPS * 8)
        hl_ready = S("hl_ready", GROUPS * 8, start=2)
        vec_chain = S("vec_chain", VEC_LINKS)
        act_chain = S("act_chain", ACT_LINKS)

        block = ctx.enter_context(nc.Block())

        def unit_done(l, u):
            if u >= N_IN:
                return B.filled(l, f"out{u - N_IN}")
            if UNITS[u] == "dv":
                return B.filled(l, "dv3") if u == 5 else token_spent.at(l, u - 3)
            if UNITS[u] == "gv":
                return B.filled(l, "gv3") if u == 23 else token_spent.at(l, u - 20 + 2)
            return B.filled(l, UNITS[u])


        passed = ctx.enter_context(nc.semaphore("passed"))

        def alone(eng):
            eng.sem_inc(passed, 1)

        def norm_index(name):
            return NORMS.index(name)

        REL = [(qb, h) for qb in (3, 2, 1) for h in range(IDX_H)]

        def scores_of(qb):
            return sel[:, SEL_AT[qb]:SEL_AT[qb + 1]]

        @block.sync
        def _(sp):
            with sp.Fori(0, (DEPTH * N_UNIT + AHEAD) // 2) as i:
                for s in range(2):
                    sp.wait_ge(lo_ready.sem, 2 * i + (s + 1))
                    sp.dma_start(raw[:, s], stream[2 * i + s]).then_inc(raw_loaded[s], 16)
            for d in range(KB):
                sp.wait_ge(*x_ready.at(DEPTH, d - KB))
                sp.dma_start(out[:, d], x[:, d]).then_inc(out_stored, 16)
            sp.wait_ge(out_stored, 16 * KB)

        @block.gpsimd
        def _(pool):
            pool.memset(ones[:], 1.0).then_inc(ones_ready.sem, 1)

            def sum_square(l, half, k):
                e = half * KB + k
                pool.wait_ge(*sq_ready.at(l, e))
                if k == 0:
                    alone(pool)
                    op = pool.tensor_copy(lnb[:], sqb[:, k % 2])
                else:
                    pool.wait_ge(*sq_summed.at(l, e - 1))
                    op = pool.tensor_tensor(lnb[:], lnb[:], sqb[:, k % 2], ALU.add)
                op.then_inc(sq_summed.sem, 1)

            pool.dma_start(con[:], consts).then_inc(const_loaded, 16)
            pool.dma_start(par[:, W_GATE:N_PAR], params[0][:, W_GATE:N_PAR]).then_inc(par_loaded, 16)
            for k in range(KB):
                sum_square(0, 0, k)
            with pool.Fori(0, DEPTH) as l:
                pool.wait_ge(*x_ready.at(l, -1))
                alone(pool)
                pool.memset(ikp[:], 0.0).then_inc(zeroed.sem, 1)
                pool.memset(dqp[:], 0.0).then_inc(zeroed.sem, 1)
                pool.memset(gqp[:], 0.0).then_inc(zeroed.sem, 1)
                pool.wait_ge(*lo_ready.at(l, POOL_LOW[0] + AHEAD - 1))
                for u in POOL_LOW:
                    pool.wait_ge(*hi_ready.at(l, u + AHEAD))
                    pool.tensor_tensor(wl[:, u % 2], raw[:, u % 2], wh[:, u % 2], ALU.subtract)\
                        .then_inc(lo_ready.sem, 1)
                    if u == 7:
                        pool.wait_ge(*B.filled(l, "rel23"))
                        alone(pool)
                        pool.memset(sct[:], 0.0).then_inc(zeroed.sem, 1)
                    if u == 19:
                        pool.wait_ge(*B.filled(l, "mv1"))
                        alone(pool)
                    if u in (19, 21):
                        pool.memset(ke[:, (u - 19) // 2], 0.0).then_inc(zeroed.sem, 1)
                for k in range(KB):
                    sum_square(l, 1, k)
                pool.wait_ge(*xl_ready.at(l, 2 * KB - 1))
                pool.dma_start(par[:], params[l + 1]).then_inc(par_loaded, 16)

                def add_share(g, d):
                    pool.wait_ge(dn_freed[d % 2].sem, l * 16 + g * 4 + (d // 2 + 2))
                    pool.tensor_tensor(x[:, d], x[:, d], rsb[:, d % 2], ALU.add).then_inc(x_ready.sem, 1)

                with pool.Fori(0, GROUPS - 1) as g:
                    for d in range(KB):
                        add_share(g, d)
                for d in range(KB):
                    add_share(GROUPS - 1, d)
                    if d >= 1:
                        sum_square(l + 1, 0, d - 1)
                sum_square(l + 1, 0, KB - 1)

        @block.tensor
        def _(pe):
            def weights_ready(l, u):
                pe.wait_ge(*lo_ready.at(l, u))

            def n_block(k):
                return slice(k * P, (k + 1) * P)

            def feature_unit(l, u, name, act_h, act_l, order=range(KB), before=None):
                s = u % 2
                weights_ready(l, u)
                pe.wait_ge(*B.vacant(l, name))
                bank = B[name]
                order = list(order)
                for n, k in enumerate(order):
                    if before is not None:
                        before(k)
                    wk_h, wk_l = wh[:, s, n_block(k)], wl[:, s, n_block(k)]
                    last = n == len(order) - 1
                    pe.matmul(bank[:], wk_l, act_h[:, k], start=(n == 0), stop=False)
                    pe.matmul(bank[:], wk_h, act_h[:, k], start=False, stop=False)
                    m = pe.matmul(bank[:], wk_h, act_l[:, k], start=False, stop=last)
                m.then_inc(*B.on_fill(name))

            def token_units(l, u0, blocks, width, stem):
                for i, (ka, kb) in enumerate(blocks):
                    u = u0 + i
                    s = u % 2
                    weights_ready(l, u)
                    for tb in range(TB):
                        bank = B[f"{stem}{tb}"]
                        if i == 0:
                            pe.wait_ge(*B.vacant(l, f"{stem}{tb}"))
                        for k in range(ka, kb):
                            c = (k - ka) * width
                            r_h, r_l = wh[:, s, c:c + width], wl[:, s, c:c + width]
                            a_h = xgh[:, k, tb * P:(tb + 1) * P]
                            a_l = xgl[:, k, tb * P:(tb + 1) * P]
                            last = k == KB - 1
                            pe.matmul(bank[:, 0:width], a_l, r_h, start=(k == 0), stop=False)
                            pe.matmul(bank[:, 0:width], a_h, r_h, start=False, stop=False)
                            m = pe.matmul(bank[:, 0:width], a_h, r_l, start=False, stop=last)
                        if i == len(blocks) - 1 and tb < TB - 1:
                            m.then_inc(*B.on_fill(f"{stem}{tb}"))
                    if i == len(blocks) - 1:
                        m.then_inc(*B.on_fill(f"{stem}{TB - 1}"))
                    else:
                        m.then_inc(token_spent.sem, 1)

            def stat(l, name, lhsT, rhs, rows=P):
                pe.wait_ge(*nsq_ready.at(l, norm_index(name)))
                pe.wait_ge(*B.vacant(l, name))
                pe.matmul(B[name][0:rows, :], lhsT, rhs, start=True, stop=True).then_inc(*B.on_fill(name))

            def sq_of(name):
                return sqb[:, norm_index(name) % 2]

            pe.wait_ge(*ones_ready.at(0, 0))
            with pe.Fori(0, DEPTH) as l:
                def x_part(k):
                    pe.wait_ge(*xl_ready.at(l, k))

                def unit(u, before=None):
                    feature_unit(l, u, UNITS[u], xgh, xgl, before=before)

                def total(name, half):
                    pe.wait_ge(*sq_summed.at(l, half * KB + KB - 1))
                    pe.wait_ge(*B.vacant(l, name))
                    pe.matmul(B[name][:], ones[:], lnb[:], start=True, stop=True).then_inc(*B.on_fill(name))

                def mla_q(h):
                    name = f"mq{h}"
                    pe.wait_ge(*nrs_used.at(l, 0))
                    pe.wait_ge(*B.vacant(l, name))
                    c = W_UQ + h * QK
                    pe.matmul(B[name][0:QK], par[:, c:c + QK], cqn[:, 0], start=True, stop=False)
                    c += H * QK
                    pe.matmul(B[name][0:QK], par[0:64, c:c + QK], cqn[0:64, 1], start=False, stop=True)\
                        .then_inc(*B.on_fill(name))

                def mla_q_rest(h):
                    stat(l, f"mqst{h}", ones[0:QK, 0:QK], sq_of(f"mqst{h}")[0:QK], QK)
                    pe.wait_ge(*qg_ready.at(l, h))
                    pe.wait_ge(*B.vacant(l, f"mrot{h}"))
                    alone(pe)
                    pe.matmul(B[f"mrot{h}"][64:QK], con[64:QK, C_ROT:C_ROT + ROPE], tf[64:QK, h % 2],
                              start=True, stop=True).then_inc(*B.on_fill(f"mrot{h}"))

                def mla_k(h):
                    name = f"mk{h}"
                    pe.wait_ge(*nrs_used.at(l, 1))
                    pe.wait_ge(*B.vacant(l, name))
                    c = W_UKV + h * (NOPE + DH)
                    pe.matmul(B[name][0:NOPE], par[:, c:c + NOPE], ckvn[:], start=True, stop=True)\
                        .then_inc(*B.on_fill(name))

                def mla_k_stat(h):
                    name = f"mkst{h}"
                    pe.wait_ge(*nsq_ready.at(l, norm_index(name)))
                    pe.wait_ge(*krsq_ready.at(l, 0))
                    pe.wait_ge(*B.vacant(l, name))
                    pe.matmul(B[name][0:QK], ones[0:NOPE, 0:QK], sq_of(name)[0:NOPE], start=True, stop=False)
                    pe.matmul(B[name][0:QK], ones[64:QK, 0:QK], cqn[64:QK, 1], start=False, stop=True)\
                        .then_inc(*B.on_fill(name))

                def mla_v(i):
                    name = f"mv{i}"
                    pe.wait_ge(*B.vacant(l, name))
                    vcols = par[:, W_UKV:N_PAR].rearrange("p (h c) -> p h c", h=H)[:, :, NOPE:NOPE + DH]
                    for j in range(2):
                        tb = 2 * i + j
                        m = pe.matmul(B[name][:, j * 256:(j + 1) * 256], ckvn[:, tb * P:(tb + 1) * P], vcols,
                                      start=True, stop=True)
                    m.then_inc(*B.on_fill(name))

                pe.wait_ge(*dn_freed[0].at(l, -1))
                alone(pe)
                unit(0, before=x_part)
                total("xstat", 0)
                pe.wait_ge(*dn_freed[1].at(l, -1))
                alone(pe)
                unit(1)
                pe.wait_ge(*rb_ready.at(l, 0))
                pe.wait_ge(*B.vacant(l, "rcol"))
                for tb in range(TB):
                    m = pe.transpose(B["rcol"][:, tb * P:(tb + 1) * P], rb[:, tb * P:(tb + 1) * P], ident)
                m.then_inc(*B.on_fill("rcol"))
                unit(2)
                token_units(l, 3, DV_BLOCKS, DVW, "dv")
                unit(6)
                pe.wait_ge(*B.freed(l, "dv1"))
                pe.wait_ge(*B.freed(l, "dv3"))
                pe.wait_ge(*B.vacant(l, "glr"))
                for tb in range(TB):
                    m = pe.transpose(B["glr"][0:RANK, tb * P:(tb + 1) * P],
                                     dvt[:, tb, DVW - RANK:DVW], ident)
                m.then_inc(*B.on_fill("glr"))
                pe.wait_ge(*B.freed(l, "iq1"))
                pe.wait_ge(*ik_ready.at(l, 3))
                for i, (qb, h) in enumerate(REL):
                    pe.wait_ge(*B.vacant(l, f"rel{i}"))
                    n = (qb + 1) * P
                    pe.matmul(B[f"rel{i}"][:, 0:n], iqT[:, h // 4, qb * P:(qb + 1) * P], ikp[:, h % 4, 0:n],
                              start=True, stop=True).then_inc(*B.on_fill(f"rel{i}"))
                unit(7)
                pe.wait_ge(*B.freed(l, "glr"))
                for pr in range(2):
                    pe.wait_ge(*B.vacant(l, f"gz{pr}"))
                    pe.matmul(B[f"gz{pr}"][:], par[0:RANK, W_GATE + pr * P:W_GATE + (pr + 1) * P], glrs[:],
                              start=True, stop=True).then_inc(*B.on_fill(f"gz{pr}"))
                unit(8)
                pe.wait_ge(*nsq_ready.at(l, 0))
                pe.wait_ge(*B.vacant(l, "cqst"))
                pe.matmul(B["cqst"][:], ones[:], sqb[:, 0], start=True, stop=False)
                pe.matmul(B["cqst"][:], ones[0:64, :], lnb[0:64], start=False, stop=True)\
                    .then_inc(*B.on_fill("cqst"))
                stat(l, "ckvst", ones[:], sq_of("ckvst"))
                unit(9)
                stat(l, "dqst0", blk, sq_of("dqst0"))
                mla_q(0)
                unit(10)
                mla_q_rest(0)
                stat(l, "dqst1", blk, sq_of("dqst1"))
                mla_q(1)
                unit(11)
                mla_q_rest(1)
                stat(l, "dkst0", blk, sq_of("dkst0"))
                mla_q(2)
                unit(12)
                mla_q_rest(2)
                stat(l, "dkst1", blk, sq_of("dkst1"))
                mla_q(3)
                unit(13)
                mla_q_rest(3)
                pe.wait_ge(*krg_ready.at(l, 0))
                pe.wait_ge(*B.vacant(l, "krot"))
                alone(pe)
                pe.matmul(B["krot"][64:QK], con[64:QK, C_ROT:C_ROT + ROPE], kT[64:QK, 2],
                          start=True, stop=True).then_inc(*B.on_fill("krot"))
                mla_k(0)
                unit(14)
                mla_k_stat(0)
                mla_k(1)
                unit(15)
                mla_k_stat(1)
                mla_k(2)
                unit(16)
                mla_k_stat(2)
                mla_k(3)
                unit(17)
                mla_k_stat(3)
                mla_v(0)
                unit(18)
                mla_v(1)
                for pr in range(2):
                    pe.wait_ge(*kend_ready.at(l, pr))
                    pe.wait_ge(*B.vacant(l, f"ketr{pr}"))
                    for tb in range(TB):
                        m = pe.transpose(B[f"ketr{pr}"][:, tb * P:(tb + 1) * P],
                                         tf[:, pr, tb * P:(tb + 1) * P], ident)
                    m.then_inc(*B.on_fill(f"ketr{pr}"))
                unit(19)
                token_units(l, 20, [(0, 2), (2, 4), (4, 6), (6, 8)], GLA_H * GLA_DV, "gv")

                pe.wait_ge(*B.freed(l, "gq1"))
                pe.wait_ge(*B.freed(l, "gk1"))

                def gla_scores(h):
                    pe.wait_ge(*B.vacant(l, f"gs{h}"))
                    for tb in range(TB):
                        tk = slice(tb * P, (tb + 1) * P)
                        m = pe.matmul(B[f"gs{h}"][:, tk], kinv[:, h // 2, tk], gqp[:, h, tk], start=True, stop=True)
                    m.then_inc(*B.on_fill(f"gs{h}"))

                def gla_out(h):
                    name = f"go{h}"
                    pe.wait_ge(*B.vacant(l, name))
                    pe.wait_ge(*B.freed(l, f"gs{h}"))
                    if h == 0:
                        pe.wait_ge(*B.freed(l, "inc11"))
                    for tb in range(TB):
                        pe.matmul(B[name][:, tb * P:(tb + 1) * P], gvt[:, tb, h * GLA_DV:(h + 1) * GLA_DV],
                                  sct[:, h % 2, tb], start=True, stop=False)
                        for c in (2 * tb, 2 * tb + 1):
                            if c == 0:
                                continue
                            m = pe.matmul(B[name][:, c * CHUNK:(c + 1) * CHUNK], st[:, c, h // 2],
                                          gqp[:, h, c * CHUNK:(c + 1) * CHUNK], start=False,
                                          stop=(c % 2 == 1))
                    m.then_inc(*B.on_fill(name))

                def logits(j):
                    i = j % (H * TB)
                    h, qb = divmod(i, TB)
                    name = f"lg{j}"
                    n = (qb + 1) * P
                    pe.wait_ge(*B.vacant(l, name))
                    if j < H * TB:
                        lhs, rhs = qT[0:QK, h, qb * P:(qb + 1) * P], kT[0:QK, h, 0:n]
                    else:
                        lhs, rhs = dqp[:, h, qb * P:(qb + 1) * P], dkn[:, h // 2, 0:n]
                    pe.matmul(B[name][:, 0:n], lhs, rhs, start=True, stop=True).then_inc(*B.on_fill(name))

                def turn(j):
                    name = f"pt{j}"
                    pe.wait_ge(*B.vacant(l, name))
                    pe.wait_ge(*pn_ready.at(l, j))
                    for kb in range(j % TB + 1):
                        m = pe.transpose(B[name][:, kb * P:(kb + 1) * P],
                                         probs(j)[:, kb * P:(kb + 1) * P], ident)
                    m.then_inc(*B.on_fill(name))

                def weigh(j):
                    h, qb = divmod(j % (H * TB), TB)
                    name = f"ao{j // PAIR}"
                    hp = h % 2
                    if j % PAIR == 0:
                        pe.wait_ge(*B.vacant(l, name))
                    pe.wait_ge(*B.freed(l, f"pt{j}"))
                    v = vm if j < H * TB else dvt
                    for kb in range(qb + 1):
                        m = pe.matmul(B[name][hp * 64:(hp + 1) * 64, qb * P:(qb + 1) * P],
                                      v[:, kb, h * DH:(h + 1) * DH], probs_t(j)[:, kb * P:(kb + 1) * P],
                                      start=(kb == 0), stop=(kb == qb))
                    m.then_inc(weighed.sem, 1)

                pe.wait_ge(*nrs_used.at(l, norm_index("mkst3")))
                pe.wait_ge(*B.freed(l, "mv1"))
                FIRST_OUT = {N_ATT - 1: (0, 2), N_ATT: (2, 4), N_ATT + 1: (4, KB - 1)}

                def first_out(d, n0, n1):
                    s, name = (N_IN + d) % 2, f"out{d}"
                    if n0 == 0:
                        weights_ready(l, N_IN + d)
                        pe.wait_ge(*B.vacant(l, name))
                    for n in range(n0, n1):
                        k = MIXED[n]
                        pe.wait_ge(*mix_ready.at(l, n))
                        wk_h, wk_l = wh[:, s, n_block(k)], wl[:, s, n_block(k)]
                        pe.matmul(B[name][:], wk_l, xgh[:, k], start=(n == 0), stop=False)
                        pe.matmul(B[name][:], wk_h, xgh[:, k], start=False, stop=False)
                        m = pe.matmul(B[name][:], wk_h, xgl[:, k], start=False, stop=(n == KB - 1))
                    if n1 == KB:
                        m.then_inc(*B.on_fill(name))

                gla_scores(0)
                for j in range(LEAD):
                    logits(j)

                for tb in range(TB):
                    pe.wait_ge(*B.freed(l, f"gv{tb}"))
                pe.wait_ge(*B.freed(l, "ketr1"))
                for pr in range(2):
                    for half in range(2):
                        name = f"inc{pr}{half}"
                        pe.wait_ge(*B.vacant(l, name))
                        for c in range(4 * half, min(4 * half + 4, NCHUNK - 1)):
                            for hp in range(2):
                                h = 2 * pr + hp
                                m = pe.matmul(B[name][hp * 64:(hp + 1) * 64, (c % 4) * P:(c % 4 + 1) * P],
                                              ke[:, c % 2, c // 2, h * GLA_DK:(h + 1) * GLA_DK],
                                              gvt[:, c // 2, h * GLA_DV:(h + 1) * GLA_DV], start=True, stop=True)
                        m.then_inc(*B.on_fill(name))

                for j in range(N_ATT + LAG):
                    if j + LEAD < N_ATT:
                        logits(j + LEAD)
                    if j in SCORE_SLOT:
                        gla_scores(SCORE_SLOT[j])
                    if j < N_ATT:
                        turn(j)
                    if j in OUT_SLOT:
                        gla_out(OUT_SLOT[j])
                    if j >= LAG:
                        weigh(j - LAG)
                    if j in STAT_SLOT:
                        h = STAT_SLOT[j]
                        stat(l, f"gst{h}", ones[:], sq_of(f"gst{h}"))
                    if j % PAIR == LAG + 2 and j > PAIR:
                        b = j // PAIR - 1
                        stat(l, f"aost{b}", blk, sq_of(f"aost{b}"))
                    if j in FIRST_OUT:
                        first_out(0, *FIRST_OUT[j])
                stat(l, "aost3", blk, sq_of("aost3"))
                first_out(1, 0, KB - 1)
                first_out(0, KB - 1, KB)
                first_out(1, KB - 1, KB)
                for d in range(2, KB):
                    feature_unit(l, N_IN + d, f"out{d}", xgh, xgl, order=MIXED)

                def mlp_unit(s, waits, src_h, src_l, filled, before=None):
                    for w in waits:
                        pe.wait_ge(*w)
                    for k in range(KB):
                        if before is not None:
                            before(k)
                        pe.matmul(B.t[s][:], wl[:, s, n_block(k)], src_h[:, k], start=(k == 0), stop=False)
                        pe.matmul(B.t[s][:], wh[:, s, n_block(k)], src_h[:, k], start=False, stop=False)
                        m = pe.matmul(B.t[s][:], wh[:, s, n_block(k)], src_l[:, k], start=False, stop=(k == KB - 1))
                    m.then_inc(filled.sem, 1)

                def up_group(g, before=None):
                    with pe.Fori(0, 4) as p:
                        for s in range(2):
                            mlp_unit(s, [(lo_ready.sem, l * N_UNIT + g * 16 + p * 2 + (N_IN + N_OUT + s + 3)),
                                         (up_freed[s].sem, l * 16 + g * 4 + p + 1),
                                         (dn_freed[s].sem, l * 16 + g * 4 + 1)],
                                     xmh, xml, up_filled[s], before if s == 0 else None)

                def down_group(g):
                    def hidden_part(k):
                        if k == 0:
                            pe.wait_ge(hl_ready.sem, l * 32 + g * 8 + (KB - 2 + 2))
                        if k >= KB - 2:
                            pe.wait_ge(hl_ready.sem, l * 32 + g * 8 + (k + 3))

                    with pe.Fori(0, 4) as p:
                        for s in range(2):
                            mlp_unit(s, [(lo_ready.sem, l * N_UNIT + g * 16 + p * 2 + (N_IN + N_OUT + 8 + s + 3)),
                                         (up_freed[s].sem, l * 16 + g * 4 + 5),
                                         (dn_freed[s].sem, l * 16 + g * 4 + p + 1)],
                                     hh, hl, dn_filled[s], hidden_part if s == 0 else None)

                def gained_part(k):
                    if k == 0:
                        pe.wait_ge(*xl_ready.at(l, 2 * KB - 3))
                    if k >= KB - 2:
                        pe.wait_ge(*xl_ready.at(l, KB + k))

                alone(pe)
                up_group(0, gained_part)
                total("mstat", 1)
                alone(pe)
                down_group(0)
                with pe.Fori(1, GROUPS) as g:
                    up_group(g)
                    down_group(g)

        @block.scalar
        def _(act):
            act.dma_start(par[:, 0:W_GATE], params[0][:, 0:W_GATE]).then_inc(gains_loaded, 16)
            for d in range(KB):
                act.dma_start(x[:, d], x_in[:, d]).then_inc(x_loaded[d], 16)
            act.wait_ge(*ones_ready.at(0, 0))

            def split(s, loads):
                act.wait_ge(raw_loaded[s], 16 * loads)
                act.activation(wh[:, s], raw[:, s], ACT.Copy).then_inc(hi_ready.sem, 1)

            act.preload_act_table_set("natural_log_exp_and_others")

            def gained(l, half, k, dst, g):
                act.activation(dst[:, k], x[:, k], ACT.Copy, scale=gain(g + k)).then_inc(xh_ready.sem, 1)
                if k >= 2:
                    act.wait_ge(*sq_summed.at(l, half * KB + k - 2))
                act.activation(sqb[:, k % 2], x[:, k], ACT.Square).then_inc(sq_ready.sem, 1)

            split(0, 1)
            split(1, 1)
            act.wait_ge(gains_loaded, 16)
            for k in range(KB):
                act.wait_ge(x_loaded[k], 16)
                gained(0, 0, k, xgh, G_ATTN)
            act.wait_ge(const_loaded, 16)
            with act.Fori(0, DEPTH) as l:
                links = [0]

                def link(ins):
                    links[0] += 1
                    ins.then_inc(act_chain.sem, 1)
                    act.wait_ge(*act_chain.at(l, links[0] - 1))

                def next_unit(u):
                    act.wait_ge(*unit_done(l, u))
                    split(u % 2, l * (N_UNIT // 2) + ((u + AHEAD) // 2 + 1))

                def square(name, src, rows=slice(0, P), wait=None):
                    if wait is not None:
                        act.wait_ge(*wait)
                    act.activation(sqb[rows, norm_index(name) % 2], src, ACT.Square).then_inc(nsq_ready.sem, 1)

                def query_square(h):
                    square(f"mqst{h}", B[f"mq{h}"][0:QK, :], slice(0, QK), wait=B.filled(l, f"mq{h}"))
                    if h == 0:
                        act.wait_ge(*exp_ready.at(l, 1))
                    if h >= 2:
                        act.wait_ge(*nrs_used.at(l, norm_index(f"mqst{h - 2}")))
                    act.activation(tf[0:QK, h % 2], B[f"mq{h}"][0:QK, :], ACT.Copy, scale=gain(G_MQ, 0, QK))\
                        .then_inc(*B.on_read(f"mq{h}"))

                def factor(name, n, rows=P):
                    i = norm_index(name)
                    act.wait_ge(*B.filled(l, name))
                    act.wait_ge(*nrs_ready.at(l, i - 1))
                    act.activation(lnb[0:rows], B[name][0:rows, :], ACT.Ln, scale=1.0 / n, bias=eps[0:rows])\
                        .then_inc(*B.on_read(name))
                    act.wait_ge(*B.freed(l, name))
                    act.wait_ge(*nrs_used.at(l, i - 2))
                    act.activation(rsb[0:rows, i % 2], lnb[0:rows], ACT.Exp, scale=-0.5).then_inc(nrs_ready.sem, 1)

                def tasks(u):
                    if u == 0:
                        act.wait_ge(*B.filled(l, "xstat"))
                        act.activation(rb[:], B["xstat"][:], ACT.Ln, scale=1.0 / D, bias=eps)\
                            .then_inc(*B.on_read("xstat"))
                        act.wait_ge(*B.freed(l, "xstat"))
                        act.activation(rb[:], rb[:], ACT.Exp, scale=-0.5).then_inc(rb_ready.sem, 1)
                    if u == 2:
                        act.wait_ge(*ik_ready.at(l, 0))
                        for j in (0, 1, 3):
                            act.activation(ikp[32 * j:32 * j + 32, j], ikp[64:96, 2], ACT.Copy)\
                                .then_inc(ik_ready.sem, 1)
                        act.wait_ge(*kr_ready.at(l, 0))
                        act.activation(cqn[64:QK, 1], kT[64:QK, 0], ACT.Square).then_inc(krsq_ready.sem, 1)
                    if u == 6:
                        act.wait_ge(*B.filled(l, "glr"))
                        act.activation(glrs[:], B["glr"][0:RANK, :], ACT.Copy).then_inc(*B.on_read("glr"))
                        for i, (qb, h) in enumerate(REL):
                            n = (qb + 1) * P
                            act.wait_ge(*B.filled(l, f"rel{i}"))
                            if i >= 2:
                                act.wait_ge(*rel_used.at(l, i - 2))
                            act.activation(sqb[:, i % 2, 0:n], B[f"rel{i}"][:, 0:n], ACT.Relu)\
                                .then_inc(*B.on_read(f"rel{i}"))
                    if u == 7:
                        for pr in range(2):
                            act.wait_ge(*B.filled(l, f"gz{pr}"))
                            bias = gain(G_BIAS + pr)
                            act.activation(tf[:, pr], B[f"gz{pr}"][:], ACT.Identity, bias=bias)
                            act.activation(e2[:, pr], B[f"gz{pr}"][:], ACT.Abs, bias=bias)\
                                .then_inc(*B.on_read(f"gz{pr}"))
                            act.wait_ge(*B.freed(l, f"gz{pr}"))
                            link(act.activation(e2[:, pr], e2[:, pr], ACT.Exp, scale=-1.0))
                            act.activation(e2[:, pr], e2[:, pr], ACT.Ln, bias=ones[:, 0:1])\
                                .then_inc(gate_ready.sem, 1)
                        act.wait_ge(*rel_used.at(l, 3 * IDX_H - 1))
                        act.wait_ge(*B.freed(l, "cq"))
                        act.activation(lnb[0:64], cqn[0:64, 1], ACT.Square)
                        square("cqst", cqn[:, 0])
                        square("ckvst", ckvn[:], wait=B.freed(l, "ckv"))
                    if u == 8:
                        for pr in range(2):
                            act.wait_ge(*decay_ready.at(l, pr))
                            act.activation(e1[:, pr], tf[:, pr], ACT.Exp, scale=1.0 / TAU)
                            act.activation(e2[:, pr], tf[:, pr], ACT.Exp, scale=-1.0 / TAU)\
                                .then_inc(exp_ready.sem, 1)
                        factor("cqst", Q_RANK)
                        factor("ckvst", KV_RANK)
                        square("dqst0", dqr[:, 0], wait=B.freed(l, "dq0"))
                    if u == 9:
                        query_square(0)
                        factor("dqst0", DH)
                        square("dqst1", dqr[:, 1], wait=B.freed(l, "dq1"))
                    if u == 10:
                        factor("mqst0", QK, QK)
                        query_square(1)
                        factor("dqst1", DH)
                        square("dkst0", dkn[:, 0], wait=B.freed(l, "dk0"))
                    if u == 11:
                        factor("mqst1", QK, QK)
                        query_square(2)
                        factor("dkst0", DH)
                        square("dkst1", dkn[:, 1], wait=B.freed(l, "dk1"))
                    if u == 12:
                        factor("mqst2", QK, QK)
                        query_square(3)
                        factor("dkst1", DH)
                    if u == 13:
                        factor("mqst3", QK, QK)
                        square("mkst0", B["mk0"][0:NOPE, :], slice(0, NOPE), wait=B.filled(l, "mk0"))
                    if 14 <= u <= 17:
                        if u < 17:
                            h = u - 13
                            square(f"mkst{h}", B[f"mk{h}"][0:NOPE, :], slice(0, NOPE), wait=B.filled(l, f"mk{h}"))
                        factor(f"mkst{u - 14}", QK, QK)
                    if u in (17, 18):
                        i = u - 17
                        act.wait_ge(*B.filled(l, f"mv{i}"))
                        act.activation(vm[:, 2 * i:2 * i + 2], B[f"mv{i}"][:].rearrange("p (t c) -> p t c", t=2), ACT.Copy)\
                            .then_inc(*B.on_read(f"mv{i}"))
                    if 16 <= u <= 19:
                        h = u - 16
                        act.wait_ge(*B.freed(l, f"gg{h}"))
                        if h == 0:
                            act.wait_ge(*nrs_used.at(l, norm_index("dqst1")))
                        if h >= 2:
                            act.wait_ge(*gg_ready.at(l, h - 2))
                        link(act.activation(pb[:, h % 2], gg[:, h], ACT.Exp, scale=-1.0))
                        act.activation(pb[:, h % 2], pb[:, h % 2], ACT.Identity, bias=ones[:, 0:1])\
                            .then_inc(gexp_ready.sem, 1)

                    if u == 5:
                        for tb in range(2):
                            act.wait_ge(*B.filled(l, f"dv{tb}"))
                            act.wait_ge(*B.freed(l, "rcol"))
                            act.activation(dvt[:, tb], B[f"dv{tb}"][:, 0:DVW], ACT.Copy, scale=rcol[:, tb:tb + 1])\
                                .then_inc(*B.on_read(f"dv{tb}"))
                    if u == 22:
                        act.wait_ge(*zeroed.at(l, 5))
                        for pr in range(2):
                            act.wait_ge(*B.filled(l, f"ketr{pr}"))
                            src = B[f"ketr{pr}"][:].rearrange("p (t c) -> p t c", t=TB)
                            cols = slice(pr * P, (pr + 1) * P)
                            act.activation(ke[0:64, 0, :, cols], src[0:64], ACT.Copy)
                            act.activation(ke[64:P, 1, :, cols], src[64:P], ACT.Copy).then_inc(*B.on_read(f"ketr{pr}"))
                    if u == 23:
                        for tb in range(2):
                            act.wait_ge(*B.filled(l, f"gv{tb}"))
                            act.activation(gvt[:, tb], B[f"gv{tb}"][:], ACT.Copy, scale=rcol[:, tb:tb + 1])\
                                .then_inc(*B.on_read(f"gv{tb}"))

                for u in range(N_IN):
                    next_unit(u)
                    tasks(u)

                def mix_high(j, k):
                    act.wait_ge(*mixf_ready.at(l, j))
                    act.activation(xgh[:, k], tf[:, j % 2], ACT.Copy).then_inc(mixh_ready.sem, 1)

                def exponentials(j):
                    n = (j % TB + 1) * P
                    act.wait_ge(*B.freed(l, f"lg{j}"))
                    act.activation(probs(j, n), probs(j, n), ACT.Exp, scale=-1.0,
                                   bias=nb[:, j:j + 1], accum_out=rsum[:, j:j + 1]).then_inc(p_ready.sem, 1)

                def turned(j):
                    n = (j % TB + 1) * P
                    act.wait_ge(*B.filled(l, f"pt{j}"))
                    if j >= PLANES:
                        act.wait_ge(*weighed.at(l, j - PLANES))
                    act.activation(probs_t(j, n), B[f"pt{j}"][:, 0:n], ACT.Copy)\
                        .then_inc(*B.on_read(f"pt{j}"))

                def out_square(b):
                    square(f"aost{b}", B[f"ao{b}"][:], wait=weighed.at(l, PAIR * (b + 1) - 1))

                for j in range(LEAD - 1):
                    exponentials(j)
                for j in range(N_ATT):
                    if j + LEAD - 1 < N_ATT:
                        exponentials(j + LEAD - 1)
                    turned(j)
                    if j - 1 in OUT_SLOT:
                        h = OUT_SLOT[j - 1]
                        square(f"gst{h}", B[f"go{h}"][:], wait=B.filled(l, f"go{h}"))
                    if j in STAT_SLOT:
                        factor(f"gst{STAT_SLOT[j]}", GLA_DV)
                    if j - 1 in STAT_SLOT:
                        mix_high(STAT_SLOT[j - 1], STAT_SLOT[j - 1])
                    if j % PAIR == LAG and j > PAIR:
                        out_square(j // PAIR - 1)
                    if j % PAIR == LAG + 2 and j > PAIR:
                        factor(f"aost{j // PAIR - 1}", DH)
                    if j % PAIR == LAG + 3 and j > PAIR:
                        mix_high(3 + j // PAIR, MIXED[3 + j // PAIR])
                out_square(3)
                factor("aost3", DH)
                mix_high(7, MIXED[7])

                for d in range(KB):
                    next_unit(N_IN + d)
                    act.wait_ge(*B.freed(l, f"out{d}"))
                    gained(l, 1, d, xmh, G_MLP)

                def hidden_group(g):
                    with act.Fori(0, 4) as p:
                        for s in range(2):
                            act.wait_ge(up_filled[s].sem, l * 16 + g * 4 + p + 1)
                            act.wait_ge(hl_ready.sem, l * 32 + g * 8 + p * 2 + (s + 1))
                            act.activation(tf[:, s], B.t[s][:], ACT.Relu).then_inc(up_freed[s].sem, 1)
                            act.wait_ge(up_freed[s].sem, l * 16 + g * 4 + p + 2)
                            act.activation(hh[:, p * 2 + s], tf[:, s], ACT.Square).then_inc(hh_ready.sem, 1)
                            split(s, l * 48 + g * 8 + p + 18)

                with act.Fori(0, GROUPS - 1) as g:
                    hidden_group(g)
                    with act.Fori(0, 4) as p:
                        for s in range(2):
                            act.wait_ge(dn_filled[s].sem, l * 16 + g * 4 + p + 1)
                            split(s, l * 48 + g * 8 + p + 22)
                hidden_group(GROUPS - 1)
                act.wait_ge(par_loaded, 16 * l + 32)
                for d in range(KB):
                    p, s = divmod(d, 2)
                    act.wait_ge(dn_filled[s].sem, l * 16 + (GROUPS - 1) * 4 + p + 1)
                    split(s, l * 48 + (GROUPS - 1) * 8 + p + 22)
                    act.wait_ge(*x_ready.at(l + 1, d - KB))
                    gained(l + 1, 0, d, xgh, G_ATTN)

        @block.vector
        def _(vec):
            for sem in (lo_ready, xl_ready, nrs_ready, nrs_used, weighed, hl_ready, *up_freed, *dn_freed):
                vec.sem_inc(sem.sem, sem.start)
            for freed in B.free:
                vec.sem_inc(freed, 1)

            def low_part(s, hi_wait):
                vec.wait_ge(*hi_wait)
                vec.tensor_tensor(wl[:, s], raw[:, s], wh[:, s], ALU.subtract).then_inc(lo_ready.sem, 1)

            low_part(0, hi_ready.at(0, 0))
            low_part(1, hi_ready.at(0, 1))
            vec.sem_inc(x_ready.sem, x_ready.start)

            def gained_low(l, half, k, dst_h, dst_l, g):
                vec.wait_ge(*xh_ready.at(l, half * KB + k))
                vec.scalar_tensor_tensor(dst_l[:, k], x[:, k], gain(g + k), dst_h[:, k],
                                         ALU.mult, ALU.subtract).then_inc(xl_ready.sem, 1)

            vec.wait_ge(gains_loaded, 16)
            for k in range(KB):
                vec.wait_ge(x_loaded[k], 16)
                gained_low(0, 0, k, xgh, xgl, G_ATTN)
            vec.wait_ge(const_loaded, 16)
            vec.wait_ge(par_loaded, 16)
            with vec.Fori(0, DEPTH) as l:
                links = [0]

                def link(ins):
                    links[0] += 1
                    ins.then_inc(vec_chain.sem, 1)
                    vec.wait_ge(*vec_chain.at(l, links[0] - 1))

                def after(ins, sem, value):
                    ins.then_inc(sem, 1)
                    vec.wait_ge(sem, value)

                def evacuate(name, dst, rows=slice(0, P), factor=None):
                    vec.wait_ge(*B.filled(l, name))
                    f = rb[rows] if factor is None else factor
                    vec.tensor_tensor(dst, B[name][rows, :], f, ALU.mult).then_inc(*B.on_read(name))

                def mark(ins):
                    links[0] += 1
                    ins.then_inc(vec_chain.sem, 1)
                    return vec_chain.at(l, links[0] - 1)

                taken = {}

                def select_steps(first, n):
                    for i0 in range(first, first + n, 3):
                        queries = [3 - i % 3 for i in range(i0, min(i0 + 3, first + n))]
                        found = {}
                        for qb in queries:
                            if qb in taken:
                                vec.wait_ge(*taken[qb])
                            alone(vec)
                            found[qb] = mark(vec.max(m8[:, qb - 1], scores_of(qb)))
                        for qb in queries:
                            vec.wait_ge(*found[qb])
                            alone(vec)
                            taken[qb] = mark(vec.match_replace(scores_of(qb), m8[:, qb - 1], scores_of(qb), TAKEN))

                def use_factor(name):
                    vec.wait_ge(*nrs_ready.at(l, norm_index(name)))
                    return rsb[:, norm_index(name) % 2]

                vec.wait_ge(*rb_ready.at(l, 0))

                def dsa_queries(pr):
                    f = use_factor(f"dqst{pr}")
                    if pr == 0:
                        vec.wait_ge(*zeroed.at(l, 1))
                    for hp in range(2):
                        r = slice(64 * hp, 64 * hp + 64)
                        op = vec.scalar_tensor_tensor(dqp[r, 2 * pr + hp], dqr[r, pr], gain(G_DQ, r.start, r.stop),
                                                      f[r], ALU.mult, ALU.mult)
                    op.then_inc(nrs_used.sem, 1)

                def dsa_keys(pr):
                    f = use_factor(f"dkst{pr}")
                    vec.scalar_tensor_tensor(dkn[:, pr], dkn[:, pr], gain(G_DK), f, ALU.mult, ALU.mult)\
                        .then_inc(nrs_used.sem, 1)

                def mla_gain(h):
                    vec.wait_ge(*B.freed(l, f"mq{h}"))
                    vec.tensor_tensor(qT[64:QK, h], tf[64:QK, h % 2], cos, ALU.mult).then_inc(qg_ready.sem, 1)

                def mla_queries(h):
                    vec.wait_ge(*B.filled(l, f"mrot{h}"))
                    vec.wait_ge(*qg_ready.at(l, h))
                    after(vec.tensor_tensor(tf[64:QK, h % 2], B[f"mrot{h}"][64:QK, :], sin, ALU.mult),
                          B.on_read(f"mrot{h}")[0], B.freed(l, f"mrot{h}")[1])
                    link(vec.tensor_tensor(tf[64:QK, h % 2], tf[64:QK, h % 2], qT[64:QK, h], ALU.add))
                    f = use_factor(f"mqst{h}")
                    after(vec.tensor_tensor(qT[0:QK, h], tf[0:QK, h % 2], f[0:QK], ALU.mult),
                          nrs_used.sem, nrs_used.at(l, norm_index(f"mqst{h}"))[1])

                def mla_keys(h):
                    f = use_factor(f"mkst{h}")
                    vec.scalar_tensor_tensor(kT[0:NOPE, h], B[f"mk{h}"][0:NOPE, :], gain(G_MK, 0, NOPE), f[0:NOPE],
                                             ALU.mult, ALU.mult).then_inc(*B.on_read(f"mk{h}"))
                    vec.tensor_tensor(kT[64:QK, h], kT[64:QK, 3], f[64:QK], ALU.mult).then_inc(nrs_used.sem, 1)

                def silu(h):
                    vec.wait_ge(*gexp_ready.at(l, h))
                    link(vec.reciprocal(pb[:, h % 2], pb[:, h % 2]))
                    vec.tensor_tensor(gg[:, h], gg[:, h], pb[:, h % 2], ALU.mult).then_inc(gg_ready.sem, 1)

                def tasks(u):
                    if u == 0:
                        evacuate("iq0", iqT[:, 0])
                    if u == 1:
                        evacuate("iq1", iqT[:, 1])
                        vec.wait_ge(*B.filled(l, "rcol"))
                        vec.tensor_copy(rcol[:].unsqueeze(2),
                                        B["rcol"][:].rearrange("p (t c) -> p t c", t=TB)[:, :, 0:1])\
                            .then_inc(*B.on_read("rcol"))
                        vec.wait_ge(*B.freed(l, "rcol"))
                    if u == 2:
                        vec.wait_ge(*B.filled(l, "small"))
                        link(vec.tensor_tensor(cqn[0:64, 1], B["small"][0:64, :], rb[0:64], ALU.mult))
                        vec.wait_ge(*zeroed.at(l, 0))
                        vec.tensor_tensor(ikp[64:96, 2], B["small"][64:96, :], rb[64:96], ALU.mult)\
                            .then_inc(ik_ready.sem, 1)
                        vec.tensor_tensor(kT[64:QK, 0], B["small"][96:P, :], rb[96:P], ALU.mult)\
                            .then_inc(*B.on_read("small"))
                        vec.wait_ge(*B.freed(l, "small"))
                        vec.tensor_scalar(kT[64:QK, 2], kT[64:QK, 0], gain(G_MK, 64, QK), None, ALU.mult)\
                            .then_inc(kr_ready.sem, 1)
                        vec.wait_ge(*kr_ready.at(l, 0))
                        vec.tensor_tensor(kT[64:QK, 3], kT[64:QK, 2], cos, ALU.mult).then_inc(krg_ready.sem, 1)
                    if u == 5:
                        for tb in range(2, TB):
                            vec.wait_ge(*B.filled(l, f"dv{tb}"))
                            vec.tensor_scalar(dvt[:, tb], B[f"dv{tb}"][:, 0:DVW], rcol[:, tb:tb + 1], None, ALU.mult)\
                                .then_inc(*B.on_read(f"dv{tb}"))
                        vec.wait_ge(*B.freed(l, "dv1"))
                        vec.wait_ge(*B.freed(l, "dv2"))
                        vec.wait_ge(*B.freed(l, "dv3"))
                        link(vec.tensor_scalar(iws[:], dvt[:, 1:4, H * DH:H * DH + IDX_H],
                                               float(IDX_H * IDX_D) ** -0.5, None, ALU.mult))
                    if u == 6:
                        evacuate("cq", cqn[:, 0])
                        for i, (qb, h) in enumerate(REL):
                            n = (qb + 1) * P
                            dst = scores_of(qb)
                            vec.wait_ge(*B.freed(l, f"rel{i}"))
                            after(vec.scalar_tensor_tensor(dst, sqb[:, i % 2, 0:n], iws[:, qb - 1, h:h + 1],
                                                           causal(qb) if h == 0 else dst, ALU.mult, ALU.add),
                                  rel_used.sem, rel_used.at(l, i)[1])
                    if u == 7:
                        evacuate("ckv", ckvn[:])
                        for pr in range(2):
                            vec.wait_ge(*gate_ready.at(l, pr))
                            link(vec.scalar_tensor_tensor(e1[:, pr], tf[:, pr], 0.0, e2[:, pr],
                                                          ALU.min, ALU.subtract))
                            vec.tensor_tensor_scan(tf[:, pr], con[:, C_SCAN:C_SCAN + T], e1[:, pr], 0.0,
                                                   ALU.mult, ALU.add).then_inc(decay_ready.sem, 1)
                    if u in (8, 9):
                        evacuate(f"dq{u - 8}", dqr[:, u - 8])
                    if u == 8:
                        f = use_factor("cqst")
                        vec.scalar_tensor_tensor(cqn[:, 0], cqn[:, 0], gain(G_QLAT), f, ALU.mult, ALU.mult)
                        vec.scalar_tensor_tensor(cqn[0:64, 1], cqn[0:64, 1], gain(G_QLAT + 1, 0, 64), f[0:64],
                                                 ALU.mult, ALU.mult).then_inc(nrs_used.sem, 1)
                        f = use_factor("ckvst")
                        vec.scalar_tensor_tensor(ckvn[:], ckvn[:], gain(G_KVLAT), f, ALU.mult, ALU.mult)\
                            .then_inc(nrs_used.sem, 1)
                    if u == 9:
                        mla_gain(0)
                        dsa_queries(0)
                    if u in (10, 11):
                        evacuate(f"dk{u - 10}", dkn[:, u - 10])
                    if u == 10:
                        mla_queries(0)
                        mla_gain(1)
                        dsa_queries(1)
                    if u == 11:
                        mla_queries(1)
                        mla_gain(2)
                        dsa_keys(0)
                    if u in (12, 13):
                        pr = u - 12
                        vec.wait_ge(*exp_ready.at(l, pr))
                        vec.wait_ge(*zeroed.at(l, 2))
                        link(vec.scalar_tensor_tensor(kinv[:, pr], rb[:], GLA_DK ** -0.5, e1[:, pr],
                                                      ALU.mult, ALU.mult))
                        vec.wait_ge(*B.filled(l, f"gq{pr}"))
                        vec.tensor_tensor(gqp[0:64, 2 * pr], B[f"gq{pr}"][0:64, :], kinv[0:64, pr], ALU.mult)
                        vec.tensor_tensor(gqp[64:P, 2 * pr + 1], B[f"gq{pr}"][64:P, :], kinv[64:P, pr], ALU.mult)\
                            .then_inc(*B.on_read(f"gq{pr}"))
                    if u == 12:
                        mla_queries(2)
                        mla_gain(3)
                        dsa_keys(1)
                    if u == 13:
                        mla_queries(3)
                        vec.wait_ge(*B.filled(l, "krot"))
                        vec.wait_ge(*krg_ready.at(l, 0))
                        after(vec.tensor_tensor(kT[64:QK, 0], B["krot"][64:QK, :], sin, ALU.mult),
                              B.on_read("krot")[0], B.freed(l, "krot")[1])
                        link(vec.tensor_tensor(kT[64:QK, 3], kT[64:QK, 3], kT[64:QK, 0], ALU.add))
                    if u in (14, 15):
                        pr = u - 14
                        link(vec.tensor_tensor(e2[:, pr], e2[:, pr], rb[:], ALU.mult))
                        vec.wait_ge(*B.filled(l, f"gk{pr}"))
                        vec.tensor_tensor(kinv[:, pr], B[f"gk{pr}"][:], e2[:, pr], ALU.mult)\
                            .then_inc(*B.on_read(f"gk{pr}"))
                        vec.wait_ge(*B.freed(l, f"gk{pr}"))
                        dec = e1[:, pr].rearrange("p (c t) -> p c t", t=CHUNK)[:, :, CHUNK - 1:CHUNK]
                        vec.tensor_tensor(tf[:, pr].rearrange("p (c t) -> p c t", t=CHUNK),
                                          kinv[:, pr].rearrange("p (c t) -> p c t", t=CHUNK),
                                          dec.to_broadcast([P, NCHUNK, CHUNK]), ALU.mult)\
                            .then_inc(kend_ready.sem, 1)
                    if 14 <= u <= 17:
                        mla_keys(u - 14)
                    if 16 <= u <= 19:
                        evacuate(f"gg{u - 16}", gg[:, u - 16])
                    if 17 <= u <= 20:
                        silu(u - 17)
                    if u == 23:
                        for tb in range(2, TB):
                            vec.wait_ge(*B.filled(l, f"gv{tb}"))
                            vec.tensor_scalar(gvt[:, tb], B[f"gv{tb}"][:], rcol[:, tb:tb + 1], None, ALU.mult)\
                                .then_inc(*B.on_read(f"gv{tb}"))

                steps = 3 * (TOPK // 8)
                per_slot = {7: 5, 8: 4, 9: 4, 10: 3, 11: 3, 12: 4, 13: 4, 14: 4, 15: 4, 16: 2, 17: 2, 18: 2,
                            19: 2, 20: 5}
                done = 0
                for u in range(N_IN):
                    if u not in POOL_LOW:
                        low_part(u % 2, hi_ready.at(l, u + AHEAD))
                    tasks(u)
                    select_steps(done, per_slot.get(u, 0))
                    done += per_slot.get(u, 0)
                assert done == steps
                for qb in (3, 2, 1):
                    vec.wait_ge(*taken[qb])
                    link(vec.tensor_scalar(scores_of(qb), scores_of(qb), TAKEN * 0.5, NEG, ALU.is_gt, ALU.mult))

                def masked_scores(h):
                    vec.wait_ge(*B.filled(l, f"gs{h}"))
                    if h >= 2:
                        vec.wait_ge(*B.filled(l, f"go{h - 2}"))
                    src = B[f"gs{h}"][:].rearrange("p (t c) -> p t c", t=TB)
                    for hp in range(2):
                        r = slice(64 * hp, 64 * hp + 64)
                        m = con[r, C_GM:C_GM + CHUNK].unsqueeze(1).to_broadcast([64, TB, CHUNK])
                        op = vec.tensor_tensor(sct[r, h % 2, :, r], src[r, :, r], m, ALU.mult)
                    op.then_inc(*B.on_read(f"gs{h}"))

                def mix(j, name, bank, g, gate=None):
                    f = use_factor(name)
                    op = vec.scalar_tensor_tensor(tf[:, j % 2], B[bank][:], gain(g), f, ALU.mult, ALU.mult)
                    op.then_inc(*B.on_read(bank))
                    vec.wait_ge(*B.freed(l, bank))
                    if gate is None:
                        vec.sem_inc(mixf_ready.sem, 1)
                    else:
                        vec.tensor_tensor(tf[:, j % 2], tf[:, j % 2], gg[:, gate], ALU.mult)\
                            .then_inc(mixf_ready.sem, 1)
                    vec.sem_inc(nrs_used.sem, 1)

                def mix_low(j):
                    vec.wait_ge(*mixh_ready.at(l, j))
                    vec.tensor_tensor(xgl[:, MIXED[j]], tf[:, j % 2], xgh[:, MIXED[j]], ALU.subtract)\
                        .then_inc(mix_ready.sem, 1)

                def mask_max(j):
                    qb = j % TB
                    n = (qb + 1) * P
                    scale = (QK if j < H * TB else DH) ** -0.5
                    mask = scores_of(qb) if j >= H * TB and qb >= 1 else causal(qb)
                    vec.wait_ge(*B.filled(l, f"lg{j}"))
                    if j >= PLANES:
                        vec.wait_ge(*B.filled(l, f"pt{j - PLANES}"))
                    alone(vec)
                    vec.tensor_tensor_reduce(probs(j, n), B[f"lg{j}"][:, 0:n], mask, -scale, 3.4e38,
                                             ALU.add, ALU.min, nb[:, j:j + 1]).then_inc(*B.on_read(f"lg{j}"))

                def normalise(j):
                    n = (j % TB + 1) * P
                    vec.wait_ge(*p_ready.at(l, j))
                    link(vec.reciprocal(rinv[:, j:j + 1], rsum[:, j:j + 1]))
                    vec.tensor_scalar(probs(j, n), probs(j, n), rinv[:, j:j + 1], None, ALU.mult)\
                        .then_inc(pn_ready.sem, 1)

                def out_mix(b):
                    mix(4 + b, f"aost{b}", f"ao{b}", (G_MLA if b < 2 else G_DSA) + b % 2)

                vec.wait_ge(*zeroed.at(l, 3))
                masked_scores(0)
                for j in range(LEAD):
                    mask_max(j)

                for pr in range(2):
                    for c in range(NCHUNK - 1):
                        name = f"inc{pr}{c // 4}"
                        inc = B[name][:, (c % 4) * P:(c % 4 + 1) * P]
                        if c % 4 == 0:
                            vec.wait_ge(*B.filled(l, name))
                        last = c % 4 == 3 or c == NCHUNK - 2
                        if c == 0:
                            op = vec.tensor_copy(st[:, 1, pr], inc)
                        else:
                            op = vec.scalar_tensor_tensor(st[:, c + 1, pr], st[:, c, pr],
                                                          e1[:, pr, c * CHUNK + CHUNK - 1:c * CHUNK + CHUNK], inc,
                                                          ALU.mult, ALU.add)
                        if last:
                            op.then_inc(*B.on_read(name))
                            vec.wait_ge(*B.freed(l, name))
                        else:
                            link(op)


                normalise(0)
                for j in range(N_ATT):
                    if j + 1 < N_ATT:
                        normalise(j + 1)
                    if j + LEAD < N_ATT:
                        mask_max(j + LEAD)
                    if j - 1 in SCORE_SLOT:
                        masked_scores(SCORE_SLOT[j - 1])
                    if j - 1 in STAT_SLOT:
                        h = STAT_SLOT[j - 1]
                        mix(h, f"gst{h}", f"go{h}", G_GLA + h, gate=h)
                    if j - 2 in STAT_SLOT:
                        mix_low(STAT_SLOT[j - 2])
                    if j % PAIR == LAG + 3 and j > PAIR:
                        out_mix(j // PAIR - 1)
                    if j % PAIR == LAG + 4 and j > PAIR:
                        mix_low(4 + j // PAIR - 1)
                out_mix(3)
                mix_low(7)

                vec.wait_ge(*lo_ready.at(l, N_IN + AHEAD - 1))
                for d in range(KB):
                    low_part(d % 2, hi_ready.at(l, N_IN + d + AHEAD))
                    vec.wait_ge(*B.filled(l, f"out{d}"))
                    vec.tensor_tensor(x[:, d], x[:, d], B[f"out{d}"][:], ALU.add).then_inc(*B.on_read(f"out{d}"))
                    gained_low(l, 1, d, xmh, xml, G_MLP)
                def hidden_group(g):
                    with vec.Fori(0, 4) as p:
                        for s in range(2):
                            vec.wait_ge(hh_ready.sem, l * 32 + g * 8 + p * 2 + (s + 1))
                            vec.tensor_tensor(sqb[:, s], tf[:, s], tf[:, s], ALU.mult).then_inc(hid_ready.sem, 1)
                            vec.wait_ge(hid_ready.sem, l * 32 + g * 8 + p * 2 + (s + 1))
                            vec.tensor_tensor(hl[:, p * 2 + s], sqb[:, s], hh[:, p * 2 + s], ALU.subtract)\
                                .then_inc(hl_ready.sem, 1)
                            low_part(s, (hi_ready.sem, l * N_UNIT + g * 16 + p * 2 + (N_IN + N_OUT + AHEAD + 1 + s)))

                def share(g, p, s):
                    vec.wait_ge(dn_filled[s].sem, l * 16 + g * 4 + p + 1)
                    vec.wait_ge(x_ready.sem, l * 32 + g * 8 + p * 2 + (7 + s))
                    vec.tensor_tensor(rsb[:, s], B.t[s][:], rb[:], ALU.mult).then_inc(dn_freed[s].sem, 1)
                    low_part(s, (hi_ready.sem, l * N_UNIT + g * 16 + p * 2 + (N_IN + N_OUT + 8 + AHEAD + 1 + s)))

                vec.wait_ge(*sq_summed.at(l, 2 * KB - 1))
                alone(vec)
                hidden_group(0)
                vec.wait_ge(*B.filled(l, "mstat"))
                vec.tensor_scalar(rb[:], B["mstat"][:], 1.0 / D, EPS, ALU.mult, ALU.add).then_inc(*B.on_read("mstat"))
                vec.wait_ge(*B.freed(l, "mstat"))
                vec.reciprocal(rb[:], rb[:]).then_inc(rb_ready.sem, 1)
                vec.wait_ge(*rb_ready.at(l, 1))
                alone(vec)
                with vec.Fori(0, 4) as p:
                    for s in range(2):
                        share(0, p, s)
                with vec.Fori(1, GROUPS - 1) as g:
                    hidden_group(g)
                    with vec.Fori(0, 4) as p:
                        for s in range(2):
                            share(g, p, s)
                hidden_group(GROUPS - 1)
                vec.wait_ge(par_loaded, 16 * l + 32)
                for d in range(KB):
                    share(GROUPS - 1, d // 2, d % 2)
                    if d >= 1:
                        gained_low(l + 1, 0, d - 1, xgh, xgl, G_ATTN)
                gained_low(l + 1, 0, KB - 1, xgh, xgl, G_ATTN)
                assert links[0] <= VEC_LINKS
                vec.sem_inc(vec_chain.sem, VEC_LINKS - links[0])


def weight_stream(w_in, w_out, w_up, w_down):
    cols = {"iq": IQ, "dq": DQ, "dk": DK, "gq": GQ, "gk": GK, "gg": GG}

    def blocks(w, rows, columns):
        part = w[rows[0]:rows[1]][:, columns]
        return part.reshape(-1, P, part.shape[1]).transpose(1, 0, 2).reshape(P, -1)

    stream = np.zeros((DEPTH * N_UNIT + AHEAD, P, 1024), w_in.dtype)
    for l in range(DEPTH):
        n = l * N_UNIT
        token = 0
        for u, name in enumerate(UNITS):
            rows = (0, D)
            if name == "small":
                c = np.r_[CQ + P:CQ + Q_RANK, IK:IK + IDX_D, KR:KR + ROPE]
            elif name == "cq":
                c = np.r_[CQ:CQ + P]
            elif name == "ckv":
                c = np.r_[CKV:CKV + KV_RANK]
            elif name == "dv":
                a, b = DV_BLOCKS[u - 3]
                rows, c = (a * P, b * P), np.r_[DV:DV + H * DH, IW:IW + IDX_H, GLR:GLR + RANK]
            elif name == "gv":
                rows, c = (2 * (u - 20) * P, 2 * (u - 19) * P), np.r_[GV:GV + GLA_H * GLA_DV]
            else:
                c0 = cols[name[:2]] + P * int(name[2:])
                c = np.r_[c0:c0 + P]
            part = blocks(w_in[l], rows, c)
            stream[n + u, :, :part.shape[1]] = part
        n += N_IN
        for d in range(KB):
            stream[n + d] = blocks(w_out[l], (0, D), np.r_[d * P:(d + 1) * P])
        n += N_OUT
        for g in range(GROUPS):
            for j in range(8):
                c0 = (g * 8 + j) * P
                stream[n + g * 16 + j] = blocks(w_up[l], (0, D), np.r_[c0:c0 + P])
                stream[n + g * 16 + 8 + j] = blocks(w_down[l], (g * 1024, (g + 1) * 1024), np.r_[j * P:(j + 1) * P])
    return stream


def parameter_blocks(a):
    par = np.zeros((DEPTH + 1, P, N_PAR), a["attn_norm"].dtype)
    for l in range(DEPTH):
        q = par[l]
        q[:, G_ATTN:G_ATTN + 8] = a["attn_norm"][l].reshape(KB, P).T
        q[:, G_MLP:G_MLP + 8] = a["mlp_norm"][l].reshape(KB, P).T
        q[:, G_BIAS:G_BIAS + 2] = a["gla_gate_bias"][l].reshape(2, P).T
        q[:, G_GLA:G_GLA + 4] = a["gla_out_norm"][l].T
        q[:, G_DQ] = np.concatenate([a["dsa_q_norm"][l]] * 2)
        q[:, G_DK] = np.concatenate([a["dsa_k_norm"][l]] * 2)
        q[:, G_DSA:G_DSA + 2] = a["dsa_out_norm"][l].reshape(2, P).T
        q[:, G_QLAT] = a["mla_q_latent_norm"][l][:P]
        q[0:64, G_QLAT + 1] = a["mla_q_latent_norm"][l][P:]
        q[:, G_KVLAT] = a["mla_kv_latent_norm"][l]
        q[0:QK, G_MQ] = a["mla_q_norm"][l]
        q[0:QK, G_MK] = a["mla_k_norm"][l]
        q[:, G_MLA:G_MLA + 2] = a["mla_out_norm"][l].reshape(2, P).T
        q[0:RANK, W_GATE:W_GATE + 256] = a["gla_gate_up"][l]
        q[:, W_UQ:W_UQ + H * QK] = a["mla_w_uq"][l][:P]
        q[0:64, W_UQ + H * QK:W_UKV] = a["mla_w_uq"][l][P:]
        q[:, W_UKV:] = a["mla_w_ukv"][l]
    return par


def constant_block():
    c = np.zeros((P, N_CONST), np.float32)
    i = np.arange(P)
    c[:, C_ID:C_ID + P] = np.eye(P)
    c[:, C_BLK:C_BLK + P] = (i[:, None] // 64) == (i[None, :] // 64)
    for j in range(ROPE // 2):
        c[64 + ROPE // 2 + j, C_ROT + j] = -1.0
        c[64 + j, C_ROT + ROPE // 2 + j] = 1.0
    c[:, C_EPS] = EPS
    c[:, C_GM:C_GM + CHUNK] = (i[:, None] % CHUNK) <= np.arange(CHUNK)[None, :]
    c[:, C_CAUSAL + T - P:C_CAUSAL + T] = np.where(i[None, :] <= i[:, None], 0.0, NEG)
    c[:, C_SCAN:C_SCAN + T] = (np.arange(T) % CHUNK) != 0
    half = ROPE // 2
    freq = np.float32(10000.0) ** (-np.arange(half, dtype=np.float32) / np.float32(half))
    ang = (np.arange(T, dtype=np.float32)[None, :] * freq[:, None]).astype(np.float32)
    for r in range(2):
        c[64 + half * r:64 + half * (r + 1), C_COS:C_COS + T] = np.cos(ang)
        c[64 + half * r:64 + half * (r + 1), C_SIN:C_SIN + T] = np.sin(ang)
    return c


def kernel(**inputs):
    import concourse.bacc as bacc
    from concourse.bass_utils import run_bass_kernel_spmd

    a = {k: np.asarray(v) for k, v in inputs.items()}
    arrays = {
        "in_x": np.ascontiguousarray(a["x"][0].T.reshape(KB, P, T).transpose(1, 0, 2)),
        "in_stream": weight_stream(a["w_in"], a["w_out"], a["w_up"], a["w_down"]),
        "in_params": parameter_blocks(a),
        "in_consts": constant_block(),
    }
    nc = bacc.Bacc("TRN2", target_bir_lowering=False, num_devices=1)
    args = [nc.dram_tensor(n, v.shape, F32, kind="ExternalInput").ap() for n, v in arrays.items()]
    out = nc.dram_tensor("out_y", (P, KB, T), F32, kind="ExternalOutput").ap()
    build_trunk(nc, *args, out)
    r = run_bass_kernel_spmd(nc, [arrays], core_ids=[0])
    y = r.results[0]["out_y"]
    return np.ascontiguousarray(y.transpose(2, 1, 0).reshape(1, T, D))
```
